# Optimizing a Trainium2 kernel written in Bass

```python
import math
import jax, jax.numpy as jnp
from jax import lax
import numpy as np

D_MODEL = 1024
BATCH = 1
SEQ = 512
DEPTH = 2

HEAD_DIM = 64
N_HEADS_A = 8
N_HEADS_B = 8
N_KV_HEADS_B = 2
DILATED_BRANCHES = ((128, 1), (512, 4), (2048, 16))
WINDOW_B = 128
REL_BUCKETS = 32
REL_MAX_DIST = 1024
N_REL_HEADS = N_HEADS_A + N_HEADS_B
D_ATTN_IN = (3 * N_HEADS_A + N_HEADS_B + 2 * N_KV_HEADS_B) * HEAD_DIM
D_ATTN_OUT = (N_HEADS_A + N_HEADS_B) * HEAD_DIM
RWKV_HEAD = 64
RWKV_HEADS = D_MODEL // RWKV_HEAD
DECAY_LORA = 64
AAA_LORA = 64
GATE_LORA = 128
D_FF = 4 * D_MODEL
N_ATTN_LAYERS = (DEPTH + 1) // 2
N_RWKV_LAYERS = DEPTH // 2
NORM_EPS = 1e-6
GN_EPS = 64e-5
NEG_INF = -1e30


F32 = jnp.float32

def rms_norm(x, g):
    x32 = x.astype(F32)
    y = x32 * lax.rsqrt(jnp.mean(x32 * x32, axis=-1, keepdims=True) + NORM_EPS)
    return (y * g.astype(F32)).astype(x.dtype)

def t5_bucket(rel):
    nb = REL_BUCKETS // 2
    max_exact = nb // 2
    bucket = jnp.where(rel > 0, nb, 0)
    n = jnp.abs(rel)
    nf = jnp.maximum(n, 1).astype(F32)
    large = max_exact + (jnp.log(nf / max_exact) / math.log(REL_MAX_DIST / max_exact)
                         * (nb - max_exact)).astype(jnp.int32)
    large = jnp.minimum(large, nb - 1)
    return bucket + jnp.where(n < max_exact, n, large)

def band_rel_bias(table_h, block, dilation):
    i = jnp.arange(block)[:, None]
    j = jnp.arange(3 * block)[None, :]
    bucket = t5_bucket((j - block - i) * dilation)
    return jnp.transpose(table_h[bucket], (2, 0, 1))

def banded_attention(q, k, v, bias, radius, block, sink=None):
    nB, H, G, L, hd = q.shape
    nb = -(-L // block)
    pad = nb * block - L
    qb = jnp.pad(q, [(0, 0)] * 3 + [(0, pad), (0, 0)]).reshape(nB, H, G, nb, block, hd)

    def windows(t):
        tb = jnp.pad(t, [(0, 0)] * 3 + [(block, block + pad), (0, 0)]).reshape(nB, H, G, nb + 2, block, hd)
        return jnp.concatenate([tb[:, :, :, :-2], tb[:, :, :, 1:-1], tb[:, :, :, 2:]], axis=-2)

    kb, vb = windows(k), windows(v)
    valid = jnp.pad(jnp.ones((L,), bool), (block, block + pad)).reshape(nb + 2, block)
    valid = jnp.concatenate([valid[:-2], valid[1:-1], valid[2:]], axis=-1)
    rel = jnp.arange(3 * block)[None, :] - block - jnp.arange(block)[:, None]
    mask = (jnp.abs(rel) <= radius)[None] & valid[:, None, :]
    s = jnp.einsum('bhgnqd,bhgnkd->bhgnqk', qb, kb).astype(F32) * (hd ** -0.5)
    s = s + bias.astype(F32)[None, :, None, None]
    s = jnp.where(mask, s, NEG_INF)
    m = jnp.max(s, axis=-1)
    if sink is not None:
        sink_b = sink.astype(F32)[None, :, None, None, None]
        m = jnp.maximum(m, sink_b)
    p = jnp.exp(s - m[..., None])
    denom = jnp.sum(p, axis=-1)
    if sink is not None:
        denom = denom + jnp.exp(sink_b - m)
    o = jnp.einsum('bhgnqk,bhgnkd->bhgnqd', p, vb.astype(F32)) / denom[..., None]
    lse = m + jnp.log(denom)
    o = o.reshape(nB, H, G, nb * block, hd)[..., :L, :]
    lse = lse.reshape(nB, H, G, nb * block)[..., :L]
    return o, lse

def dilated_attention(q, k, v, table_a):
    nB, H, S, hd = q.shape
    outs, lses = [], []
    for window, dil in DILATED_BRANCHES:
        radius = window // 2 // dil

        def split(t):
            return t.reshape(nB, H, S // dil, dil, hd).transpose(0, 1, 3, 2, 4)

        bias = band_rel_bias(table_a, radius, dil)
        o, lse = banded_attention(split(q), split(k), split(v), bias, radius, radius)
        outs.append(o.transpose(0, 1, 3, 2, 4).reshape(nB, H, S, hd))
        lses.append(lse.transpose(0, 1, 3, 2).reshape(nB, H, S))
    wts = jax.nn.softmax(jnp.stack(lses), axis=0)
    return jnp.einsum('rbhs,rbhsd->bhsd', wts, jnp.stack(outs))

def window_gqa(q, k, v, sink, table_b):
    rep = N_HEADS_B // N_KV_HEADS_B
    k = jnp.repeat(k, rep, axis=1)
    v = jnp.repeat(v, rep, axis=1)
    bias = band_rel_bias(table_b, WINDOW_B, 1)
    o, _ = banded_attention(q[:, :, None], k[:, :, None], v[:, :, None], bias, WINDOW_B, WINDOW_B, sink)
    return o[:, :, 0]

def attention_mixer(h, w_in, sink, w_out, rel_table):
    nB, S, _ = h.shape
    proj = h @ w_in
    sizes = [N_HEADS_A * HEAD_DIM] * 3 + [N_HEADS_B * HEAD_DIM, N_KV_HEADS_B * HEAD_DIM, N_KV_HEADS_B * HEAD_DIM]
    cuts = [int(c) for c in np.cumsum(sizes)[:-1]]
    qa, ka, va, qb, kb, vb = jnp.split(proj, cuts, axis=-1)

    def heads(t):
        return t.reshape(nB, S, -1, HEAD_DIM).transpose(0, 2, 1, 3)

    oa = dilated_attention(heads(qa), heads(ka), heads(va), rel_table[:, :N_HEADS_A])
    ob = window_gqa(heads(qb), heads(kb), heads(vb), sink, rel_table[:, N_HEADS_A:])
    o = jnp.concatenate([oa, ob], axis=1).astype(h.dtype)
    o = o.transpose(0, 2, 1, 3).reshape(nB, S, D_ATTN_OUT)
    return o @ w_out

def rwkv7_scan(r, w, k, v, kk, a):
    def step(state, inp):
        r_t, w_t, k_t, v_t, kk_t, a_t = inp
        sa = jnp.einsum('bhvk,bhk->bhv', state, -kk_t)
        state = (state * w_t[:, :, None, :] + sa[..., None] * (kk_t * a_t)[:, :, None, :]
                 + v_t[..., None] * k_t[:, :, None, :])
        return state, jnp.einsum('bhvk,bhk->bhv', state, r_t)

    nB, S, H, N = r.shape
    xs = tuple(jnp.moveaxis(t, 1, 0) for t in (r, w, k, v, kk, a))
    _, out = lax.scan(step, jnp.zeros((nB, H, N, N), F32), xs)
    return jnp.moveaxis(out, 0, 1)

def group_norm(o, gn_w, gn_b):
    mu = jnp.mean(o, axis=-1, keepdims=True)
    var = jnp.mean(jnp.square(o - mu), axis=-1, keepdims=True)
    y = (o - mu) * lax.rsqrt(var + GN_EPS)
    nB, S, H, N = o.shape
    return y.reshape(nB, S, H * N) * gn_w.astype(F32) + gn_b.astype(F32)

def rwkv7_mixer(h, mu_prev, mu_next, w_r, w_k, w_v, w_o, k_k, k_a, r_k, gn_w, gn_b,
                w0, w1, w2, a0, a1, a2, g1, g2):
    nB, S, D = h.shape
    H, N = RWKV_HEADS, RWKV_HEAD
    dx_p = jnp.pad(h, ((0, 0), (1, 0), (0, 0)))[:, :-1] - h
    dx_n = jnp.pad(h, ((0, 0), (0, 1), (0, 0)))[:, 1:] - h

    def mix(c):
        return h + dx_p * mu_prev[c] + dx_n * mu_next[c]

    def heads(t):
        return t.astype(F32).reshape(nB, S, H, N)

    xw, xa, xg = mix(1), mix(4), mix(5)
    r = mix(0) @ w_r
    k = mix(2) @ w_k
    v = mix(3) @ w_v
    kk = heads(k * k_k)
    kk = kk / jnp.maximum(jnp.sqrt(jnp.sum(kk * kk, axis=-1, keepdims=True)), 1e-12)
    rh, vh = heads(r), heads(v)
    dir_out = []
    for d in range(2):
        w_log = -jax.nn.softplus(-(w0[d] + jnp.tanh(xw @ w1[d]) @ w2[d])) - 0.5
        decay = jnp.exp(-jnp.exp(w_log.astype(F32)))
        a = jax.nn.sigmoid(a0[d] + (xa @ a1[d]) @ a2[d])
        g = jax.nn.sigmoid(xg @ g1[d]) @ g2[d]
        kd = heads(k * (1 + (a - 1) * k_a))
        ins = [rh, heads(decay), kd, vh, kk, heads(a)]
        if d == 1:
            ins = [jnp.flip(t, axis=1) for t in ins]
        o = rwkv7_scan(*ins)
        if d == 1:
            o = jnp.flip(o, axis=1)
        bonus = jnp.sum(rh * kd * r_k.astype(F32), axis=-1, keepdims=True) * vh
        dir_out.append((group_norm(o, gn_w, gn_b) + bonus.reshape(nB, S, D)) * g.astype(F32))
    y = dir_out[0] + dir_out[1]
    return y.astype(h.dtype) @ w_o

def first_inputs(seed: int = 0) -> dict:
    key = jax.random.key(seed)
    ks = iter(jax.random.split(key, 40))

    def nrm(shape, scale):
        return scale * jax.random.normal(next(ks), shape, F32)

    NA, NR, D = N_ATTN_LAYERS, N_RWKV_LAYERS, D_MODEL
    return {
        'x': nrm((BATCH, SEQ, D), 1.0),
        'rel_table': nrm((REL_BUCKETS, N_REL_HEADS), 0.5),
        'norm_g': 1.0 + nrm((DEPTH, 4, D), 0.05),
        'attn_w_in': nrm((NA, D, D_ATTN_IN), D ** -0.5),
        'attn_sink': nrm((NA, N_HEADS_B), 0.5),
        'attn_w_out': nrm((NA, D_ATTN_OUT, D), D_ATTN_OUT ** -0.5),
        'rk_mu_prev': jax.random.uniform(next(ks), (NR, 6, D), F32, 0.0, 0.5),
        'rk_mu_next': jax.random.uniform(next(ks), (NR, 6, D), F32, 0.0, 0.5),
        'rk_w_r': nrm((NR, D, D), D ** -0.5),
        'rk_w_k': nrm((NR, D, D), D ** -0.5),
        'rk_w_v': nrm((NR, D, D), D ** -0.5),
        'rk_w_o': nrm((NR, D, D), D ** -0.5),
        'rk_k_k': 0.85 + nrm((NR, D), 0.05),
        'rk_k_a': 1.0 + nrm((NR, D), 0.05),
        'rk_r_k': nrm((NR, RWKV_HEADS, RWKV_HEAD), 0.1),
        'rk_gn_w': 1.0 + nrm((NR, D), 0.05),
        'rk_gn_b': nrm((NR, D), 0.02),
        'rk_w0': -2.0 + nrm((NR, 2, D), 1.0),
        'rk_w1': nrm((NR, 2, D, DECAY_LORA), D ** -0.5),
        'rk_w2': nrm((NR, 2, DECAY_LORA, D), 0.1 * DECAY_LORA ** -0.5),
        'rk_a0': nrm((NR, 2, D), 0.5),
        'rk_a1': nrm((NR, 2, D, AAA_LORA), D ** -0.5),
        'rk_a2': nrm((NR, 2, AAA_LORA, D), 0.5 * AAA_LORA ** -0.5),
        'rk_g1': nrm((NR, 2, D, GATE_LORA), D ** -0.5),
        'rk_g2': nrm((NR, 2, GATE_LORA, D), GATE_LORA ** -0.5),
        'mlp_w1': nrm((DEPTH, D, D_FF), D ** -0.5),
        'mlp_w2': nrm((DEPTH, D_FF, D), D_FF ** -0.5),
    }

def first_block(x, rel_table, norm_g, attn_w_in, attn_sink, attn_w_out,
              rk_mu_prev, rk_mu_next, rk_w_r, rk_w_k, rk_w_v, rk_w_o, rk_k_k, rk_k_a, rk_r_k,
              rk_gn_w, rk_gn_b, rk_w0, rk_w1, rk_w2, rk_a0, rk_a1, rk_a2, rk_g1, rk_g2,
              mlp_w1, mlp_w2):
    h = x
    for layer in range(DEPTH):
        g = norm_g[layer]
        i = layer // 2
        u = rms_norm(h, g[0])
        if layer % 2 == 0:
            u = attention_mixer(u, attn_w_in[i], attn_sink[i], attn_w_out[i], rel_table)
        else:
            u = rwkv7_mixer(u, rk_mu_prev[i], rk_mu_next[i], rk_w_r[i], rk_w_k[i], rk_w_v[i], rk_w_o[i],
                            rk_k_k[i], rk_k_a[i], rk_r_k[i], rk_gn_w[i], rk_gn_b[i],
                            rk_w0[i], rk_w1[i], rk_w2[i], rk_a0[i], rk_a1[i], rk_a2[i], rk_g1[i], rk_g2[i])
        h = h + rms_norm(u, g[1])
        u = rms_norm(h, g[2])
        u = jnp.square(jax.nn.relu(u @ mlp_w1[layer])) @ mlp_w2[layer]
        h = h + rms_norm(u, g[3])
    return h


DEPTH_2 = 1

PLE_DIM = 256
S5_WIDTH = 512
S5_GROUP = 16
S5_GROUPS = S5_WIDTH // S5_GROUP
S5_STATE = 64
S5_DT_MIN = 1e-3
S5_DT_MAX = 1e-1
LRU_WIDTH = 1280
LRU_HEADS = 10
LRU_HEAD_DIM = LRU_WIDTH // LRU_HEADS
LRU_C = 8.0
CONV_WIDTH = 4
IN_SPLITS = (
    S5_WIDTH,
    2 * S5_WIDTH,
    2 * S5_WIDTH + LRU_WIDTH,
    2 * S5_WIDTH + 2 * LRU_WIDTH,
    2 * S5_WIDTH + 2 * LRU_WIDTH + D_MODEL,
)
IN_COLS = 2 * S5_WIDTH + 2 * LRU_WIDTH + 2 * D_MODEL


def rms_norm_2(x, g):
    xf = x.astype(jnp.float32)
    y = xf * lax.rsqrt(jnp.mean(xf * xf, axis=-1, keepdims=True) + NORM_EPS)
    return (y * g.astype(jnp.float32)).astype(x.dtype)

def _linear_combine(e1, e2):
    a1, b1 = e1
    a2, b2 = e2
    return (a1 * a2, a2 * b1 + b2)

def s5_ssm(u, a_re, a_im, log_dt, b_re, b_im, c_re, c_im, d_skip):
    f32 = jnp.float32
    bsz, seqlen, _ = u.shape
    uf = u.astype(f32)
    ug = uf.reshape(bsz, seqlen, S5_GROUPS, S5_GROUP)
    lam = lax.complex(a_re.astype(f32), a_im.astype(f32))
    dt = jnp.exp(log_dt.astype(f32))[:, None]
    a_bar = jnp.exp(lam * dt)
    zoh = (a_bar - 1.0) / lam
    b = lax.complex(b_re.astype(f32), b_im.astype(f32))
    b_bar = zoh[..., None] * b
    bu = lax.complex(jnp.einsum('blgc,gnc->lbgn', ug, jnp.real(b_bar)),
                     jnp.einsum('blgc,gnc->lbgn', ug, jnp.imag(b_bar)))
    a_seq = jnp.broadcast_to(a_bar[None, None], (seqlen, 1, S5_GROUPS, S5_STATE))
    _, states = lax.associative_scan(_linear_combine, (a_seq, bu), axis=0)
    y = (jnp.einsum('lbgn,gcn->blgc', jnp.real(states), c_re.astype(f32))
         - jnp.einsum('lbgn,gcn->blgc', jnp.imag(states), c_im.astype(f32)))
    y = y.reshape(bsz, seqlen, S5_WIDTH) + d_skip.astype(f32) * uf
    return y.astype(u.dtype)

def causal_depthwise_conv(x, w, b):
    y = lax.conv_general_dilated(
        x, w[:, None, :].astype(x.dtype), window_strides=(1,),
        padding=[(CONV_WIDTH - 1, 0)],
        dimension_numbers=('NWC', 'WIO', 'NWC'),
        feature_group_count=x.shape[-1])
    return y + b

def rg_lru(x, w_a, b_a, w_x, b_x, lam):
    f32 = jnp.float32
    bsz, seqlen, _ = x.shape
    xf = x.astype(f32)
    xh = xf.reshape(bsz, seqlen, LRU_HEADS, LRU_HEAD_DIM)
    r = jax.nn.sigmoid(jnp.einsum('blhi,hij->blhj', xh, w_a.astype(f32)).reshape(bsz, seqlen, LRU_WIDTH)
                       + b_a.astype(f32))
    i = jax.nn.sigmoid(jnp.einsum('blhi,hij->blhj', xh, w_x.astype(f32)).reshape(bsz, seqlen, LRU_WIDTH)
                       + b_x.astype(f32))
    log_a = -LRU_C * r * jax.nn.softplus(-lam.astype(f32))
    a = jnp.exp(log_a)
    mult = jnp.sqrt(-jnp.expm1(2.0 * log_a))
    _, h = lax.associative_scan(_linear_combine, (a, mult * (i * xf)), axis=1)
    return h.astype(x.dtype)

def second_inputs(seed: int = 0) -> dict:
    key = jax.random.key(seed)
    ks = jax.random.split(key, 32)
    f32 = jnp.float32

    def nrm(k, shape, scale):
        return jax.random.normal(k, shape, f32) * scale

    L, D, G, N, C, HD = DEPTH_2, D_MODEL, S5_GROUPS, S5_STATE, S5_GROUP, LRU_HEAD_DIM
    x = nrm(ks[0], (BATCH, SEQ, D), 1.0)
    p = nrm(ks[1], (DEPTH_2, BATCH, SEQ, PLE_DIM), 1.0)
    g_pre = 1.0 + nrm(ks[2], (L, D), 0.05)
    w_in = nrm(ks[3], (L, D, IN_COLS), D ** -0.5)
    s5_a_re = -0.5 + nrm(ks[4], (L, G, N), 0.01)
    s5_a_im = math.pi * jnp.arange(N, dtype=f32)[None, None, :] + nrm(ks[5], (L, G, N), 0.01)
    s5_log_dt = jax.random.uniform(ks[6], (L, G), f32, math.log(S5_DT_MIN), math.log(S5_DT_MAX))
    s5_b_re = nrm(ks[7], (L, G, N, C), C ** -0.5)
    s5_b_im = nrm(ks[8], (L, G, N, C), C ** -0.5)
    s5_c_re = nrm(ks[9], (L, G, C, N), N ** -0.5)
    s5_c_im = nrm(ks[10], (L, G, C, N), N ** -0.5)
    s5_d = nrm(ks[11], (L, S5_WIDTH), 1.0)
    w_glu = nrm(ks[12], (L, S5_WIDTH, 2 * S5_WIDTH), S5_WIDTH ** -0.5)
    w_bs = nrm(ks[13], (L, S5_WIDTH, D), S5_WIDTH ** -0.5)
    conv_w = nrm(ks[14], (L, CONV_WIDTH, LRU_WIDTH), CONV_WIDTH ** -0.5)
    conv_b = nrm(ks[15], (L, LRU_WIDTH), 0.01)
    lru_w_a = nrm(ks[16], (L, LRU_HEADS, HD, HD), HD ** -0.5)
    lru_b_a = nrm(ks[17], (L, LRU_WIDTH), 0.01)
    lru_w_x = nrm(ks[18], (L, LRU_HEADS, HD, HD), HD ** -0.5)
    lru_b_x = nrm(ks[19], (L, LRU_WIDTH), 0.01)
    a_c = jax.random.uniform(ks[20], (L, LRU_WIDTH), f32, 0.9, 0.999)
    sig = a_c ** (1.0 / LRU_C)
    lru_lambda = jnp.log(sig) - jnp.log1p(-sig)
    w_bl = nrm(ks[21], (L, LRU_WIDTH, D), LRU_WIDTH ** -0.5)
    w_out = nrm(ks[22], (L, D, D), D ** -0.5)
    g_post = 1.0 + nrm(ks[23], (L, D), 0.05)
    w_ple = nrm(ks[24], (L, PLE_DIM, D), PLE_DIM ** -0.5)
    w_ple_gate = nrm(ks[25], (L, D, D), D ** -0.5)
    return {
        'x': x, 'p': p, 'g_pre': g_pre, 'w_in': w_in,
        's5_a_re': s5_a_re, 's5_a_im': s5_a_im, 's5_log_dt': s5_log_dt,
        's5_b_re': s5_b_re, 's5_b_im': s5_b_im, 's5_c_re': s5_c_re, 's5_c_im': s5_c_im,
        's5_d': s5_d, 'w_glu': w_glu, 'w_bs': w_bs,
        'conv_w': conv_w, 'conv_b': conv_b,
        'lru_w_a': lru_w_a, 'lru_b_a': lru_b_a, 'lru_w_x': lru_w_x, 'lru_b_x': lru_b_x,
        'lru_lambda': lru_lambda, 'w_bl': w_bl, 'w_out': w_out, 'g_post': g_post,
        'w_ple': w_ple, 'w_ple_gate': w_ple_gate,
    }

def second_block(x, p, g_pre, w_in, s5_a_re, s5_a_im, s5_log_dt, s5_b_re, s5_b_im,
              s5_c_re, s5_c_im, s5_d, w_glu, w_bs, conv_w, conv_b,
              lru_w_a, lru_b_a, lru_w_x, lru_b_x, lru_lambda, w_bl, w_out, g_post,
              w_ple, w_ple_gate):
    for i in range(DEPTH_2):
        h = rms_norm_2(x, g_pre[i])
        proj = h @ w_in[i]
        s5_x, s5_g, lru_x, lru_g, gate_s, gate_l = jnp.split(proj, IN_SPLITS, axis=-1)

        y_s = s5_ssm(s5_x, s5_a_re[i], s5_a_im[i], s5_log_dt[i], s5_b_re[i], s5_b_im[i],
                     s5_c_re[i], s5_c_im[i], s5_d[i])
        glu_a, glu_b = jnp.split(jax.nn.gelu(y_s) @ w_glu[i], 2, axis=-1)
        y_s = glu_a * jax.nn.sigmoid(glu_b) * jax.nn.silu(s5_g)
        z_s = y_s @ w_bs[i]

        c = causal_depthwise_conv(lru_x, conv_w[i], conv_b[i])
        y_l = rg_lru(c, lru_w_a[i], lru_b_a[i], lru_w_x[i], lru_b_x[i], lru_lambda[i])
        z_l = (y_l * jax.nn.silu(lru_g)) @ w_bl[i]

        merged = jax.nn.sigmoid(gate_s) * z_s + jax.nn.sigmoid(gate_l) * z_l
        x = x + rms_norm_2(merged @ w_out[i], g_post[i])

        x = x + (p[i] @ w_ple[i]) * jax.nn.sigmoid(x @ w_ple_gate[i])
    return x


def setup_inputs(seed=0):
    out = dict(first_inputs(seed))
    for name, value in second_inputs(seed + 1).items():
        if name != "x":
            out[name + "_2"] = value
    return out


def reference(
    x, rel_table, norm_g, attn_w_in, attn_sink, attn_w_out, rk_mu_prev, rk_mu_next, rk_w_r,
    rk_w_k, rk_w_v, rk_w_o, rk_k_k, rk_k_a, rk_r_k, rk_gn_w, rk_gn_b, rk_w0, rk_w1, rk_w2,
    rk_a0, rk_a1, rk_a2, rk_g1, rk_g2, mlp_w1, mlp_w2, p_2, g_pre_2, w_in_2, s5_a_re_2,
    s5_a_im_2, s5_log_dt_2, s5_b_re_2, s5_b_im_2, s5_c_re_2, s5_c_im_2, s5_d_2, w_glu_2, w_bs_2,
    conv_w_2, conv_b_2, lru_w_a_2, lru_b_a_2, lru_w_x_2, lru_b_x_2, lru_lambda_2, w_bl_2,
    w_out_2, g_post_2, w_ple_2, w_ple_gate_2,
):
    x = first_block(
        x, rel_table, norm_g, attn_w_in, attn_sink, attn_w_out, rk_mu_prev, rk_mu_next, rk_w_r,
        rk_w_k, rk_w_v, rk_w_o, rk_k_k, rk_k_a, rk_r_k, rk_gn_w, rk_gn_b, rk_w0, rk_w1, rk_w2,
        rk_a0, rk_a1, rk_a2, rk_g1, rk_g2, mlp_w1, mlp_w2,
    )
    return second_block(
        x, p_2, g_pre_2, w_in_2, s5_a_re_2, s5_a_im_2, s5_log_dt_2, s5_b_re_2, s5_b_im_2,
        s5_c_re_2, s5_c_im_2, s5_d_2, w_glu_2, w_bs_2, conv_w_2, conv_b_2, lru_w_a_2, lru_b_a_2,
        lru_w_x_2, lru_b_x_2, lru_lambda_2, w_bl_2, w_out_2, g_post_2, w_ple_2, w_ple_gate_2,
    )


_drawn_inputs = setup_inputs


def setup_inputs(seed=0):
    import zlib

    import numpy as np

    out = dict(_drawn_inputs(seed))
    spreads = {}
    factors = {'attn_sink': 8.0,
     'rk_gn_b': 4.613,
     'rk_w1': 5.709,
     'rk_w2': 6.013,
     's5_a_re_2': 64.0,
     's5_a_im_2': 37.576,
     's5_log_dt_2': 45.056,
     's5_b_re_2': 52.864,
     's5_b_im_2': 54.632,
     's5_c_re_2': 52.768,
     's5_c_im_2': 51.952,
     'conv_b_2': 5.697,
     'lru_b_a_2': 44.761,
     'lru_b_x_2': 8.0,
     'g_post_2': 2.849}
    for name, (base, spread) in spreads.items():
        noise = np.random.default_rng([zlib.crc32(name.encode()), seed]).standard_normal(out[name].shape)
        drawn = base * np.exp(spread * noise) if base else spread * noise
        out[name] = __import__('jax').numpy.asarray(drawn.astype(out[name].dtype))
    for name, factor in factors.items():
        out[name] = (out[name] * factor).astype(out[name].dtype)
    return out
```

```python
from contextlib import ExitStack

import numpy as np

import concourse.bass as bass
from concourse import mybir

P = 128
SEQ = 512
D = 1024
DT = D // P
FF = 4 * D
FT = FF // P
HEAD = 64
NORM_EPS = 1e-6
GN_EPS = 64e-5
NEG = -1e30
ARENA = 30800
UPB = 8
RING = 8
BLOCK = UPB * P
CH = 64
NCH = SEQ // CH
LEVELS = 6
S5W, S5G, S5N = 512, 32, 64
ST = S5G * S5N // P
XT = S5W // P
LRUW = 1280
LT = LRUW // P
CONV = 4
PLE = 256
TWO_PI = 6.283185
PI_BELOW = 3.1415925
ROUND = 1.5 * 2.0 ** 23
ROUND12 = 1.5 * 2.0 ** 11
TURN_PARTS = [6.28125, 0.0019350051879882812, 3.01991598196e-07]
DECAY = float(np.exp(-0.5))
SINK_W = 3 * P + SEQ
PAD = SEQ + 2
LPAD = SEQ + CONV - 1

F32 = mybir.dt.float32
ALU = mybir.AluOpType
ACT = mybir.ActivationFunctionType
AX = mybir.AxisListType

DENSE = [
    ("qk", 13, DT), ("v", 5, DT), ("attn_out", DT, DT),
    ("up0", FT, DT), ("down0", DT, FT),
    ("lora_w", 1, DT), ("lora_a", 1, DT), ("lora_g", 2, DT),
    ("r", DT, DT), ("k", DT, DT), ("rv", DT, DT), ("o", DT, DT),
    ("up1", FT, DT), ("down1", DT, FT),
    ("w_in", 40, DT), ("w_in_end", 2 * XT + 2 * LT + 2 * DT - 40, DT), ("glu", 2 * XT, XT), ("w_bs", DT, XT),
    ("lru", 2 * LT, 1), ("w_bl", DT, LT), ("w_out", DT, DT), ("ple", DT, PLE // P), ("gate", DT, DT),
]


def plan():
    first_block, first_tile, last_tile = {}, {}, []
    tile = 0
    for name, n, k in DENSE:
        first_block[name], first_tile[name] = len(last_tile), tile
        units = n * k
        for b in range(-(-units // UPB)):
            last = min(units, (b + 1) * UPB) - 1
            last_tile.append(tile + last // k + 1)
        tile += n
    return first_block, first_tile, last_tile


FIRST_BLOCK, FIRST_TILE, LAST_TILE = plan()
SHAPE = {name: (n, k) for name, n, k in DENSE}
NBLOCKS = len(LAST_TILE)

COLS = {}
_at = 0
for _name, _n in [("norm_g", 8 * DT), ("mu_prev", 6 * DT), ("mu_next", 6 * DT), ("k_k", DT), ("k_a", DT),
                  ("r_k", DT), ("gn_w", DT), ("gn_b", DT), ("w0", 2 * DT), ("a0", 2 * DT), ("g_pre", DT),
                  ("g_post", DT), ("a_re", ST), ("a_im", ST), ("log_dt", ST), ("s5_d", XT),
                  ("conv_w", CONV * LT), ("conv_b", LT), ("b_a", LT), ("b_x", LT), ("lam", LT),
                  ("sink", 16)]:
    COLS[_name] = _at
    _at += _n
NCOLS = _at

CONSTS = {}
_at = 0
for _name, _n in [("mean", P), ("head_sum", P), ("head_mean", P), ("ident", P), ("iota", SEQ), ("carry", SEQ),
                  ("eye", CH), ("incl", 2 * CH), ("strict", 2 * CH), ("level_n", 2 * CH),
                  ("level", 2 * LEVELS * CH), ("eps", 4)]:
    CONSTS[_name] = _at
    _at += _n
NCONST = _at


def constants():
    c = np.zeros((P, NCONST), np.float32)

    def put(name, a):
        c[:, CONSTS[name]:CONSTS[name] + a.shape[1]] = a

    heads = np.kron(np.eye(P // HEAD), np.ones((HEAD, HEAD)))
    put("mean", np.full((P, P), 1.0 / D))
    put("head_sum", heads)
    put("head_mean", heads / HEAD)
    put("ident", np.eye(P))
    put("iota", np.broadcast_to(np.arange(SEQ, dtype=np.float32), (P, SEQ)))
    put("carry", np.broadcast_to(np.arange(SEQ) % CH != 0, (P, SEQ)))
    row, col = np.arange(CH)[:, None], np.arange(CH)[None, :]

    def both(m):
        return np.concatenate([m, m], axis=0)

    def level(rows_first, l):
        w = 1 << l
        same = (row // (2 * w)) == (col // (2 * w))
        low, high = (row, col) if rows_first else (col, row)
        return same & (low // w % 2 == 0) & (high // w % 2 == 1)

    put("eye", both(np.eye(CH)))
    put("incl", np.concatenate([both(row <= col), both(row >= col)], axis=1))
    put("strict", np.concatenate([both(row < col), both(row > col)], axis=1))
    put("level_n", np.concatenate([both(level(True, 0)), both(level(False, 0))], axis=1))
    put("level", np.concatenate([both(level(d == 1, l)) for d in range(2) for l in range(LEVELS)], axis=1))
    put("eps", np.broadcast_to(np.array([NORM_EPS, GN_EPS, 0.0, 1.0], np.float32), (P, 4)))
    return c


def bias_constants():
    d = np.arange(2 * SEQ) - (SEQ - 1)
    n = np.abs(d)
    nf = np.maximum(n, 1).astype(np.float32)
    large = 8 + (np.log(nf / np.float32(8)) / np.float32(np.log(1024 / 8)) * np.float32(8)).astype(np.int32)
    bucket = np.where(d > 0, 16, 0) + np.where(n < 8, n, np.minimum(large, 15))
    onehot = np.zeros((32, 2 * SEQ), np.float32)
    onehot[bucket, np.arange(2 * SEQ)] = 1.0
    count = sum(((n % dil == 0) & (n // dil <= window // 2 // dil)).astype(np.int64)
                for window, dil in ((128, 1), (512, 4), (2048, 16)))
    line_a = np.where(count > 0, np.log(np.maximum(count, 1)), NEG)
    line_b = np.where(n <= 128, 0.0, NEG)
    lines = np.concatenate([np.broadcast_to(line_a, (8, 2 * SEQ)), np.broadcast_to(line_b, (8, 2 * SEQ))])
    return onehot, lines.astype(np.float32)




def program(nc, t, out):
    ctx = ExitStack()
    with ctx:
        def sb(name, width):
            return ctx.enter_context(nc.sbuf_tensor(name, [P, width], F32))

        sems = {}

        def sem(name):
            if name not in sems:
                sems[name] = ctx.enter_context(nc.semaphore(name))
            return sems[name]

        ring = sb("ring", RING * BLOCK)
        h = sb("h", DT * SEQ)
        u = sb("u", DT * PAD)
        cols = sb("cols", NCOLS)
        consts = sb("consts", NCONST)
        sq = sb("sq", 2 * SEQ)
        rstd = sb("rstd", SEQ)
        small = sb("small", 64)
        der = sb("der", 6 * DT + DT + 8 * ST + 2 * LT)
        s5c = sb("s5c", ST * 2 * 32)
        arena = sb("arena", ARENA)

        ps = ctx.enter_context(nc.psum_tensor("ps", [P, 8 * SEQ], F32))
        lines_dram = nc.dram_tensor("bias_lines", [16, 2 * SEQ], F32)

        top = [0]

        def take(width):
            a = arena[:, top[0]:top[0] + width]
            top[0] += width
            assert top[0] <= ARENA, top[0]
            return a

        def bank(b, width=SEQ):
            return ps[:, b * SEQ:b * SEQ + width]

        def tile(buf, i):
            return buf[:, bass.ts(i, SEQ)]

        def u_tile(i, shift=0):
            return u[:, bass.ds(i * PAD + 1 + shift, SEQ)]

        def col(name, i=0):
            return cols[:, bass.ds(COLS[name] + i, 1)]

        def const(name, i=0, width=P):
            return consts[:, CONSTS[name] + i * width:CONSTS[name] + (i + 1) * width]

        def square_tile(n, x):
            return u_tile(x) if n % 2 else sq[:, x % 2 * SEQ:(x % 2 + 1) * SEQ]

        def chunks(a):
            return a.rearrange("p (c s) -> p c s", c=NCH)

        def mask(name, i):
            return const(name, i, CH).unsqueeze(1).to_broadcast([P, NCH, CH])

        MU0, OMKA, DT_, X_, TH_, MAG, PHH, PHL, ZRE, ZIM = [
            0, 48, 56, 56 + ST, 56 + 2 * ST, 56 + 3 * ST, 56 + 4 * ST, 56 + 5 * ST, 56 + 6 * ST, 56 + 7 * ST]
        SP4 = 56 + 8 * ST

        def derived(at, n=1):
            return der[:, at:at + n]

        wbuf = take(DT * SEQ)
        stage0 = top[0]
        qT = take(DT * SEQ)
        kT = take(5 * SEQ)
        vtok = take(4 * 640)
        attnT = take(DT * SEQ)
        bias = [take(SINK_W) for _ in range(4)]
        q_st = [take(SEQ) for _ in range(2)]
        k_st = take(SEQ)
        s_sb = [take(SEQ) for _ in range(2)]
        p_sb = [take(SEQ) for _ in range(2)]
        pt_sb = [take(SEQ) for _ in range(2)]
        o_tok = [take(P) for _ in range(2)]
        line_sb, line_const = attnT[0:16, 0:2 * SEQ], attnT[0:16, 2 * SEQ:4 * SEQ]
        rel_sb, onehot = attnT[0:32, 4 * SEQ:4 * SEQ + 16], attnT[0:32, 5 * SEQ:7 * SEQ]
        bias0 = stage0 + (DT + 5 + DT) * SEQ + 4 * 640
        s5_in = arena[:, bias0:bias0 + ST * 64]
        s5_t = [arena[:, bias0 + ST * (64 + 32 * n):bias0 + ST * (96 + 32 * n)] for n in range(2)]
        tmp0 = bias0 + ST * 128
        top[0] = stage0
        mid = take(FT * SEQ)
        relu = [take(SEQ) for _ in range(2)]
        top[0] = stage0
        rT = wbuf
        kk = take(DT * SEQ)
        kTr = take(DT * SEQ)
        vTr = take(DT * SEQ)
        lo_w, lo_a = take(SEQ), take(SEQ)
        lo_g = [take(SEQ) for _ in range(2)]
        lora2 = take(6 * P)
        pair0 = top[0]
        mixb = [take(DT * SEQ) for _ in range(2)]
        top[0] = pair0
        spare = [u[:, n * SEQ:(n + 1) * SEQ] for n in range(DT)]
        spare += [take(SEQ) for _ in range((ARENA - top[0]) // SEQ - 2)]
        names = ["al", "ro", "ka", "be", "kd", "g", "L", "Ma", "Mb", "Mr", "T", "TT", "X", "LM"]
        R = [dict(zip(names, spare[len(names) * d:])) for d in range(2)]
        vt, v_st = sq[:, 0:SEQ], sq[:, SEQ:2 * SEQ]
        st_w = [take(CH) for _ in range(2)]
        st_u = [take(CH) for _ in range(2)]
        st_s = [[take(CH) for _ in range(2)] for _ in range(2)]
        st_p = [take(CH) for _ in range(2)]
        p_end = [take(NCH) for _ in range(2)]
        top[0] = stage0
        s5x = take(XT * SEQ)
        s5g = take(XT * SEQ)
        lrug = take(LT * SEQ)
        gs = take(DT * SEQ)
        gl = take(DT * SEQ)
        lrux = take(LT * LPAD)
        free0 = [take(SEQ) for _ in range((ARENA - top[0]) // SEQ)]
        sgt = free0[0:2]
        s5b = u[:, 0:2 * ST * P]
        free1 = [tile(wbuf, n) for n in range(DT)] + free0
        V = [dict(zip(["A", "B", "S", "C", "v1", "v2", "v3", "v4"], free1[8 * n:])) for n in range(2)]
        conv = [u[:, n * SEQ:(n + 1) * SEQ] for n in range(DT)] + [tile(s5x, n) for n in range(2)]
        rate = [tile(wbuf, n) for n in range(DT)] + [tile(s5x, n) for n in range(2, 4)]
        i_t, root, fa, fb = free0[0:2], free0[2:4], free0[4:6], free0[6:8]
        pT = s5g[:, 0:2 * SEQ]

        def tmp(n):
            return arena[:, tmp0 + n * ST:tmp0 + (n + 1) * ST]

        y_ready, y_taken = sem("y_ready"), sem("y_taken")
        landed = [sem(f"weights_landed_{s}") for s in range(RING)]
        block = ctx.enter_context(nc.Block())

        @block.sync
        def _(sp):
            def stream(first, end):
                b = first
                while b < end:
                    step, m = None, 1
                    while b >= RING and b + RING * (m + 1) <= end:
                        now = [LAST_TILE[b + RING * m + j - RING] for j in range(RING)]
                        was = [LAST_TILE[b + RING * (m - 1) + j - RING] for j in range(RING)]
                        gaps = {x - y for x, y in zip(now, was)}
                        if len(gaps) != 1 or step not in (None, min(gaps)):
                            break
                        step, m = min(gaps), m + 1
                    if m >= 2:
                        with sp.Fori(0, m) as i:
                            for j in range(RING):
                                sp.wait_ge(y_ready, i * step + LAST_TILE[b + j - RING])
                                slot = (b + j) % RING
                                sp.dma_start(ring[:, slot * BLOCK:(slot + 1) * BLOCK],
                                             t["wall"][bass.ds(i * RING + b + j, 1)].rearrange("a p n -> (a p) n")
                                             ).then_inc(landed[slot], 16)
                        b += RING * m
                    else:
                        if b >= RING:
                            sp.wait_ge(y_ready, LAST_TILE[b - RING])
                        slot = b % RING
                        sp.dma_start(ring[:, slot * BLOCK:(slot + 1) * BLOCK], t["wall"][b]).then_inc(landed[slot], 16)
                        b += 1

            sp.dma_start(h[:, :], t["x"]).then_inc(sem("x_loaded"), 16)
            sp.dma_start(consts[:, :], t["consts"]).then_inc(sem("consts_loaded"), 16)
            sp.dma_start(cols[:, :], t["cols"]).then_inc(sem("cols_loaded"), 16)
            sp.dma_start(rel_sb, t["rel_table"]).then_inc(sem("rel_loaded"), 16)
            sp.dma_start(onehot, t["onehot"]).then_inc(sem("onehot_loaded"), 16)
            sp.dma_start(line_const, t["lines"]).then_inc(sem("line_const_loaded"), 16)
            sp.dma_start(s5_in, t["s5_c"]).then_inc(sem("s5_c_loaded"), 16)
            stream(0, FIRST_BLOCK["attn_out"] + RING)

            def load_bias(i, half):
                for e in range(2):
                    head = i * 2 + e if half == 0 else i + 8 + 4 * e
                    src = bass.AP(lines_dram, head * (2 * SEQ), [[1, P], [1, SINK_W]])
                    sp.dma_start(bias[2 * half + e], src).then_inc(sem(f"bias_landed_{2 * half + e}"), 16)

            sp.wait_ge(sem("lines_stored"), 16)
            sp.wait_ge(sem("s5c_ready"), 1)
            load_bias(0, 0)
            load_bias(0, 1)
            with sp.Fori(1, 4) as i:
                for half in range(2):
                    sp.wait_ge(sem("s_biased"), i * 16 + (8 * half - 8))
                    load_bias(i, half)
            stream(FIRST_BLOCK["attn_out"] + RING, FIRST_BLOCK["o"] + RING)

            def load_lora2(i):
                sp.dma_start(lora2, t["lora2"][bass.ds(i, 1)].rearrange("a p n -> (a p) n")
                             ).then_inc(sem("lora2_landed"), 16)

            sp.wait_ge(y_ready, FIRST_TILE["r"])
            load_lora2(0)
            with sp.Fori(1, DT) as i:
                sp.wait_ge(sem("z_ready"), i * 6)
                load_lora2(i)
            stream(FIRST_BLOCK["o"] + RING, NBLOCKS)

        @block.tensor
        def _(pe):
            def dense(name, rhs, steps=1, rhs_ready=None, first=0, count=None):
                n, k = SHAPE[name]
                per = n // steps
                b0, t0 = FIRST_BLOCK[name], FIRST_TILE[name]

                def step(i):
                    for j in range(per):
                        if t0 + j >= 2:
                            pe.wait_ge(y_taken, i * per + (t0 + j - 1))
                        for x in range(k):
                            unit = j * k + x
                            b = b0 + unit // UPB
                            if unit % UPB == 0 or x == 0:
                                rounds = per * k // UPB // RING if steps > 1 else 0
                                pe.wait_ge(landed[b % RING], i * (16 * rounds) + 16 * (b // RING + 1))
                            if rhs_ready is not None:
                                rhs_ready(j, x)
                            at = (b % RING) * BLOCK + unit % UPB * P
                            mm = nc.tensor.matmul(bank((t0 + j) % 2), ring[:, at:at + P], rhs(x),
                                                  start=x == 0, stop=x == k - 1)
                        mm.then_inc(y_ready, 1)

                if steps == 1:
                    step(0)
                else:
                    assert per % 2 == 0 and per * k % (UPB * RING) == 0
                    with pe.Fori(0, steps) as i:
                        step(i)

            def mean_square(n):
                for x in range(DT):
                    pe.wait_ge(sem("sq_ready"), DT * n + x + 1)
                    if x == 0 and n:
                        pe.wait_ge(sem("rms_ready"), n)
                    nc.tensor.matmul(bank(7), const("mean"), square_tile(n, x),
                                     start=x == 0, stop=x == DT - 1).then_inc(sem("sq_used"), 1)

            def normed_tile(n):
                return lambda j, x: pe.wait_ge(sem("normed"), DT * n + x + 1) if j == 0 else None

            pe.wait_ge(sem("rel_loaded"), 16)
            pe.wait_ge(sem("onehot_loaded"), 16)
            for half in range(2):
                mm = nc.tensor.matmul(bank(5 + half)[0:16, :], rel_sb, onehot[:, half * SEQ:(half + 1) * SEQ],
                                      start=True, stop=True)
            mm.then_inc(sem("lines_ready"), 1)

            pe.wait_ge(sem("consts_loaded"), 16)
            mean_square(0)
            dense("qk", u_tile, rhs_ready=normed_tile(0))
            t0, b0 = FIRST_TILE["v"], FIRST_BLOCK["qk"]
            for j in range(5):
                pe.wait_ge(y_taken, t0 + j - 1)
                first = SHAPE["qk"][0] * DT + j * DT
                b = b0 + first // UPB
                pe.wait_ge(landed[b % RING], 16 * (b // RING + 1))
                for tok in range(4):
                    for x in range(DT):
                        at = (b % RING) * BLOCK + x * P
                        mm = nc.tensor.matmul(bank((t0 + j) % 2)[:, tok * P:(tok + 1) * P],
                                              u[:, x * PAD + 1 + tok * P:x * PAD + 1 + (tok + 1) * P],
                                              ring[:, at:at + P], start=x == 0, stop=x == DT - 1)
                mm.then_inc(y_ready, 1)
            pe.wait_ge(y_taken, FIRST_TILE["attn_out"])

            with pe.Fori(0, 4) as i:
                def place(n):
                    return n // 8, n % 8 // 2, n % 2

                def scores(n):
                    half, qi, e = place(n)
                    if n % 8 == 0:
                        pe.wait_ge(sem("q_staged"), i * 2 + (half + 1))
                        pe.wait_ge(sem("k_staged"), i + 1)
                    if n >= 2:
                        pe.wait_ge(sem("s_biased"), i * 16 + (n - 1))
                    rows = slice(e * HEAD, (e + 1) * HEAD)
                    keys = k_st[rows, :] if half == 0 else kT[rows, 4 * SEQ:5 * SEQ]
                    nc.tensor.matmul(bank(2 + n % 2), q_st[half][rows, qi * P:(qi + 1) * P], keys,
                                     start=True, stop=True).then_inc(sem("s_ready"), 1)

                def turn(n):
                    pe.wait_ge(sem("p_ready"), i * 16 + (n + 1))
                    if n >= 2:
                        pe.wait_ge(sem("pt_taken"), i * 16 + (n - 1))
                    for x in range(4):
                        tr = nc.tensor.transpose(bank(4 + n % 2)[:, x * P:(x + 1) * P],
                                                 p_sb[n % 2][:, x * P:(x + 1) * P], const("ident"))
                    tr.then_inc(sem("pt_ready"), 1)

                def values(n):
                    half, qi, e = place(n)
                    pe.wait_ge(sem("pt_taken"), i * 16 + (n + 1))
                    if n >= 2:
                        pe.wait_ge(sem("o_taken"), i * 16 + (n - 1))
                    for x in range(4):
                        at = x * 640 + e * HEAD
                        v = vtok[:, bass.ds(i * P + at, HEAD)] if half == 0 else vtok[:, at + 512:at + 512 + HEAD]
                        mm = nc.tensor.matmul(bank(6 + n % 2, HEAD),
                                              pt_sb[n % 2][:, x * P:(x + 1) * P], v, start=x == 0, stop=x == 3)
                    mm.then_inc(sem("o_ready"), 1)

                def turn_out(m):
                    pe.wait_ge(sem("o_taken"), i * 16 + (2 * m + 2))
                    if m >= 2:
                        pe.wait_ge(sem("ot_taken"), i * 8 + m)
                    nc.tensor.transpose(bank(m % 2, P), o_tok[m % 2], const("ident")
                                        ).then_inc(sem("ot_ready"), 1)

                pe.wait_ge(sem("ot_taken"), i * 8 + 1)
                scores(0)
                scores(1)
                for n in range(16):
                    turn(n)
                    if n + 2 < 16:
                        scores(n + 2)
                    if n >= 1:
                        values(n - 1)
                    if n >= 3 and n % 2:
                        turn_out((n - 3) // 2)
                values(15)
                turn_out(7)

            pe.wait_ge(sem("ot_taken"), 33)
            dense("attn_out", lambda x: tile(attnT, x))
            mean_square(1)
            def mlp(n, up, down, first_norm):
                mean_square(first_norm)
                for x in range(DT):
                    pe.wait_ge(sem("normed"), DT * first_norm + x + 1)
                dense(up, u_tile, steps=4)
                pe.wait_ge(y_taken, FIRST_TILE[down])
                dense(down, lambda x: tile(mid, x), steps=4)
                mean_square(first_norm + 1)

            mlp(0, "up0", "down0", 2)
            mean_square(4)
            for m, (name, waits) in enumerate([("lora_w", 1), ("lora_a", 1), ("lora_g", 1), ("r", 1), ("k", 1), ("rv", 1)]):
                dense(name, lambda x: tile(mixb[m % 2], x),
                      rhs_ready=lambda j, x: pe.wait_ge(sem("mixed"), DT * m + x + 1) if j == 0 else None)
            for x in range(DT):
                pe.wait_ge(sem("kk_squared"), x + 1)
                if x == 0:
                    pe.wait_ge(y_taken, FIRST_TILE["o"])
                if x >= 2:
                    pe.wait_ge(sem("kk_clamped"), x - 1)
                nc.tensor.matmul(bank(6 + x % 2), const("head_sum"), sq[:, x % 2 * SEQ:(x % 2 + 1) * SEQ],
                                 start=True, stop=True).then_inc(sem("kk_summed"), 1)
            pe.wait_ge(sem("kk_ready"), DT)

            def each(out, lhsT, rhs):
                pe.nop(nofuse=True)
                for c in range(NCH):
                    for e in range(2):
                        rows, at = slice(e * HEAD, (e + 1) * HEAD), slice(c * CH, (c + 1) * CH)
                        mm = nc.tensor.matmul(out[rows, at], lhsT[rows, at], rhs[rows, at], start=True, stop=True)
                return mm

            def each_turned(out, a):
                pe.nop(nofuse=True)
                for c in range(NCH):
                    for e in range(2):
                        rows, at = slice(e * HEAD, (e + 1) * HEAD), slice(c * CH, (c + 1) * CH)
                        mm = nc.tensor.matmul(out[rows, at], a[rows, at], const("eye", 0, CH)[rows, :],
                                              start=True, stop=True)
                return mm

            with pe.Fori(0, DT) as i:
                pe.wait_ge(sem("pair_done"), i + 1)
                pe.wait_ge(sem("lora2_landed"), i * 16 + 16)
                for n, hidden in enumerate([lo_w, lo_w, lo_a, lo_a, lo_g[0], lo_g[1]]):
                    nc.tensor.matmul(bank(n), lora2[:, n * P:(n + 1) * P], hidden, start=True, stop=True
                                     ).then_inc(sem("z_ready"), 1)
                A, B, C, O = [[bank(4 * d + x) for d in range(2)] for x in range(4)]
                pe.wait_ge(sem("z_taken"), i * 6 + 6)
                pe.wait_ge(sem("v_staged"), i + 1)
                for d in range(2):
                    pe.wait_ge(sem("features_v"), i * 2 + (d + 1))
                    pe.wait_ge(sem("features_p"), i * 2 + (d + 1))
                    each(A[d], R[d]["be"], R[d]["al"]).then_inc(sem("scores_ready"), 1)
                for d in range(2):
                    each(B[d], R[d]["al"], R[d]["be"]).then_inc(sem("scores_ready"), 1)
                for d in range(2):
                    each(C[d], R[d]["ka"], R[d]["al"]).then_inc(sem("scores_ready"), 1)
                for d in range(2):
                    each(O[d], R[d]["ka"], R[d]["ro"]).then_inc(sem("scores_ready"), 1)
                for d in range(2):
                    pe.wait_ge(sem("masked_v"), i * 8 + (1 + d))
                    each(A[d], R[d]["be"], R[d]["ro"]).then_inc(sem("scores_ready"), 1)
                for d in range(2):
                    pe.wait_ge(sem("copied_a"), i * 7 + (1 + d))
                    each_turned(B[d], R[d]["be"]).then_inc(sem("scores_ready"), 1)
                for d in range(2):
                    pe.wait_ge(sem("masked_v"), i * 8 + (3 + d))
                    each_turned(C[d], R[d]["ka"]).then_inc(sem("scores_ready"), 1)
                pe.wait_ge(sem("masked_v"), i * 8 + 5)
                each_turned(O[0], v_st).then_inc(sem("scores_ready"), 1)
                pe.wait_ge(sem("masked_v"), i * 8 + 8)
                pe.wait_ge(sem("copied_a"), i * 7 + 7)
                pe.wait_ge(sem("t_started"), i * 4 + 4)
                for l in range(1, LEVELS):
                    for d in range(2):
                        n = 2 * (l - 1) + d
                        pe.wait_ge(sem("level_masked"), i * 10 + (n + 1))
                        if l > 1:
                            pe.wait_ge(sem("t_updated"), i * 10 + (n - 1))
                        each(A[d], R[d]["LM"], R[d]["T"]).then_inc(sem("x_ready"), 1)
                    for d in range(2):
                        n = 2 * (l - 1) + d
                        pe.wait_ge(sem("x_taken"), i * 10 + (n + 1))
                        mm = each(B[d], R[d]["TT"], R[d]["X"])
                        if l < LEVELS - 1:
                            mm = each(C[d], R[d]["X"], R[d]["TT"])
                        mm.then_inc(sem("dt_ready"), 1)
                for j in range(NCH):
                    for d in range(2):
                        n = 2 * j + d
                        c = j if d == 0 else NCH - 1 - j
                        at = slice(c * CH, (c + 1) * CH)
                        if j == 0:
                            pe.wait_ge(sem("t_updated"), i * 10 + (9 + d))
                        else:
                            pe.wait_ge(sem("state_ready"), i * 14 + (n - 1))
                        pe.nop(nofuse=True)
                        for e in range(2):
                            rows = slice(e * HEAD, (e + 1) * HEAD)
                            mm = nc.tensor.matmul(A[d][rows, 0:CH], R[d]["Ma"][rows, at], vt[rows, at],
                                                  start=True, stop=j == 0)
                            if j:
                                mm = nc.tensor.matmul(A[d][rows, 0:CH], R[d]["al"][rows, at], st_s[d][j % 2][rows, :],
                                                      start=False, stop=True)
                        mm.then_inc(sem("w_ready"), 1)
                    for d in range(2):
                        n = 2 * j + d
                        c = j if d == 0 else NCH - 1 - j
                        at = slice(c * CH, (c + 1) * CH)
                        pe.wait_ge(sem("w_taken"), i * 16 + (n + 1))
                        pe.nop(nofuse=True)
                        for e in range(2):
                            rows = slice(e * HEAD, (e + 1) * HEAD)
                            mm = nc.tensor.matmul(B[d][rows, 0:CH], R[d]["T"][rows, at], st_w[d][rows, :],
                                                  start=True, stop=True)
                        mm.then_inc(sem("u_ready"), 1)
                    for d in range(2):
                        n = 2 * j + d
                        c = j if d == 0 else NCH - 1 - j
                        at = slice(c * CH, (c + 1) * CH)
                        pe.wait_ge(sem("u_taken"), i * 16 + (n + 1))
                        pe.nop(nofuse=True)
                        if j < NCH - 1:
                            for e in range(2):
                                rows = slice(e * HEAD, (e + 1) * HEAD)
                                nc.tensor.matmul(C[d][rows, 0:CH], R[d]["be"][rows, at], st_u[d][rows, :],
                                                 start=True, stop=False)
                                mm = nc.tensor.matmul(C[d][rows, 0:CH], R[d]["ka"][rows, at], vt[rows, at],
                                                      start=False, stop=True)
                            mm.then_inc(sem("s_ready_rw"), 1)
                        for e in range(2):
                            rows = slice(e * HEAD, (e + 1) * HEAD)
                            nc.tensor.matmul(O[d][rows, at], st_u[d][rows, :], R[d]["Mb"][rows, at],
                                             start=True, stop=False)
                            mm = nc.tensor.matmul(O[d][rows, at], vt[rows, at], R[d]["Mr"][rows, at],
                                                  start=False, stop=j == 0)
                            if j:
                                mm = nc.tensor.matmul(O[d][rows, at], st_s[d][j % 2][rows, :], R[d]["ro"][rows, at],
                                                      start=False, stop=True)
                        mm.then_inc(sem("o_ready_rw"), 1)
                for d in range(2):
                    pe.wait_ge(sem("o_copied"), i * 2 + (d + 1))
                    nc.tensor.matmul(A[d], const("head_mean"), R[d]["L"], start=True, stop=True
                                     ).then_inc(sem("mean_ready"), 1)
                for d in range(2):
                    nc.tensor.matmul(C[d], const("head_sum"), R[d]["kd"], start=True, stop=True
                                     ).then_inc(sem("bonus_ready"), 1)
                for d in range(2):
                    pe.wait_ge(sem("o_squared"), i * 2 + (d + 1))
                    nc.tensor.matmul(B[d], const("head_mean"), R[d]["Ma"], start=True, stop=True
                                     ).then_inc(sem("var_ready"), 1)
            pe.wait_ge(sem("pair_done"), DT + 1)
            dense("o", lambda x: tile(rT, x))
            mean_square(5)
            mlp(1, "up1", "down1", 6)
            mean_square(8)
            for x in range(DT):
                pe.wait_ge(sem("normed"), DT * 8 + x + 1)
            dense("w_in", u_tile, steps=5)
            dense("w_in_end", u_tile)
            pe.wait_ge(sem("s5b_landed"), 16)
            pe.wait_ge(y_taken, FIRST_TILE["glu"])

            def s5_out(j):
                pe.wait_ge(sem("s5_turned"), 2 * (j + 1))
                m, rows = j // 4, slice(j % 4 * 32, j % 4 * 32 + 32)
                if j % 4 == 0 and m >= 2:
                    pe.wait_ge(sem("s5_skipped"), m - 1)
                nc.tensor.matmul(bank(6 + m % 2)[rows, :], s5c[:, j * 64:j * 64 + 32], V[j % 2]["v1"],
                                 start=True, stop=False)
                nc.tensor.matmul(bank(6 + m % 2)[rows, :], s5c[:, j * 64 + 32:j * 64 + 64], V[j % 2]["v3"],
                                 start=False, stop=True).then_inc(sem("s5_out"), 1)

            for j in range(ST):
                if j >= 2:
                    pe.wait_ge(sem("s5_in_taken"), 4 * (j - 1))
                for x in range(2):
                    nc.tensor.matmul(bank(2 + 2 * (j % 2) + x), s5b[:, (2 * j + x) * P:(2 * j + x + 1) * P],
                                     tile(s5x, j // 4), start=True, stop=True).then_inc(sem("s5_in"), 1)
                if j >= 1:
                    s5_out(j - 1)
            s5_out(ST - 1)
            dense("glu", lambda x: tile(s5x, x),
                  rhs_ready=lambda j, x: pe.wait_ge(sem("gelu_ready"), x + 1) if j == 0 else None)
            dense("w_bs", lambda x: tile(s5g, x),
                  rhs_ready=lambda j, x: pe.wait_ge(sem("s5_gated"), x + 1) if j == 0 else None)
            t0, b0 = FIRST_TILE["lru"], FIRST_BLOCK["lru"]
            for n in range(2 * LT):
                pe.wait_ge(y_taken, t0 + n - 1)
                if n % UPB == 0:
                    b = b0 + n // UPB
                    pe.wait_ge(landed[b % RING], 16 * (b // RING + 1))
                at = ((b0 + n // UPB) % RING) * BLOCK + n % UPB * P
                pe.wait_ge(sem("conv_ready"), n // 2 + 1)
                nc.tensor.matmul(bank((t0 + n) % 2), ring[:, at:at + P], conv[n // 2], start=True, stop=True
                                 ).then_inc(y_ready, 1)
            dense("w_bl", lambda x: tile(lrug, x),
                  rhs_ready=lambda j, x: pe.wait_ge(sem("lru_gated"), x + 1) if j == 0 else None)
            dense("w_out", lambda x: tile(gs, x),
                  rhs_ready=lambda j, x: pe.wait_ge(sem("merged"), x + 1) if j == 0 else None)
            mean_square(9)
            pe.wait_ge(sem("p_loaded"), 16)
            dense("ple", lambda x: pT[:, x * SEQ:(x + 1) * SEQ])
            dense("gate", lambda x: tile(h, x),
                  rhs_ready=lambda j, x: pe.wait_ge(sem("h_ready"), 4 * DT + x + 1) if j == 0 else None)

        @block.scalar
        def _(act):
            def squares(n, x, src):
                if n % 2 == 0 and x >= 2:
                    act.wait_ge(sem("sq_used"), DT * n + x - 1)
                nc.scalar.activation(square_tile(n, x), src, ACT.Square).then_inc(sem("sq_ready"), 1)

            def root_mean(n):
                act.wait_ge(sem("sq_used"), DT * (n + 1))
                if n:
                    act.wait_ge(sem("normed"), DT * n)
                nc.scalar.activation(rstd[:, :], bank(7), ACT.Sqrt, bias=const("eps", 0, 1)).then_inc(sem("rms_ready"), 1)

            def pre_norm(n):
                for x in range(DT):
                    if n == 0:
                        act.wait_ge(sem("x_loaded"), 16)
                    else:
                        act.wait_ge(sem("h_ready"), (n // 2 - 1) * DT + x + 1)
                    squares(n, x, tile(h, x))
                root_mean(n)

            def take_out(name, n, dst=wbuf):
                for x in range(DT):
                    act.wait_ge(y_ready, FIRST_TILE[name] + x + 1)
                    squares(n, x, bank((FIRST_TILE[name] + x) % 2))
                    nc.scalar.activation(tile(dst, x), bank((FIRST_TILE[name] + x) % 2), ACT.Copy).then_inc(y_taken, 1)
                root_mean(n)

            def take_tile(name, x, dst, func=ACT.Copy, **kw):
                act.wait_ge(y_ready, FIRST_TILE[name] + x + 1)
                nc.scalar.activation(dst, bank((FIRST_TILE[name] + x) % 2), func, **kw).then_inc(y_taken, 1)

            act.wait_ge(sem("cols_loaded"), 16)
            act.wait_ge(sem("consts_loaded"), 16)
            nc.scalar.activation(derived(DT_, ST), cols[:, COLS["log_dt"]:COLS["log_dt"] + ST], ACT.Exp
                                 ).then_inc(sem("dt_exp"), 1)
            act.wait_ge(sem("s5_angles"), 1)
            nc.scalar.activation(derived(MAG, ST), derived(X_, ST), ACT.Exp).then_inc(sem("s5_exp"), 1)
            nc.scalar.activation(tmp(0), derived(X_, ST), ACT.Tanh, scale=0.5).then_inc(sem("s5_exp"), 1)
            nc.scalar.activation(tmp(1), derived(TH_, ST), ACT.Sin).then_inc(sem("s5_exp"), 1)
            nc.scalar.activation(tmp(2), derived(TH_, ST), ACT.Sin, scale=0.5).then_inc(sem("s5_exp"), 1)
            act.wait_ge(sem("lam_abs"), 1)
            nc.scalar.activation(tmp(10)[:, 0:LT], tmp(9)[:, 0:LT], ACT.Exp, scale=-1.0).then_inc(sem("lam_exp"), 1)
            act.wait_ge(sem("lines_summed"), 2)
            act.dma_start(lines_dram[:, :], line_sb).then_inc(sem("lines_stored"), 16)

            pre_norm(0)
            for x in range(DT):
                take_tile("qk", x, tile(qT, x), scale=float(HEAD) ** -0.5)
            for x in range(5):
                take_tile("qk", DT + x, tile(kT, x))
            for x in range(5):
                take_tile("v", x, vtok.rearrange("p (t n) -> p t n", t=4)[:, :, x * P:(x + 1) * P])
            with act.Fori(0, 4) as i:
                def exponent(n):
                    head = (2 * i + n % 2) if n < 8 else (i + 8 + 4 * (n % 2))
                    act.wait_ge(sem("max_ready"), i * 16 + (n + 1))
                    if n >= 2:
                        act.wait_ge(sem("pt_ready"), i * 16 + (n - 1))
                    r = n % 4
                    nc.scalar.activation(p_sb[n % 2], s_sb[n % 2], ACT.Exp, bias=small[:, 4 + r:5 + r],
                                         accum_out=small[:, 8 + r:9 + r]).then_inc(sem("p_ready"), 1)
                    nc.scalar.activation(small[:, 12 + r:13 + r], col("sink", head), ACT.Exp,
                                         bias=small[:, 4 + r:5 + r]).then_inc(sem("sink_ready"), 1)

                def output(n):
                    act.wait_ge(sem("o_ready"), i * 16 + (n + 1))
                    act.wait_ge(sem("rden_ready"), i * 16 + (n + 1))
                    m, r = n // 2, n % 4
                    if m >= 2:
                        act.wait_ge(sem("ot_ready"), i * 8 + (m - 1))
                    nc.scalar.activation(o_tok[m % 2][:, n % 2 * HEAD:(n % 2 + 1) * HEAD],
                                         bank(6 + n % 2, HEAD), ACT.Copy,
                                         scale=small[:, 16 + r:17 + r]).then_inc(sem("o_taken"), 1)

                def turned(m):
                    act.wait_ge(sem("ot_ready"), i * 8 + (m + 1))
                    at = m % 4 * P + (4 * SEQ if m >= 4 else 0)
                    nc.scalar.activation(attnT[:, bass.ds(i * SEQ + at, P)], bank(m % 2, P)[:, ::-1],
                                         ACT.Copy).then_inc(sem("ot_taken"), 1)

                for n in range(16):
                    exponent(n)
                    if n >= 2:
                        output(n - 2)
                    if n >= 5 and n % 2:
                        turned((n - 5) // 2)
                output(14)
                turned(6)
                output(15)
                turned(7)
            take_out("attn_out", 1)

            def mlp(up, down, first_norm):
                pre_norm(first_norm)
                t0 = FIRST_TILE[up]
                with act.Fori(0, 4) as i:
                    for j in range(8):
                        act.wait_ge(y_ready, i * 8 + (t0 + j + 1))
                        if j >= 2:
                            act.wait_ge(y_taken, i * 8 + (t0 + j - 1))
                        else:
                            act.wait_ge(y_taken, i * 8 + t0)
                        nc.scalar.activation(relu[j % 2], bank((t0 + j) % 2), ACT.Relu).then_inc(sem("relu_ready"), 1)
                take_out(down, first_norm + 1)

            mlp("up0", "down0", 2)
            pre_norm(4)
            act.wait_ge(sem("mu_ready"), 1)
            for m, c in enumerate([1, 4, 5, 0, 2, 3]):
                if m >= 2:
                    name = ["lora_w", "lora_a", "lora_g", "r"][m - 2]
                    act.wait_ge(y_ready, FIRST_TILE[name] + SHAPE[name][0])
                for x in range(DT):
                    if m == 0:
                        act.wait_ge(sem("normed"), 4 * DT + x + 1)
                    at = MU0 + c * DT + x
                    nc.scalar.activation(tile(mixb[m % 2], x), u_tile(x), ACT.Copy, scale=der[:, at:at + 1]
                                         ).then_inc(sem("mix_started"), 1)
                if m == 0:
                    continue
                if m == 1:
                    take_tile("lora_w", 0, lo_w, ACT.Tanh)
                elif m == 2:
                    take_tile("lora_a", 0, lo_a)
                elif m == 3:
                    for x in range(2):
                        take_tile("lora_g", x, lo_g[x], ACT.Sigmoid)
                else:
                    for x in range(DT):
                        take_tile("r" if m == 4 else "k", x, tile(rT if m == 4 else kTr, x))
            for x in range(DT):
                take_tile("rv", x, tile(vTr, x))
            for x in range(DT):
                if x >= 2:
                    act.wait_ge(sem("kk_summed"), x - 1)
                nc.scalar.activation(sq[:, x % 2 * SEQ:(x % 2 + 1) * SEQ], tile(kTr, x), ACT.Square,
                                     scale=col("k_k", x)).then_inc(sem("kk_squared"), 1)
                if x >= 1:
                    act.wait_ge(sem("kk_clamped"), x)
                    nc.scalar.activation(tile(kk, x - 1), tile(kk, x - 1), ACT.Sqrt).then_inc(sem("kk_root"), 1)
            act.wait_ge(sem("kk_clamped"), DT)
            nc.scalar.activation(tile(kk, DT - 1), tile(kk, DT - 1), ACT.Sqrt).then_inc(sem("kk_root"), 1)

            with act.Fori(0, DT) as i:
                act.wait_ge(sem("pair_done"), i + 1)
                for d in range(2):
                    act.wait_ge(sem("z_ready"), i * 6 + (1 + d))
                    nc.scalar.activation(R[d]["al"], bank(d), ACT.Sigmoid, bias=col("w0", i + d * DT)
                                         ).then_inc(sem("z_taken"), 1)
                for d in range(2):
                    act.wait_ge(sem("z_ready"), i * 6 + (3 + d))
                    nc.scalar.activation(R[d]["be"], bank(2 + d), ACT.Sigmoid, bias=col("a0", i + d * DT)
                                         ).then_inc(sem("z_taken"), 1)
                for d in range(2):
                    act.wait_ge(sem("z_ready"), i * 6 + (5 + d))
                    nc.scalar.activation(R[d]["g"], bank(4 + d), ACT.Copy).then_inc(sem("z_taken"), 1)
                for d in range(2):
                    act.wait_ge(sem("decay_summed"), i * 2 + (d + 1))
                    nc.scalar.activation(R[d]["ka"], R[d]["ro"], ACT.Exp, scale=DECAY).then_inc(sem("decays_ready"), 1)
                    act.wait_ge(sem("decays_ready"), i * 6 + (3 * d + 1))
                    nc.scalar.activation(R[d]["ro"], R[d]["ro"], ACT.Exp, scale=-DECAY).then_inc(sem("decays_ready"), 1)
                    nc.scalar.activation(R[d]["al"], R[d]["al"], ACT.Exp, scale=-DECAY).then_inc(sem("decays_ready"), 1)
                copies = [(3, 4, "L", 0), (4, 4, "L", 1), (11, 4, "be", 0), (12, 4, "be", 1),
                          (13, 8, "ka", 0), (14, 8, "ka", 1)]
                for ready, _, name, d in copies:
                    act.wait_ge(sem("scores_ready"), i * 15 + ready)
                    src = bank(4 * d + (2 if name == "ka" else 1))
                    nc.scalar.activation(R[d][name], src, ACT.Copy).then_inc(sem("copied_a"), 1)
                act.wait_ge(sem("scores_ready"), i * 15 + 15)
                nc.scalar.activation(vt, bank(3), ACT.Copy).then_inc(sem("copied_a"), 1)
                for n in range(2 * (LEVELS - 1)):
                    act.wait_ge(sem("x_ready"), i * 10 + (n + 1))
                    nc.scalar.activation(R[n % 2]["X"], bank(4 * (n % 2)), ACT.Copy).then_inc(sem("x_taken"), 1)
                for n in range(2 * NCH):
                    act.wait_ge(sem("w_ready"), i * 16 + (n + 1))
                    nc.scalar.activation(st_w[n % 2], bank(4 * (n % 2), CH), ACT.Copy).then_inc(sem("w_taken"), 1)
                for d in range(2):
                    act.wait_ge(sem("o_ready_rw"), i * 16 + (15 + d))
                    nc.scalar.activation(R[d]["L"], bank(4 * d + 3), ACT.Copy).then_inc(sem("o_copied"), 1)
                for d in range(2):
                    act.wait_ge(sem("o_centered"), i * 2 + (d + 1))
                    nc.scalar.activation(R[d]["Ma"], R[d]["L"], ACT.Square).then_inc(sem("o_squared"), 1)
                for d in range(2):
                    act.wait_ge(sem("var_ready"), i * 2 + (d + 1))
                    nc.scalar.activation(R[d]["Mb"], bank(4 * d + 1), ACT.Sqrt, bias=const("eps", 1, 1)
                                         ).then_inc(sem("deviation"), 1)
            take_out("o", 5, kTr)
            mlp("up1", "down1", 6)
            pre_norm(8)
            tiles = ([("s5x", x) for x in range(XT)] + [("s5g", x) for x in range(XT)]
                     + [("lrux", x) for x in range(LT)] + [("lrug", x) for x in range(LT)]
                     + [("gs", x) for x in range(DT)] + [("gl", x) for x in range(DT)])
            t0 = FIRST_TILE["w_in"]
            gated = []
            for n, (name, x) in enumerate(tiles):
                act.wait_ge(y_ready, t0 + n + 1)
                src = bank((t0 + n) % 2)
                if name in ("s5g", "lrug"):
                    if len(gated) >= 2:
                        act.wait_ge(y_taken, t0 + gated[-2] + 1)
                    nc.scalar.activation(sgt[len(gated) % 2], src, ACT.Sigmoid).then_inc(sem("silu_sigmoid"), 1)
                    gated.append(n)
                    continue
                if n in (2 * XT, 2 * XT + 2 * LT):
                    act.wait_ge(y_taken, t0 + n)
                if name == "s5x":
                    nc.scalar.activation(tile(s5x, x), src, ACT.Copy).then_inc(y_taken, 1)
                elif name == "lrux":
                    nc.scalar.activation(lrux[:, x * LPAD + CONV - 1:(x + 1) * LPAD], src, ACT.Copy).then_inc(y_taken, 1)
                else:
                    nc.scalar.activation(tile(gs if name == "gs" else gl, x), src, ACT.Sigmoid).then_inc(y_taken, 1)
            act.dma_start(s5b, t["s5_b"]).then_inc(sem("s5b_landed"), 16)
            for j in range(ST):
                v = V[j % 2]
                act.wait_ge(sem("s5_phase"), j + 1)
                nc.scalar.activation(v["S"], v["A"], ACT.Sin, scale=TWO_PI).then_inc(sem("s5_sine"), 1)
                nc.scalar.activation(v["C"], v["A"], ACT.Sin, scale=TWO_PI / 2).then_inc(sem("s5_sine"), 1)
            for x in range(XT):
                act.wait_ge(sem("s5_skipped"), x + 1)
                nc.scalar.activation(tile(s5x, x), tile(s5x, x), ACT.Gelu_apprx_tanh).then_inc(sem("gelu_ready"), 1)
            act.wait_ge(sem("gelu_ready"), XT)
            t0 = FIRST_TILE["glu"]
            for x in range(XT):
                act.wait_ge(y_ready, t0 + 2 * x + 1)
                if x >= 2:
                    act.wait_ge(sem("s5_gated"), x - 1)
                nc.scalar.activation(sgt[x % 2], bank((t0 + 2 * x) % 2), ACT.Sigmoid).then_inc(sem("glu_sigmoid"), 1)
            t0 = FIRST_TILE["lru"]
            act.wait_ge(y_taken, t0)
            for x in range(LT):
                act.wait_ge(y_ready, t0 + 2 * x + 1)
                nc.scalar.activation(rate[x], bank((t0 + 2 * x) % 2), ACT.Sigmoid, bias=col("b_a", x)).then_inc(y_taken, 1)
                act.wait_ge(y_ready, t0 + 2 * x + 2)
                if x >= 2:
                    act.wait_ge(sem("lru_in"), x - 1)
                nc.scalar.activation(i_t[x % 2], bank((t0 + 2 * x + 1) % 2), ACT.Sigmoid, bias=col("b_x", x)).then_inc(y_taken, 1)
                act.wait_ge(y_taken, t0 + 2 * x + 1)
                nc.scalar.activation(rate[x], rate[x], ACT.Tanh, scale=der[:, SP4 + x:SP4 + x + 1]).then_inc(sem("tanh_ready"), 1)
            for x in range(LT):
                act.wait_ge(sem("tanh_ready"), x + 1)
                if x >= 2:
                    act.wait_ge(sem("lru_b"), x - 1)
                nc.scalar.activation(root[x % 2], rate[x], ACT.Sqrt, scale=4.0).then_inc(sem("root_ready"), 1)
            act.wait_ge(y_ready, FIRST_TILE["lru"])
            act.dma_start(pT, t["p"]).then_inc(sem("p_loaded"), 16)
            take_out("w_out", 9)
            for x in range(DT):
                take_tile("ple", x, tile(gl, x))
            for x in range(DT):
                act.wait_ge(y_ready, FIRST_TILE["gate"] + x + 1)
                if x >= 2:
                    act.wait_ge(sem("gated"), x - 1)
                nc.scalar.activation(sgt[x % 2], bank((FIRST_TILE["gate"] + x) % 2), ACT.Sigmoid).then_inc(y_taken, 1)
            for x in range(DT):
                act.wait_ge(sem("final"), x + 1)
                act.dma_start(out[:, x * SEQ:(x + 1) * SEQ], tile(gl, x)).then_inc(sem("out_stored"), 16)
            act.wait_ge(sem("out_stored"), 16 * DT)

        @block.vector
        def _(dve):
            V_ = nc.vector
            steps = [0]

            def link(ins):
                steps[0] += 1
                ins.then_inc(sem("param_step"), 1)
                dve.wait_ge(sem("param_step"), steps[0])

            def normalise(n, g, x_of, out_of):
                dve.wait_ge(sem("rms_ready"), n + 1)
                V_.reciprocal(rstd[:, :], rstd[:, :]).then_inc(sem("rstd_ready"), 1)
                dve.wait_ge(sem("rstd_ready"), n + 1)
                for x in range(DT):
                    V_.scalar_tensor_tensor(out=out_of(x), in0=x_of(x), scalar=col(g[0], g[1] + x), in1=rstd[:, :],
                                            op0=ALU.mult, op1=ALU.mult).then_inc(sem("normed"), 1)

            def pre_norm(n, g):
                normalise(n, g, lambda x: tile(h, x), u_tile)

            def post_norm(n, g, buf=wbuf):
                normalise(n, g, lambda x: tile(buf, x), lambda x: tile(buf, x))

            dve.wait_ge(sem("line_const_loaded"), 16)
            dve.wait_ge(sem("lines_ready"), 1)
            for half in range(2):
                at = slice(half * SEQ, (half + 1) * SEQ)
                V_.tensor_tensor(line_sb[:, at], bank(5 + half)[0:16, :], line_const[:, at], ALU.add
                                 ).then_inc(sem("lines_summed"), 1)
            dve.wait_ge(sem("cols_loaded"), 16)

            def cs(name, n):
                return cols[:, COLS[name]:COLS[name] + n]

            dve.wait_ge(sem("dt_exp"), 1)
            TT, TS, STT = V_.tensor_tensor, V_.tensor_scalar, V_.scalar_tensor_tensor
            TT(derived(X_, ST), cs("a_re", ST), derived(DT_, ST), ALU.mult).then_inc(sem("param_x"), 1)
            link(TT(derived(TH_, ST), cs("a_im", ST), derived(DT_, ST), ALU.mult))
            th = derived(TH_, ST)
            link(TS(tmp(3), th, 1.0 / TWO_PI, ROUND, ALU.mult, ALU.add))
            link(TS(tmp(3), tmp(3), -ROUND, None, ALU.add))
            for part in TURN_PARTS:
                link(STT(out=th, in0=tmp(3), scalar=-part, in1=th, op0=ALU.mult, op1=ALU.add))
            dve.wait_ge(sem("param_x"), 1)
            TS(th, th, PI_BELOW, -PI_BELOW, ALU.min, ALU.max).then_inc(sem("s5_angles"), 1)
            dve.wait_ge(sem("s5_angles"), 1)
            link(TS(tmp(4), th, 1.0 / TWO_PI, None, ALU.mult))
            link(TS(tmp(5), tmp(4), ROUND12, None, ALU.add))
            link(TS(derived(PHH, ST), tmp(5), -ROUND12, None, ALU.add))
            link(TT(derived(PHL, ST), tmp(4), derived(PHH, ST), ALU.subtract))
            dve.wait_ge(sem("s5_exp"), 4)
            t_, sin_, sh_ = tmp(0), tmp(1), tmp(2)
            link(TS(tmp(3), t_, -1.0, 1.0, ALU.mult, ALU.add))
            link(V_.reciprocal(tmp(3), tmp(3)))
            link(STT(out=t_, in0=t_, scalar=2.0, in1=tmp(3), op0=ALU.mult, op1=ALU.mult))
            link(TT(sh_, sh_, sh_, ALU.mult))
            link(TS(tmp(3), sh_, -2.0, 1.0, ALU.mult, ALU.add))
            link(TT(tmp(3), tmp(3), t_, ALU.mult))
            link(STT(out=tmp(3), in0=sh_, scalar=-2.0, in1=tmp(3), op0=ALU.mult, op1=ALU.add))
            link(TT(tmp(4), derived(MAG, ST), sin_, ALU.mult))
            re, im = cs("a_re", ST), cs("a_im", ST)
            link(TT(tmp(5), re, re, ALU.mult))
            link(TT(tmp(6), im, im, ALU.mult))
            link(TT(tmp(5), tmp(5), tmp(6), ALU.add))
            link(V_.reciprocal(tmp(5), tmp(5)))
            link(TT(tmp(6), tmp(3), re, ALU.mult))
            link(TT(tmp(7), tmp(4), im, ALU.mult))
            link(TT(tmp(6), tmp(6), tmp(7), ALU.add))
            link(TT(derived(ZRE, ST), tmp(6), tmp(5), ALU.mult))
            link(TT(tmp(6), tmp(4), re, ALU.mult))
            link(TT(tmp(7), tmp(3), im, ALU.mult))
            link(TT(tmp(6), tmp(6), tmp(7), ALU.subtract))
            link(TT(derived(ZIM, ST), tmp(6), tmp(5), ALU.mult))
            dve.wait_ge(sem("s5_c_loaded"), 16)
            cin = s5_in.rearrange("p (j r n) -> p j r n", j=ST, r=2)
            cout = s5c[:, :].rearrange("p (j r n) -> p j r n", j=ST, r=2)
            ca, cb = [a.rearrange("p (j n) -> p j n", j=ST) for a in s5_t]
            zre = derived(ZRE, ST).unsqueeze(2).to_broadcast([P, ST, 32])
            zim = derived(ZIM, ST).unsqueeze(2).to_broadcast([P, ST, 32])
            link(TT(ca, cin[:, :, 0, :], zre, ALU.mult))
            link(TT(cb, cin[:, :, 1, :], zim, ALU.mult))
            link(TT(cout[:, :, 0, :], ca, cb, ALU.subtract))
            link(TT(ca, cin[:, :, 0, :], zim, ALU.mult))
            link(TT(cb, cin[:, :, 1, :], zre, ALU.mult))
            link(TT(ca, ca, cb, ALU.add))
            link(TS(cout[:, :, 1, :], ca, -1.0, None, ALU.mult))
            lam, y, z, z2, acc = cs("lam", LT), tmp(10)[:, 0:LT], tmp(11)[:, 0:LT], tmp(12)[:, 0:LT], tmp(13)[:, 0:LT]
            STT(out=tmp(9)[:, 0:LT], in0=lam, scalar=-1.0, in1=lam, op0=ALU.mult, op1=ALU.max).then_inc(sem("lam_abs"), 1)
            dve.wait_ge(sem("lam_exp"), 1)
            link(TS(z, y, 2.0, None, ALU.add))
            link(V_.reciprocal(z, z))
            link(TT(z, z, y, ALU.mult))
            link(TT(z2, z, z, ALU.mult))
            link(TS(acc, z2, 1.0 / 17, 1.0 / 15, ALU.mult, ALU.add))
            for n in (13, 11, 9, 7, 5, 3, 1):
                link(TT(acc, acc, z2, ALU.mult))
                link(TS(acc, acc, 1.0 / n, None, ALU.add))
            link(TT(acc, acc, z, ALU.mult))
            link(TS(z2, lam, -1.0, 0.0, ALU.mult, ALU.max))
            link(STT(out=z2, in0=acc, scalar=2.0, in1=z2, op0=ALU.mult, op1=ALU.add))
            link(TS(der[:, SP4:SP4 + LT], z2, 4.0, None, ALU.mult))
            mu0 = der[:, MU0:MU0 + 6 * DT]
            link(TT(mu0, cs("mu_prev", 6 * DT), cs("mu_next", 6 * DT), ALU.add))
            TS(mu0, mu0, -1.0, 1.0, ALU.mult, ALU.add).then_inc(sem("mu_ready"), 1)
            link(TS(der[:, OMKA:OMKA + DT], cs("k_a", DT), -1.0, 1.0, ALU.mult, ALU.add))
            V_.tensor_copy(small[:, 40:41], der[:, OMKA:OMKA + 1]).then_inc(sem("s5c_ready"), 1)

            pre_norm(0, ("norm_g", 0))
            with dve.Fori(0, 4) as i:
                def biased(n):
                    half, qi, e = n // 8, n % 8 // 2, n % 2
                    head = (2 * i + e) if n < 8 else (i + 8 + 4 * e)
                    r = n % 4
                    dve.wait_ge(sem("s_ready"), i * 16 + (n + 1))
                    if n % 8 < 2:
                        dve.wait_ge(sem(f"bias_landed_{2 * half + e}"), i * 16 + 16)
                    if n >= 2:
                        dve.wait_ge(sem("p_ready"), i * 16 + (n - 1))
                    dve.nop(nofuse=True)
                    V_.tensor_tensor_reduce(s_sb[n % 2], bank(2 + n % 2), bias[2 * half + e][:, (3 - qi) * P:(3 - qi) * P + SEQ],
                                            1.0, -3.0e38, ALU.add, ALU.max, small[:, r:r + 1]).then_inc(sem("s_biased"), 1)
                    dve.wait_ge(sem("s_biased"), i * 16 + (n + 1))
                    TS(small[:, 4 + r:5 + r], small[:, r:r + 1], col("sink", head), -1.0, ALU.max, ALU.mult
                       ).then_inc(sem("max_ready"), 1)

                def denominator(n):
                    r = n % 4
                    dve.wait_ge(sem("sink_ready"), i * 16 + (n + 1))
                    TT(small[:, 20 + r:21 + r], small[:, 8 + r:9 + r], small[:, 12 + r:13 + r], ALU.add
                       ).then_inc(sem("den_ready"), 1)
                    dve.wait_ge(sem("den_ready"), i * 16 + (n + 1))
                    V_.reciprocal(small[:, 16 + r:17 + r], small[:, 20 + r:21 + r]).then_inc(sem("rden_ready"), 1)

                def turned(n):
                    dve.wait_ge(sem("pt_ready"), i * 16 + (n + 1))
                    if n >= 2:
                        dve.wait_ge(sem("o_ready"), i * 16 + (n - 1))
                    V_.tensor_copy(pt_sb[n % 2], bank(4 + n % 2)).then_inc(sem("pt_taken"), 1)

                for n in range(16):
                    biased(n)
                    if n >= 1:
                        denominator(n - 1)
                        turned(n - 1)
                denominator(15)
                turned(15)
            post_norm(1, ("norm_g", DT))
            def mlp(up, first_norm, g):
                pre_norm(first_norm, ("norm_g", g * DT))
                t0 = FIRST_TILE[up]
                with dve.Fori(0, 4) as i:
                    for j in range(8):
                        dve.wait_ge(sem("relu_ready"), i * 8 + ((0 if up == "up0" else FT) + j + 1))
                        TT(mid[:, bass.ds(i * (8 * SEQ) + j * SEQ, SEQ)], bank((t0 + j) % 2), relu[j % 2], ALU.mult
                           ).then_inc(y_taken, 1)
                post_norm(first_norm + 1, ("norm_g", (g + 1) * DT))

            mlp("up0", 2, 2)
            pre_norm(4, ("norm_g", 4 * DT))
            dve.wait_ge(sem("normed"), 5 * DT)
            dve.wait_ge(sem("pads_zeroed"), 2)
            for m, c in enumerate([1, 4, 5, 0, 2, 3]):
                for x in range(DT):
                    dve.wait_ge(sem("mix_started"), m * DT + x + 1)
                    STT(out=tile(mixb[m % 2], x), in0=u_tile(x, -1), scalar=col("mu_prev", c * DT + x),
                        in1=tile(mixb[m % 2], x), op0=ALU.mult, op1=ALU.add).then_inc(sem("mix_half"), 1)
                for x in range(DT):
                    dve.wait_ge(sem("mix_half"), m * DT + x + 1)
                    STT(out=tile(mixb[m % 2], x), in0=u_tile(x, 1), scalar=col("mu_next", c * DT + x),
                        in1=tile(mixb[m % 2], x), op0=ALU.mult, op1=ALU.add).then_inc(sem("mixed"), 1)
            for x in range(DT):
                dve.wait_ge(sem("kk_summed"), x + 1)
                TS(tile(kk, x), bank(6 + x % 2), 1e-24, None, ALU.max).then_inc(sem("kk_clamped"), 1)
            for x in range(DT):
                dve.wait_ge(sem("kk_root"), x + 1)
                V_.reciprocal(tile(kk, x), tile(kk, x)).then_inc(sem("kk_inverse"), 1)
            for x in range(DT):
                dve.wait_ge(sem("kk_inverse"), x + 1)
                STT(out=tile(kk, x), in0=tile(kTr, x), scalar=col("k_k", x), in1=tile(kk, x),
                    op0=ALU.mult, op1=ALU.mult).then_inc(sem("kk_ready"), 1)

            dve.wait_ge(sem("kk_ready"), DT)
            with dve.Fori(0, DT) as i:
                def ends(a, d):
                    return chunks(a)[:, :, CH - 1] if d == 0 else chunks(a)[:, :, 0]

                for d in range(2):
                    r = R[d]
                    dve.wait_ge(sem("z_taken"), i * 6 + (1 + d))
                    src, dst = (r["al"], r["ro"]) if d == 0 else (r["al"][:, ::-1], r["ro"][:, ::-1])
                    V_.tensor_tensor_scan(dst, const("carry", 0, SEQ), src, 0.0, ALU.mult, ALU.add
                                          ).then_inc(sem("decay_scanned"), 1)
                for d in range(2):
                    r = R[d]
                    dve.wait_ge(sem("decay_scanned"), i * 2 + (d + 1))
                    TT(r["al"], r["ro"], r["al"], ALU.subtract).then_inc(sem("decay_summed"), 1)
                for d in range(2):
                    r = R[d]
                    dve.wait_ge(sem("z_taken"), i * 6 + (3 + d))
                    TS(r["kd"], r["be"], col("k_a", i), der[:, bass.ds(i + OMKA, 1)], ALU.mult, ALU.add
                       ).then_inc(sem("kd_factor"), 1)
                for d in range(2):
                    r = R[d]
                    dve.wait_ge(sem("decays_ready"), i * 6 + 3 * (d + 1))
                    V_.tensor_copy(p_end[d], ends(r["ro"], d)).then_inc(sem("p_end_ready"), 1)
                    STT(out=r["al"], in0=r["al"], scalar=-1.0, in1=tile(kk, i), op0=ALU.mult, op1=ALU.mult
                        ).then_inc(sem("al_ready"), 1)
                    dve.wait_ge(sem("p_end_ready"), i * 2 + (d + 1))
                    TT(r["ro"], r["ro"], tile(rT, i), ALU.mult).then_inc(sem("features_v"), 1)
                for d in range(2):
                    r = R[d]
                    dve.wait_ge(sem("features_p"), i * 2 + (d + 1))
                    STT(out=r["kd"], in0=r["kd"], scalar=col("r_k", i), in1=tile(rT, i), op0=ALU.mult, op1=ALU.mult
                        ).then_inc(sem("bonus_terms"), 1)
                masked = [(1, "T", 0, 0, "level_n"), (2, "T", 0, 1, "level_n"), (5, "Ma", 2, 0, "strict"),
                          (6, "Ma", 2, 1, "strict"), (7, "Mr", 3, 0, "incl"), (8, "Mr", 3, 1, "incl"),
                          (9, "Mb", 0, 0, "incl"), (10, "Mb", 0, 1, "incl")]
                for ready, name, b, d, kind in masked:
                    dve.wait_ge(sem("scores_ready"), i * 15 + ready)
                    TT(chunks(R[d][name]), chunks(bank(4 * d + b)), mask(kind, d), ALU.mult).then_inc(sem("masked_v"), 1)
                for l in range(1, LEVELS):
                    for d in range(2):
                        n = 2 * (l - 1) + d
                        dve.wait_ge(sem("dt_ready"), i * 10 + (n + 1))
                        last = TT(R[d]["T"], R[d]["T"], bank(4 * d + 1), ALU.add)
                        if l < LEVELS - 1:
                            last = TT(R[d]["TT"], R[d]["TT"], bank(4 * d + 2), ALU.add)
                        last.then_inc(sem("t_updated"), 1)
                for j in range(NCH):
                    for d in range(2):
                        n = 2 * j + d
                        dve.wait_ge(sem("u_ready"), i * 16 + (n + 1))
                        V_.tensor_copy(st_u[d], bank(4 * d + 1, CH)).then_inc(sem("u_taken"), 1)
                    if j == NCH - 1:
                        break
                    for d in range(2):
                        n = 2 * j + d
                        c = j if d == 0 else NCH - 1 - j
                        nxt = c + 1 if d == 0 else c - 1
                        new = st_s[d][(j + 1) % 2]
                        dve.wait_ge(sem("s_ready_rw"), i * 14 + (n + 1))
                        if j == 0:
                            TS(new, bank(4 * d + 2, CH), p_end[d][:, c:c + 1], None, ALU.mult).then_inc(sem("state_ready"), 1)
                        else:
                            dve.wait_ge(sem("state_decayed"), i * 12 + (n - 1))
                            STT(out=new, in0=bank(4 * d + 2, CH), scalar=p_end[d][:, c:c + 1], in1=st_p[d],
                                op0=ALU.mult, op1=ALU.add).then_inc(sem("state_ready"), 1)
                    if j < NCH - 2:
                        for d in range(2):
                            n = 2 * j + d
                            c = j if d == 0 else NCH - 1 - j
                            nxt = c + 1 if d == 0 else c - 1
                            dve.wait_ge(sem("state_ready"), i * 14 + (n + 1))
                            TS(st_p[d], st_s[d][(j + 1) % 2], p_end[d][:, nxt:nxt + 1], None, ALU.mult
                               ).then_inc(sem("state_decayed"), 1)
                for d in range(2):
                    dve.wait_ge(sem("mean_ready"), i * 2 + (d + 1))
                    TT(R[d]["L"], R[d]["L"], bank(4 * d), ALU.subtract).then_inc(sem("o_centered"), 1)
                for d in range(2):
                    dve.wait_ge(sem("bonus_ready"), i * 2 + (d + 1))
                    TT(R[d]["Mr"], tile(vTr, i), bank(4 * d + 2), ALU.mult).then_inc(sem("bonus_done"), 1)
                for d in range(2):
                    dve.wait_ge(sem("deviation"), i * 2 + (d + 1))
                    V_.reciprocal(R[d]["Mb"], R[d]["Mb"]).then_inc(sem("deviation_inverse"), 1)
                for d in range(2):
                    dve.wait_ge(sem("deviation_inverse"), i * 2 + (d + 1))
                    TT(R[d]["L"], R[d]["L"], R[d]["Mb"], ALU.mult).then_inc(sem("o_scaled"), 1)
                for d in range(2):
                    dve.wait_ge(sem("o_scaled"), i * 2 + (d + 1))
                    TS(R[d]["L"], R[d]["L"], col("gn_w", i), col("gn_b", i), ALU.mult, ALU.add).then_inc(sem("o_normed"), 1)
            post_norm(5, ("norm_g", 5 * DT), kTr)
            mlp("up1", 6, 6)
            pre_norm(8, ("g_pre", 0))
            t0 = FIRST_TILE["w_in"]
            gates = 0
            for n in list(range(XT, 2 * XT)) + list(range(2 * XT + LT, 2 * XT + 2 * LT)):
                dst = tile(s5g, n - XT) if n < 2 * XT else tile(lrug, n - 2 * XT - LT)
                dve.wait_ge(sem("silu_sigmoid"), gates + 1)
                if n in (XT, 2 * XT + LT):
                    dve.wait_ge(y_taken, t0 + n)
                TT(dst, bank((t0 + n) % 2), sgt[gates % 2], ALU.mult).then_inc(y_taken, 1)
                gates += 1

            def phase(j):
                v = V[j % 2]
                a, b = v["A"], v["B"]
                if j >= 2:
                    dve.wait_ge(sem("s5_turned"), 2 * (j - 1))
                else:
                    dve.wait_ge(y_taken, FIRST_TILE["glu"])
                iota = const("iota", 0, SEQ)
                link(TS(a, iota, der[:, PHH + j:PHH + j + 1], None, ALU.mult))
                link(TS(b, a, ROUND, -ROUND, ALU.add, ALU.add))
                link(TT(a, a, b, ALU.subtract))
                link(STT(out=a, in0=iota, scalar=der[:, PHL + j:PHL + j + 1], in1=a, op0=ALU.mult, op1=ALU.add))
                link(TS(b, a, ROUND, -ROUND, ALU.add, ALU.add))
                TT(a, a, b, ALU.subtract).then_inc(sem("s5_phase"), 1)

            phase(0)
            for j in range(ST):
                v = V[j % 2]
                if j + 1 < ST:
                    phase(j + 1) if False else None
                dve.wait_ge(sem("s5_sine"), 2 * (j + 1))
                link(TT(v["C"], v["C"], v["C"], ALU.mult))
                link(TS(v["C"], v["C"], -2.0, 1.0, ALU.mult, ALU.add))
                dve.wait_ge(sem("s5_in"), 2 * (j + 1))
                br, bi = bank(2 + 2 * (j % 2)), bank(3 + 2 * (j % 2))
                TT(v["v1"], br, v["C"], ALU.mult).then_inc(sem("s5_in_taken"), 1)
                TT(v["v2"], bi, v["S"], ALU.mult).then_inc(sem("s5_in_taken"), 1)
                TT(v["v3"], bi, v["C"], ALU.mult).then_inc(sem("s5_in_taken"), 1)
                TT(v["v4"], br, v["S"], ALU.mult).then_inc(sem("s5_in_taken"), 1)
                mag = der[:, MAG + j:MAG + j + 1].to_broadcast([P, SEQ])
                dve.wait_ge(sem("s5_back"), 2 * j + 1)
                V_.tensor_tensor_scan(v["A"], mag, v["v1"], 0.0, ALU.mult, ALU.add).then_inc(sem("s5_scanned"), 1)
                dve.wait_ge(sem("s5_back"), 2 * j + 2)
                V_.tensor_tensor_scan(v["B"], mag, v["v3"], 0.0, ALU.mult, ALU.add).then_inc(sem("s5_scanned"), 1)
                if j + 1 < ST:
                    phase(j + 1)
                if j % 4 == 3:
                    m = j // 4
                    dve.wait_ge(sem("s5_out"), j + 1)
                    STT(out=tile(s5x, m), in0=tile(s5x, m), scalar=col("s5_d", m), in1=bank(6 + m % 2),
                        op0=ALU.mult, op1=ALU.add).then_inc(sem("s5_skipped"), 1)
            t0 = FIRST_TILE["glu"]
            for x in range(XT):
                dve.wait_ge(y_ready, t0 + 2 * x + 2)
                dve.wait_ge(sem("glu_sigmoid"), x + 1)
                TT(sgt[x % 2], bank((t0 + 2 * x + 1) % 2), sgt[x % 2], ALU.mult).then_inc(y_taken, 2)
                dve.wait_ge(y_taken, t0 + 2 * x + 2)
                TT(tile(s5g, x), tile(s5g, x), sgt[x % 2], ALU.mult).then_inc(sem("s5_gated"), 1)
            t0 = FIRST_TILE["w_bs"]
            for x in range(DT):
                dve.wait_ge(y_ready, t0 + x + 1)
                TT(tile(gs, x), tile(gs, x), bank((t0 + x) % 2), ALU.mult).then_inc(y_taken, 1)
            dve.wait_ge(sem("conv_zeroed"), 1)
            dve.wait_ge(y_ready, FIRST_TILE["w_bs"])
            for x in range(LT):
                def tap(n):
                    return lrux[:, x * LPAD + n:x * LPAD + n + SEQ]
                link(TS(conv[x], tap(0), col("conv_w", x), col("conv_b", x), ALU.mult, ALU.add))
                for n in range(1, CONV):
                    ins = STT(out=conv[x], in0=tap(n), scalar=col("conv_w", n * LT + x), in1=conv[x], op0=ALU.mult, op1=ALU.add)
                    if n < CONV - 1:
                        link(ins)
                    else:
                        ins.then_inc(sem("conv_ready"), 1)
            for x in range(LT):
                dve.wait_ge(sem("tanh_ready"), x + 1)
                a, b = fa[x % 2], fb[x % 2]
                link(TS(b, rate[x], 1.0, None, ALU.add))
                link(V_.reciprocal(b, b))
                link(TS(a, rate[x], -1.0, 1.0, ALU.mult, ALU.add))
                link(TT(a, a, b, ALU.mult))
                dve.wait_ge(sem("root_ready"), x + 1)
                link(TT(b, b, root[x % 2], ALU.mult))
                dve.wait_ge(sem("lru_in"), x + 1)
                TT(b, b, conv[x], ALU.mult).then_inc(sem("lru_b"), 1)
                dve.wait_ge(sem("lru_b"), x + 1)
                link(V_.tensor_tensor_scan(rate[x], a, b, 0.0, ALU.mult, ALU.add))
                TT(tile(lrug, x), tile(lrug, x), rate[x], ALU.mult).then_inc(sem("lru_gated"), 1)
            t0 = FIRST_TILE["w_bl"]
            for x in range(DT):
                dve.wait_ge(y_ready, t0 + x + 1)
                TT(tile(gl, x), tile(gl, x), bank((t0 + x) % 2), ALU.mult).then_inc(y_taken, 1)
            post_norm(9, ("g_post", 0))
            t0 = FIRST_TILE["gate"]
            for x in range(DT):
                dve.wait_ge(y_taken, t0 + x + 1)
                TT(tile(gl, x), tile(gl, x), sgt[x % 2], ALU.mult).then_inc(sem("gated"), 1)

        @block.gpsimd
        def _(pool):
            G = nc.gpsimd
            up = u[:, :].rearrange("p (t n) -> p t n", t=DT)
            G.memset(up[:, :, 0:1], 0.0).then_inc(sem("pads_zeroed"), 1)
            G.memset(up[:, :, PAD - 1:PAD], 0.0).then_inc(sem("pads_zeroed"), 1)
            G.memset(small[:, 48:49], 0.0).then_inc(sem("ot_taken"), 1)
            G.memset(small[:, 49:50], 0.0).then_inc(sem("pair_done"), 1)

            def add_out(n, buf=wbuf):
                for x in range(DT):
                    pool.wait_ge(sem("normed"), n * DT + x + 1)
                    G.tensor_tensor(tile(h, x), tile(h, x), tile(buf, x), ALU.add).then_inc(sem("h_ready"), 1)

            with pool.Fori(0, 4) as i:
                pool.wait_ge(y_taken, FIRST_TILE["attn_out"])
                pool.wait_ge(sem("ot_taken"), i * 8 + 1)
                G.tensor_copy(k_st, kT[:, bass.ts(i, SEQ)]).then_inc(sem("k_staged"), 1)
                for half in range(2):
                    by_block = qT[:, bass.ds(i * SEQ + half * 4 * SEQ, SEQ)].rearrange("p (b s) -> p b s", s=P)
                    G.tensor_copy(q_st[half].rearrange("p (b s) -> p b s", s=P)[:, :, ::-1], by_block).then_inc(sem("q_staged"), 1)
            add_out(1)
            add_out(3)
            pool.wait_ge(y_taken, FIRST_TILE["o"])
            pool.wait_ge(sem("kk_ready"), DT)
            with pool.Fori(0, DT) as i:
                pool.wait_ge(sem("pair_done"), i + 1)
                G.tensor_copy(v_st, tile(vTr, i)).then_inc(sem("v_staged"), 1)
                for d in range(2):
                    r = R[d]
                    pool.wait_ge(sem("kd_factor"), i * 2 + (d + 1))
                    pool.nop(nofuse=True)
                    G.tensor_tensor(r["kd"], r["kd"], tile(kTr, i), ALU.mult).then_inc(sem("kd_ready"), 1)
                    G.tensor_tensor(r["be"], r["be"], tile(kk, i), ALU.mult).then_inc(sem("rate_kk"), 1)
                for d in range(2):
                    r = R[d]
                    pool.wait_ge(sem("decays_ready"), i * 6 + (3 * d + 1))
                    pool.wait_ge(sem("rate_kk"), i * 2 + (d + 1))
                    G.tensor_tensor(r["be"], r["be"], r["ka"], ALU.mult).then_inc(sem("be_ready"), 1)
                    pool.wait_ge(sem("be_ready"), i * 2 + (d + 1))
                    pool.wait_ge(sem("kd_ready"), i * 2 + (d + 1))
                    G.tensor_tensor(r["ka"], r["ka"], r["kd"], ALU.mult).then_inc(sem("features_p"), 1)
                eye = const("eye", 0, CH).unsqueeze(1).to_broadcast([P, NCH, CH])
                for d in range(2):
                    r = R[d]
                    pool.wait_ge(sem("masked_v"), i * 8 + (1 + d))
                    G.tensor_tensor(chunks(r["T"]), chunks(r["T"]), eye, ALU.add).then_inc(sem("t_started"), 1)
                for d in range(2):
                    r = R[d]
                    pool.wait_ge(sem("copied_a"), i * 7 + (1 + d))
                    G.tensor_tensor(chunks(r["TT"]), chunks(r["L"]), mask("level", d * LEVELS), ALU.mult
                                    ).then_inc(sem("tt_masked"), 1)
                    pool.wait_ge(sem("tt_masked"), i * 2 + (1 + d))
                    G.tensor_tensor(chunks(r["TT"]), chunks(r["TT"]), eye, ALU.add).then_inc(sem("t_started"), 1)
                for l in range(1, LEVELS):
                    for d in range(2):
                        n = 2 * (l - 1) + d
                        if l > 1:
                            pool.wait_ge(sem("x_ready"), i * 10 + (n - 1))
                        G.tensor_tensor(chunks(R[d]["LM"]), chunks(R[d]["L"]), mask("level", d * LEVELS + l), ALU.mult
                                        ).then_inc(sem("level_masked"), 1)
                for d in range(2):
                    r = R[d]
                    pool.wait_ge(sem("o_normed"), i * 2 + (d + 1))
                    G.tensor_tensor(r["L"], r["L"], r["Mr"], ALU.add).then_inc(sem("with_bonus"), 1)
                for d in range(2):
                    r = R[d]
                    pool.wait_ge(sem("with_bonus"), i * 2 + (d + 1))
                    G.tensor_tensor(r["L"], r["L"], r["g"], ALU.mult).then_inc(sem("dir_gated"), 1)
                pool.wait_ge(sem("dir_gated"), i * 2 + 2)
                pool.nop(nofuse=True)
                G.tensor_tensor(tile(rT, i), R[0]["L"], R[1]["L"], ALU.add).then_inc(sem("pair_done"), 1)
            add_out(5, kTr)
            add_out(7)
            pool.wait_ge(sem("rms_ready"), 9)
            pool.wait_ge(y_ready, FIRST_TILE["w_in"])
            G.memset(lrux.rearrange("p (t n) -> p t n", t=LT)[:, :, 0:CONV - 1], 0.0).then_inc(sem("conv_zeroed"), 1)
            for j in range(ST):
                v = V[j % 2]
                pool.wait_ge(sem("s5_in_taken"), 4 * j + 2)
                G.tensor_tensor(v["v1"], v["v1"], v["v2"], ALU.add).then_inc(sem("s5_back"), 1)
                pool.wait_ge(sem("s5_in_taken"), 4 * j + 4)
                G.tensor_tensor(v["v3"], v["v3"], v["v4"], ALU.subtract).then_inc(sem("s5_back"), 1)
                pool.wait_ge(sem("s5_scanned"), 2 * (j + 1))
                G.tensor_tensor(v["v1"], v["A"], v["C"], ALU.mult).then_inc(sem("s5_part"), 1)
                G.tensor_tensor(v["v2"], v["B"], v["S"], ALU.mult).then_inc(sem("s5_part"), 1)
                G.tensor_tensor(v["v3"], v["B"], v["C"], ALU.mult).then_inc(sem("s5_part"), 1)
                G.tensor_tensor(v["v4"], v["A"], v["S"], ALU.mult).then_inc(sem("s5_part"), 1)
                pool.wait_ge(sem("s5_part"), 4 * j + 2)
                G.tensor_tensor(v["v1"], v["v1"], v["v2"], ALU.subtract).then_inc(sem("s5_turned"), 1)
                pool.wait_ge(sem("s5_part"), 4 * j + 4)
                G.tensor_tensor(v["v3"], v["v3"], v["v4"], ALU.add).then_inc(sem("s5_turned"), 1)
            for x in range(LT):
                pool.wait_ge(y_taken, FIRST_TILE["lru"] + 2 * x + 2)
                G.tensor_tensor(conv[x], conv[x], i_t[x % 2], ALU.mult).then_inc(sem("lru_in"), 1)
            for x in range(DT):
                pool.wait_ge(y_taken, FIRST_TILE["w_bl"] + x + 1)
                G.tensor_tensor(tile(gs, x), tile(gs, x), tile(gl, x), ALU.add).then_inc(sem("merged"), 1)
            add_out(9)
            for x in range(DT):
                pool.wait_ge(sem("gated"), x + 1)
                G.tensor_tensor(tile(gl, x), tile(gl, x), tile(h, x), ALU.add).then_inc(sem("final"), 1)


def units(w):
    k, n = w.shape
    return w.reshape(k // P, P, n // P, P).transpose(2, 0, 1, 3)


def columns(a):
    return np.ascontiguousarray(a.reshape(-1, P).T)


def tiles(a):
    return np.ascontiguousarray(a.reshape(-1, P, a.shape[1]).transpose(1, 0, 2).reshape(P, -1))


def lay_out(**inputs):
    a = {n: np.asarray(v) for n, v in inputs.items()}
    zeros = np.zeros
    wi, wo = a["attn_w_in"][0], a["attn_w_out"][0]
    na = 8 * HEAD
    order = np.concatenate([np.arange(HEAD) + HEAD * hd for pair in range(4) for hd in (pair, pair + 4)])
    qk = np.concatenate([wi[:, 0:na], wi[:, 3 * na:4 * na][:, order], wi[:, na:2 * na], wi[:, 4 * na:4 * na + P]], axis=1)
    v = np.concatenate([wi[:, 2 * na:3 * na], wi[:, 4 * na + P:]], axis=1)
    wo = np.concatenate([wo[0:na], wo[na:][order]])
    both = lambda w: np.concatenate([w[0, 0], w[0, 1]], axis=1)
    glu = a["w_glu_2"][0]
    glu = np.concatenate([glu[:, o + x * P:o + (x + 1) * P] for x in range(XT) for o in (S5W, 0)], axis=1)
    lru = np.stack([w[0, n] for n in range(LT) for w in (a["lru_w_a_2"], a["lru_w_x_2"])])[:, None]
    w_in = units(a["w_in_2"][0])
    parts = {"qk": units(qk), "v": units(v), "attn_out": units(wo), "up0": units(a["mlp_w1"][0]), "down0": units(a["mlp_w2"][0]),
             "lora_w": units(both(a["rk_w1"])), "lora_a": units(both(a["rk_a1"])), "lora_g": units(both(a["rk_g1"])),
             "r": units(a["rk_w_r"][0]), "k": units(a["rk_w_k"][0]), "rv": units(a["rk_w_v"][0]), "o": units(a["rk_w_o"][0]),
             "up1": units(a["mlp_w1"][1]), "down1": units(a["mlp_w2"][1]),
             "w_in": w_in[0:40], "w_in_end": w_in[40:], "glu": units(glu), "w_bs": units(a["w_bs_2"][0]), "lru": lru,
             "w_bl": units(a["w_bl_2"][0]), "w_out": units(a["w_out_2"][0]), "ple": units(a["w_ple_2"][0]),
             "gate": units(a["w_ple_gate_2"][0])}
    wall = zeros((NBLOCKS, P, UPB, P), np.float32)
    for name, n, k in DENSE:
        w = parts[name].reshape(n * k, P, P)
        for x in range(0, n * k, UPB):
            some = w[x:x + UPB]
            wall[FIRST_BLOCK[name] + x // UPB][:, 0:len(some)] = some.transpose(1, 0, 2)
    lora2 = zeros((DT, P, 6, P), np.float32)
    for d in range(2):
        half = slice(64 * d, 64 * d + 64)
        lora2[:, half, d] = a["rk_w2"][0, d].reshape(64, DT, P).transpose(1, 0, 2)
        lora2[:, half, 2 + d] = a["rk_a2"][0, d].reshape(64, DT, P).transpose(1, 0, 2)
        lora2[:, :, 4 + d] = a["rk_g2"][0, d].reshape(P, DT, P).transpose(1, 0, 2)
    sink = np.full(16, NEG, np.float32)
    sink[8:] = a["attn_sink"][0]
    fields = {"norm_g": a["norm_g"], "mu_prev": a["rk_mu_prev"], "mu_next": a["rk_mu_next"], "k_k": a["rk_k_k"],
              "k_a": a["rk_k_a"], "r_k": a["rk_r_k"], "gn_w": a["rk_gn_w"], "gn_b": a["rk_gn_b"], "w0": a["rk_w0"],
              "a0": a["rk_a0"], "g_pre": a["g_pre_2"], "g_post": a["g_post_2"], "a_re": a["s5_a_re_2"],
              "a_im": a["s5_a_im_2"], "log_dt": np.repeat(a["s5_log_dt_2"][0], S5N), "s5_d": a["s5_d_2"],
              "conv_w": a["conv_w_2"], "conv_b": a["conv_b_2"], "b_a": a["lru_b_a_2"], "b_x": a["lru_b_x_2"],
              "lam": a["lru_lambda_2"]}
    cols = np.zeros((P, NCOLS), np.float32)
    for name, value in fields.items():
        c = columns(value)
        cols[:, COLS[name]:COLS[name] + c.shape[1]] = c
    cols[:, COLS["sink"]:COLS["sink"] + 16] = sink
    s5_b = zeros((P, ST, 2, P), np.float32)
    s5_c = zeros((P, ST, 2, 32), np.float32)
    for g in range(S5G):
        j, n, rows = g // 2, S5N * (g % 2), g * 16 % P
        for x, (b, c) in enumerate([("s5_b_re_2", "s5_c_re_2"), ("s5_b_im_2", "s5_c_im_2")]):
            s5_b[rows:rows + 16, j, x, n:n + S5N] = a[b][0, g].T
            s5_c[n:n + S5N, j, x, 16 * (g % 2):16 * (g % 2) + 16] = a[c][0, g].T
    onehot, lines = bias_constants()
    return {"x": tiles(a["x"][0].T), "wall": wall.reshape(NBLOCKS, P, BLOCK), "lora2": lora2.reshape(DT, P, 6 * P),
            "cols": cols, "consts": constants(), "rel_table": a["rel_table"], "onehot": onehot, "lines": lines,
            "s5_b": s5_b.reshape(P, -1), "s5_c": s5_c.reshape(P, -1), "p": tiles(a["p_2"][0, 0].T)}


def kernel(**inputs):
    import concourse.bacc as bacc
    from concourse.bass_utils import run_bass_kernel_spmd

    nc = bacc.Bacc("TRN2", target_bir_lowering=False, num_devices=1)
    arrays = {f"in_{n}": v for n, v in lay_out(**inputs).items()}
    t = {n[3:]: nc.dram_tensor(n, v.shape, F32, kind="ExternalInput").ap() for n, v in arrays.items()}
    out = nc.dram_tensor("out", (P, DT * SEQ), F32, kind="ExternalOutput").ap()
    program(nc, t, out)
    got = run_bass_kernel_spmd(nc, [arrays], core_ids=[0]).results[0]["out"]
    return np.ascontiguousarray(got.reshape(P, DT, SEQ).transpose(2, 1, 0)).reshape(1, SEQ, D)
```

```python
from contextlib import ExitStack

import numpy as np

import concourse.bass as bass
from concourse import mybir

P = 128
SEQ = 512
D = 1024
DT = D // P
FF = 4 * D
FT = FF // P
HEAD = 64
NORM_EPS = 1e-6
GN_EPS = 64e-5
NEG = -1e30
ARENA = 30800
UPB = 8
RING = 4
AHEAD = 2
BLOCK = UPB * P
CH = 64
NCH = SEQ // CH
LEVELS = 6
S5W, S5G, S5N = 512, 32, 64
ST = S5G * S5N // P
XT = S5W // P
LRUW = 1280
LT = LRUW // P
CONV = 4
PLE = 256
TWO_PI = 6.283185
PI_BELOW = 3.1415925
ROUND = 1.5 * 2.0 ** 23
ROUND12 = 1.5 * 2.0 ** 11
TURN_PARTS = [6.28125, 0.0019350051879882812, 3.01991598196e-07]
DECAY = float(np.exp(-0.5))
SINK_W = 3 * P + SEQ
PAD = SEQ + 2
LPAD = SEQ + CONV - 1

F32 = mybir.dt.float32
F32R = mybir.dt.float32r
ALU = mybir.AluOpType
ACT = mybir.ActivationFunctionType
AX = mybir.AxisListType

DENSE = [
    ("qk", 13, DT), ("v", 5, DT), ("attn_out", DT, DT),
    ("up0a", FT // 2, DT), ("down0a", DT, FT // 2), ("up0b", FT // 2, DT), ("down0b", DT, FT // 2),
    ("lora_w", 1, DT), ("lora_a", 1, DT), ("lora_g", 2, DT),
    ("r", DT, DT), ("k", DT, DT), ("rv", DT, DT), ("o", DT, DT),
    ("up1a", FT // 2, DT), ("down1a", DT, FT // 2), ("up1b", FT // 2, DT), ("down1b", DT, FT // 2),
    ("w_in", 40, DT), ("w_in_end", 2 * XT + 2 * LT + 2 * DT - 40, DT), ("glu", 2 * XT, XT), ("w_bs", DT, XT),
    ("lru", 2 * LT, 1), ("w_bl", DT, LT), ("w_out", DT, DT), ("ple", DT, PLE // P), ("gate", DT, DT),
]


SPLIT = {"qk", "v", "attn_out", "w_in", "w_in_end", "up0a", "down0a", "up0b", "down0b", "up1a", "down1a", "up1b", "down1b"}


def plan():
    first_block, first_tile, last_tile, split_count = {}, {}, [], []
    tile = split = 0
    for name, n, k in DENSE:
        first_block[name], first_tile[name] = len(last_tile), tile
        units = n * k
        for b in range(-(-units // UPB)):
            last = min(units, (b + 1) * UPB) - 1
            last_tile.append(tile + last // k + 1)
            split += name in SPLIT
            split_count.append(split)
        tile += n
    return first_block, first_tile, last_tile, split_count


FIRST_BLOCK, FIRST_TILE, LAST_TILE, SPLIT_COUNT = plan()
SHAPE = {name: (n, k) for name, n, k in DENSE}
NBLOCKS = len(LAST_TILE)

COLS = {}
_at = 0
for _name, _n in [("norm_g", 8 * DT), ("mu_prev", 6 * DT), ("mu_next", 6 * DT), ("k_k", DT), ("k_a", DT),
                  ("r_k", DT), ("gn_w", DT), ("gn_b", DT), ("w0", 2 * DT), ("a0", 2 * DT), ("g_pre", DT),
                  ("g_post", DT), ("a_re", ST), ("a_im", ST), ("log_dt", ST), ("s5_d", XT),
                  ("conv_w", CONV * LT), ("conv_b", LT), ("b_a", LT), ("b_x", LT), ("lam", LT),
                  ("sink", 16)]:
    COLS[_name] = _at
    _at += _n
NCOLS = _at

CONSTS = {}
_at = 0
for _name, _n in [("mean", P), ("head_sum", P), ("head_mean", P), ("ident", P), ("iota", SEQ), ("carry", SEQ),
                  ("eye", CH), ("incl", 2 * CH), ("strict", 2 * CH), ("level_n", 2 * CH),
                  ("level", 2 * LEVELS * CH), ("eps", 4)]:
    CONSTS[_name] = _at
    _at += _n
NCONST = _at


def constants():
    c = np.zeros((P, NCONST), np.float32)

    def put(name, a):
        c[:, CONSTS[name]:CONSTS[name] + a.shape[1]] = a

    heads = np.kron(np.eye(P // HEAD), np.ones((HEAD, HEAD)))
    put("mean", np.full((P, P), 1.0 / D))
    put("head_sum", heads)
    put("head_mean", heads / HEAD)
    put("ident", np.eye(P))
    put("iota", np.broadcast_to(np.arange(SEQ, dtype=np.float32), (P, SEQ)))
    put("carry", np.broadcast_to(np.arange(SEQ) % CH != 0, (P, SEQ)))
    row, col = np.arange(CH)[:, None], np.arange(CH)[None, :]

    def both(m):
        return np.concatenate([m, m], axis=0)

    def level(rows_first, l):
        w = 1 << l
        same = (row // (2 * w)) == (col // (2 * w))
        low, high = (row, col) if rows_first else (col, row)
        return same & (low // w % 2 == 0) & (high // w % 2 == 1)

    put("eye", both(np.eye(CH)))
    put("incl", np.concatenate([both(row <= col), both(row >= col)], axis=1))
    put("strict", np.concatenate([both(row < col), both(row > col)], axis=1))
    put("level_n", np.concatenate([both(level(True, 0)), both(level(False, 0))], axis=1))
    put("level", np.concatenate([both(level(d == 1, l)) for d in range(2) for l in range(LEVELS)], axis=1))
    put("eps", np.broadcast_to(np.array([NORM_EPS, GN_EPS, 0.0, 1.0], np.float32), (P, 4)))
    return c


def bias_constants():
    d = np.arange(2 * SEQ) - (SEQ - 1)
    n = np.abs(d)
    nf = np.maximum(n, 1).astype(np.float32)
    large = 8 + (np.log(nf / np.float32(8)) / np.float32(np.log(1024 / 8)) * np.float32(8)).astype(np.int32)
    bucket = np.where(d > 0, 16, 0) + np.where(n < 8, n, np.minimum(large, 15))
    onehot = np.zeros((32, 2 * SEQ), np.float32)
    onehot[bucket, np.arange(2 * SEQ)] = 1.0
    count = sum(((n % dil == 0) & (n // dil <= window // 2 // dil)).astype(np.int64)
                for window, dil in ((128, 1), (512, 4), (2048, 16)))
    line_a = np.where(count > 0, np.log(np.maximum(count, 1)), NEG)
    line_b = np.where(n <= 128, 0.0, NEG)
    lines = np.concatenate([np.broadcast_to(line_a, (8, 2 * SEQ)), np.broadcast_to(line_b, (8, 2 * SEQ))])
    return onehot, lines.astype(np.float32)




def program(nc, t, out):
    ctx = ExitStack()
    with ctx:
        def sb(name, width):
            return ctx.enter_context(nc.sbuf_tensor(name, [P, width], F32))

        sems = {}

        def sem(name):
            if name not in sems:
                sems[name] = ctx.enter_context(nc.semaphore(name))
            return sems[name]

        def rounded(name, buf, width, first=0, dtype=F32R):
            return nc.alloc_sbuf_tensor_at(name, [P, width], dtype, offset=nc.lookup_mloc(buf).addr + 4 * first)

        ring = sb("ring", RING * BLOCK)
        ring_lo = rounded("ring_lo", ring, RING * BLOCK)
        ring_hi = ctx.enter_context(nc.sbuf_tensor("ring_hi", [P, RING * BLOCK], F32R))
        h = sb("h", DT * SEQ)
        u = sb("u", DT * PAD)
        u_lo = rounded("u_lo", u, DT * PAD)
        cols = sb("cols", NCOLS)
        consts = sb("consts", NCONST)
        sq = sb("sq", 2 * SEQ)
        rstd = sb("rstd", SEQ)
        small = sb("small", 64)
        der = sb("der", 6 * DT + DT + 8 * ST + 2 * LT)
        s5c = sb("s5c", ST * 2 * 32)
        arena = sb("arena", ARENA)

        ps = ctx.enter_context(nc.psum_tensor("ps", [P, 8 * SEQ], F32))
        lines_dram = nc.dram_tensor("bias_lines", [16, 2 * SEQ], F32)

        top = [0]

        def take(width):
            a = arena[:, top[0]:top[0] + width]
            top[0] += width
            assert top[0] <= ARENA, top[0]
            return a

        def take_rounded(name, width):
            take(width)
            return rounded(name, arena, width, top[0] - width)

        def take_parts(name, width):
            value, low = take(width), rounded(name + "_lo", arena, width, top[0] - width)
            return value, low, take_rounded(name + "_hi", width)

        def bank(b, width=SEQ):
            return ps[:, b * SEQ:b * SEQ + width]

        def tile(buf, i):
            return buf[:, bass.ts(i, SEQ)]

        def u_tile(i, shift=0):
            return u[:, bass.ds(i * PAD + 1 + shift, SEQ)]

        def u_lo_tile(i):
            return u_lo[:, bass.ds(i * PAD + 1, SEQ)]

        def col(name, i=0):
            return cols[:, bass.ds(COLS[name] + i, 1)]

        def const(name, i=0, width=P):
            return consts[:, CONSTS[name] + i * width:CONSTS[name] + (i + 1) * width]

        def square_tile(n, x):
            return u_tile(x) if n % 2 else sq[:, x % 2 * SEQ:(x % 2 + 1) * SEQ]

        def chunks(a):
            return a.rearrange("p (c s) -> p c s", c=NCH)

        def mask(name, i):
            return const(name, i, CH).unsqueeze(1).to_broadcast([P, NCH, CH])

        MU0, OMKA, DT_, X_, TH_, MAG, PHH, PHL, ZRE, ZIM = [
            0, 48, 56, 56 + ST, 56 + 2 * ST, 56 + 3 * ST, 56 + 4 * ST, 56 + 5 * ST, 56 + 6 * ST, 56 + 7 * ST]
        SP4 = 56 + 8 * ST

        def derived(at, n=1):
            return der[:, at:at + n]

        wbuf = take(DT * SEQ)
        stage0 = top[0]
        qT = take(DT * SEQ)
        kT = take(5 * SEQ)
        vtok = take(4 * 640)
        attnT = take(DT * SEQ)
        bias = [take(SINK_W) for _ in range(4)]
        q_st = [take(SEQ) for _ in range(2)]
        k_st = take(SEQ)
        s_sb = [take(SEQ) for _ in range(2)]
        p_sb = [take(SEQ) for _ in range(2)]
        pt_sb = [take(SEQ) for _ in range(2)]
        o_tok = [take(P) for _ in range(2)]
        line_sb, line_const = attnT[0:16, 0:2 * SEQ], attnT[0:16, 2 * SEQ:4 * SEQ]
        rel_sb, onehot = attnT[0:32, 4 * SEQ:4 * SEQ + 16], attnT[0:32, 5 * SEQ:7 * SEQ]
        bias0 = stage0 + (DT + 5 + DT) * SEQ + 4 * 640
        attn_u_hi = take_rounded("attn_u_hi", DT * SEQ)
        attnT_lo = rounded("attnT_lo", arena, DT * SEQ, bias0 - DT * SEQ)
        attnT_hi = rounded("attnT_hi", arena, DT * SEQ, top[0] - DT * SEQ)
        s5_in = arena[:, bias0:bias0 + ST * 64]
        s5_t = [arena[:, bias0 + ST * (64 + 32 * n):bias0 + ST * (96 + 32 * n)] for n in range(2)]
        tmp0 = bias0 + ST * 128
        top[0] = stage0
        mid, mid_lo, mid_hi = take_parts("mid", FT // 2 * SEQ)
        mlp_u_hi = take_rounded("mlp_u_hi", DT * SEQ)
        relu = [take(SEQ) for _ in range(2)]
        top[0] = stage0
        rT = wbuf
        kk = take(DT * SEQ)
        kTr = take(DT * SEQ)
        vTr = take(DT * SEQ)
        lo_w, lo_a = take(SEQ), take(SEQ)
        lo_g = [take(SEQ) for _ in range(2)]
        lora2 = take(6 * P)
        pair0 = top[0]
        mixb = [take(DT * SEQ) for _ in range(2)]
        top[0] = pair0
        spare = [u[:, n * SEQ:(n + 1) * SEQ] for n in range(DT)]
        ring_hi_values = rounded("ring_hi_values", ring_hi, RING * BLOCK, dtype=F32)
        spare += [b[:, n * SEQ:(n + 1) * SEQ] for b in (ring, ring_hi_values) for n in range(RING * BLOCK // SEQ)]
        spare += [take(SEQ) for _ in range((ARENA - top[0]) // SEQ - 2)]
        FEATURES, SCORES = ["al", "ro", "ka", "be", "kd", "g"], ["L", "Ma", "Mb", "Mr", "T", "TT", "X", "LM"]
        feats = [[{name: spare.pop(0) for name in FEATURES} for _ in range(2)] for _ in range(2)]
        R = [{name: spare.pop(0) for name in SCORES} for _ in range(2)]
        vt, v_st = sq[:, 0:SEQ], sq[:, SEQ:2 * SEQ]
        st_w = [take(CH) for _ in range(2)]
        st_u = [take(CH) for _ in range(2)]
        st_s = [[take(CH) for _ in range(2)] for _ in range(2)]
        st_p = [take(CH) for _ in range(2)]
        p_end = [[take(NCH) for _ in range(2)] for _ in range(2)]

        def over_pairs(engine, body):
            def fixed(i):
                return lambda per, c=0: i * per + c

            body(0, fixed(0), None, fixed(1))
            with engine.Fori(0, (DT - 2) // 2) as r:
                for q in range(2):
                    prev, n, nxt = [lambda per, c=0, k=k: r * (2 * per) + (k * per + c) for k in (q, q + 1, q + 2)]
                    body(1 - q, n, prev, nxt)
            body((DT - 1) % 2, fixed(DT - 1), fixed(DT - 2), None)

        def pair_tile(buf, n):
            return buf[:, bass.ds(n(SEQ), SEQ)]

        def pair_col(name, n, d=0):
            return cols[:, bass.ds(n(1, COLS[name] + d * DT), 1)]
        top[0] = stage0
        in_u_hi = rounded("in_u_hi", arena, DT * SEQ)
        s5x = take(XT * SEQ)
        s5g = take(XT * SEQ)
        lrug = take(LT * SEQ)
        gs = take(DT * SEQ)
        gl = take(DT * SEQ)
        lrux = take(LT * LPAD)
        free0 = [take(SEQ) for _ in range((ARENA - top[0]) // SEQ)]
        sgt = free0[0:2]
        s5b = u[:, 0:2 * ST * P]
        free1 = [tile(wbuf, n) for n in range(DT)] + free0
        V = [dict(zip(["A", "B", "S", "C", "v1", "v2", "v3", "v4"], free1[8 * n:])) for n in range(2)]
        conv = [u[:, n * SEQ:(n + 1) * SEQ] for n in range(DT)] + [tile(s5x, n) for n in range(2)]
        rate = [tile(wbuf, n) for n in range(DT)] + [tile(s5x, n) for n in range(2, 4)]
        i_t, root, fa, fb = free0[0:2], free0[2:4], free0[4:6], free0[6:8]
        pT = s5g[:, 0:2 * SEQ]

        def tmp(n):
            return arena[:, tmp0 + n * ST:tmp0 + (n + 1) * ST]

        y_ready, y_taken = sem("y_ready"), sem("y_taken")
        landed = [sem(f"weights_landed_{s}") for s in range(RING)]
        block = ctx.enter_context(nc.Block())

        @block.sync
        def _(sp):
            def stream(first, end):
                b = first
                while b < end:
                    step, m = None, 1
                    while b >= RING and b + RING * (m + 1) <= end:
                        now = [LAST_TILE[b + RING * m + j - RING] for j in range(RING)]
                        was = [LAST_TILE[b + RING * (m - 1) + j - RING] for j in range(RING)]
                        gaps = {x - y for x, y in zip(now, was)}
                        if len(gaps) != 1 or step not in (None, min(gaps)):
                            break
                        step, m = min(gaps), m + 1
                    if m >= 2:
                        with sp.Fori(0, m) as i:
                            for j in range(RING):
                                sp.wait_ge(y_ready, i * step + LAST_TILE[b + j - RING])
                                slot = (b + j) % RING
                                sp.dma_start(ring[:, slot * BLOCK:(slot + 1) * BLOCK],
                                             t["wall"][bass.ds(i * RING + b + j, 1)].rearrange("a p n -> (a p) n")
                                             ).then_inc(landed[slot], 16)
                        b += RING * m
                    else:
                        if b >= RING:
                            sp.wait_ge(y_ready, LAST_TILE[b - RING])
                        slot = b % RING
                        sp.dma_start(ring[:, slot * BLOCK:(slot + 1) * BLOCK], t["wall"][b]).then_inc(landed[slot], 16)
                        b += 1

            sp.dma_start(h[:, :], t["x"]).then_inc(sem("x_loaded"), 16)
            sp.dma_start(consts[:, :], t["consts"]).then_inc(sem("consts_loaded"), 16)
            sp.dma_start(cols[:, :], t["cols"]).then_inc(sem("cols_loaded"), 16)
            sp.dma_start(rel_sb, t["rel_table"]).then_inc(sem("rel_loaded"), 16)
            sp.dma_start(onehot, t["onehot"]).then_inc(sem("onehot_loaded"), 16)
            sp.dma_start(line_const, t["lines"]).then_inc(sem("line_const_loaded"), 16)
            sp.dma_start(s5_in, t["s5_c"]).then_inc(sem("s5_c_loaded"), 16)
            stream(0, FIRST_BLOCK["attn_out"] + RING)

            def load_bias(i, half):
                for e in range(2):
                    head = i * 2 + e if half == 0 else i + 8 + 4 * e
                    src = bass.AP(lines_dram, head * (2 * SEQ), [[1, P], [1, SINK_W]])
                    sp.dma_start(bias[2 * half + e], src).then_inc(sem(f"bias_landed_{2 * half + e}"), 16)

            sp.wait_ge(sem("lines_stored"), 16)
            sp.wait_ge(sem("s5c_ready"), 1)
            load_bias(0, 0)
            load_bias(0, 1)
            with sp.Fori(1, 4) as i:
                for half in range(2):
                    sp.wait_ge(sem("s_biased"), i * 16 + (8 * half - 8))
                    load_bias(i, half)
            stream(FIRST_BLOCK["attn_out"] + RING, FIRST_BLOCK["o"])

            def load_lora2(i):
                sp.dma_start(lora2, t["lora2"][bass.ds(i, 1)].rearrange("a p n -> (a p) n")
                             ).then_inc(sem("lora2_landed"), 16)

            sp.wait_ge(y_ready, FIRST_TILE["r"])
            load_lora2(0)
            with sp.Fori(1, DT) as i:
                sp.wait_ge(sem("z_ready"), i * 6)
                load_lora2(i)
            sp.wait_ge(sem("pair_done"), DT)
            stream(FIRST_BLOCK["o"], NBLOCKS)

        @block.tensor
        def _(pe):
            def dense(name, rhs, steps=1, rhs_ready=None, first=0, count=None):
                n, k = SHAPE[name]
                per = n // steps
                b0, t0 = FIRST_BLOCK[name], FIRST_TILE[name]

                def step(i):
                    for j in range(per):
                        if t0 + j >= 2:
                            pe.wait_ge(y_taken, i * per + (t0 + j - 1))
                        for x in range(k):
                            unit = j * k + x
                            b = b0 + unit // UPB
                            if unit % UPB == 0 or x == 0:
                                if name in SPLIT:
                                    pe.wait_ge(sem("weights_split"), i * (per * k // UPB) + SPLIT_COUNT[b])
                                else:
                                    rounds = per * k // UPB // RING if steps > 1 else 0
                                    pe.wait_ge(landed[b % RING], i * (16 * rounds) + 16 * (b // RING + 1))
                            if rhs_ready is not None:
                                rhs_ready(j, x)
                            at = (b % RING) * BLOCK + unit % UPB * P
                            if name in SPLIT:
                                high, low = rhs(x)
                                y, w_hi, w_lo = bank((t0 + j) % 2), ring_hi[:, at:at + P], ring_lo[:, at:at + P]
                                nc.tensor.matmul(y, w_hi, high, start=x == 0, stop=False)
                                nc.tensor.matmul(y, w_hi, low, start=False, stop=False)
                                mm = nc.tensor.matmul(y, w_lo, high, start=False, stop=x == k - 1)
                                continue
                            mm = nc.tensor.matmul(bank((t0 + j) % 2), ring[:, at:at + P], rhs(x),
                                                  start=x == 0, stop=x == k - 1)
                        mm.then_inc(y_ready, 1)

                if steps == 1:
                    step(0)
                else:
                    assert per % 2 == 0 and per * k % (UPB * RING) == 0
                    with pe.Fori(0, steps) as i:
                        step(i)

            def mean_square(n):
                for x in range(DT):
                    pe.wait_ge(sem("sq_ready"), DT * n + x + 1)
                    if x == 0 and n:
                        pe.wait_ge(sem("rms_ready"), n)
                    nc.tensor.matmul(bank(7), const("mean"), square_tile(n, x),
                                     start=x == 0, stop=x == DT - 1).then_inc(sem("sq_used"), 1)

            def split_tile(n):
                return lambda j, x: pe.wait_ge(sem("u_split"), DT * n + x + 1) if j == 0 else None

            pe.wait_ge(sem("rel_loaded"), 16)
            pe.wait_ge(sem("onehot_loaded"), 16)
            for half in range(2):
                mm = nc.tensor.matmul(bank(5 + half)[0:16, :], rel_sb, onehot[:, half * SEQ:(half + 1) * SEQ],
                                      start=True, stop=True)
            mm.then_inc(sem("lines_ready"), 1)

            pe.wait_ge(sem("consts_loaded"), 16)
            mean_square(0)
            dense("qk", lambda x: (tile(attn_u_hi, x), u_lo_tile(x)), rhs_ready=split_tile(0))
            t0, b0 = FIRST_TILE["v"], FIRST_BLOCK["qk"]
            for j in range(5):
                pe.wait_ge(y_taken, t0 + j - 1)
                first = SHAPE["qk"][0] * DT + j * DT
                b = b0 + first // UPB
                pe.wait_ge(sem("weights_split"), SPLIT_COUNT[b])
                for tok in range(4):
                    for x in range(DT):
                        at = (b % RING) * BLOCK + x * P
                        y = bank((t0 + j) % 2)[:, tok * P:(tok + 1) * P]
                        high = attn_u_hi[:, x * SEQ + tok * P:x * SEQ + (tok + 1) * P]
                        low = u_lo[:, x * PAD + 1 + tok * P:x * PAD + 1 + (tok + 1) * P]
                        w_hi, w_lo = ring_hi[:, at:at + P], ring_lo[:, at:at + P]
                        nc.tensor.matmul(y, high, w_hi, start=x == 0, stop=False)
                        nc.tensor.matmul(y, high, w_lo, start=False, stop=False)
                        mm = nc.tensor.matmul(y, low, w_hi, start=False, stop=x == DT - 1)
                mm.then_inc(y_ready, 1)
            pe.wait_ge(y_taken, FIRST_TILE["attn_out"])

            with pe.Fori(0, 4) as i:
                def place(n):
                    return n // 8, n % 8 // 2, n % 2

                def scores(n):
                    half, qi, e = place(n)
                    if n % 8 == 0:
                        pe.wait_ge(sem("q_staged"), i * 2 + (half + 1))
                        pe.wait_ge(sem("k_staged"), i + 1)
                    if n >= 2:
                        pe.wait_ge(sem("s_biased"), i * 16 + (n - 1))
                    rows = slice(e * HEAD, (e + 1) * HEAD)
                    keys = k_st[rows, :] if half == 0 else kT[rows, 4 * SEQ:5 * SEQ]
                    nc.tensor.matmul(bank(2 + n % 2), q_st[half][rows, qi * P:(qi + 1) * P], keys,
                                     start=True, stop=True).then_inc(sem("s_ready"), 1)

                def turn(n):
                    pe.wait_ge(sem("p_ready"), i * 16 + (n + 1))
                    if n >= 2:
                        pe.wait_ge(sem("pt_taken"), i * 16 + (n - 1))
                    for x in range(4):
                        tr = nc.tensor.transpose(bank(4 + n % 2)[:, x * P:(x + 1) * P],
                                                 p_sb[n % 2][:, x * P:(x + 1) * P], const("ident"))
                    tr.then_inc(sem("pt_ready"), 1)

                def values(n):
                    half, qi, e = place(n)
                    pe.wait_ge(sem("pt_taken"), i * 16 + (n + 1))
                    if n >= 2:
                        pe.wait_ge(sem("o_taken"), i * 16 + (n - 1))
                    for x in range(4):
                        at = x * 640 + e * HEAD
                        v = vtok[:, bass.ds(i * P + at, HEAD)] if half == 0 else vtok[:, at + 512:at + 512 + HEAD]
                        mm = nc.tensor.matmul(bank(6 + n % 2, HEAD),
                                              pt_sb[n % 2][:, x * P:(x + 1) * P], v, start=x == 0, stop=x == 3)
                    mm.then_inc(sem("o_ready"), 1)

                def turn_out(m):
                    pe.wait_ge(sem("o_taken"), i * 16 + (2 * m + 2))
                    if m >= 2:
                        pe.wait_ge(sem("ot_taken"), i * 8 + m)
                    nc.tensor.transpose(bank(m % 2, P), o_tok[m % 2], const("ident")
                                        ).then_inc(sem("ot_ready"), 1)

                pe.wait_ge(sem("ot_taken"), i * 8 + 1)
                scores(0)
                scores(1)
                for n in range(16):
                    turn(n)
                    if n + 2 < 16:
                        scores(n + 2)
                    if n >= 1:
                        values(n - 1)
                    if n >= 3 and n % 2:
                        turn_out((n - 3) // 2)
                values(15)
                turn_out(7)

            pe.wait_ge(sem("ot_taken"), 33)
            dense("attn_out", lambda x: (tile(attnT_hi, x), tile(attnT_lo, x)),
                  rhs_ready=lambda j, x: pe.wait_ge(sem("attn_split"), x + 1) if j == 0 else None)
            mean_square(1)
            def mlp(n, first_norm):
                mean_square(first_norm)
                for half, part in enumerate("ab"):
                    dense(f"up{n}{part}", lambda x: (tile(mlp_u_hi, x), u_lo_tile(x)), steps=2,
                          rhs_ready=split_tile(n + 1))
                    dense(f"down{n}{part}", lambda x: (tile(mid_hi, x), tile(mid_lo, x)), steps=4, rhs_ready=lambda j, x: (
                        pe.wait_ge(sem("mid_split"), FT * n + FT // 2 * half + x + 1) if j == 0 else None))
                mean_square(first_norm + 1)

            mlp(0, 2)
            mean_square(4)
            for m, (name, waits) in enumerate([("lora_w", 1), ("lora_a", 1), ("lora_g", 1), ("r", 1), ("k", 1), ("rv", 1)]):
                dense(name, lambda x: tile(mixb[m % 2], x),
                      rhs_ready=lambda j, x: pe.wait_ge(sem("mixed"), DT * m + x + 1) if j == 0 else None)
            for x in range(DT):
                pe.wait_ge(sem("kk_squared"), x + 1)
                if x == 0:
                    pe.wait_ge(y_taken, FIRST_TILE["o"])
                if x >= 2:
                    pe.wait_ge(sem("kk_clamped"), x - 1)
                nc.tensor.matmul(bank(6 + x % 2), const("head_sum"), sq[:, x % 2 * SEQ:(x % 2 + 1) * SEQ],
                                 start=True, stop=True).then_inc(sem("kk_summed"), 1)
            pe.wait_ge(sem("kk_ready"), DT)

            def each(out, lhsT, rhs):
                pe.nop(nofuse=True)
                for c in range(NCH):
                    for e in range(2):
                        rows, at = slice(e * HEAD, (e + 1) * HEAD), slice(c * CH, (c + 1) * CH)
                        mm = nc.tensor.matmul(out[rows, at], lhsT[rows, at], rhs[rows, at], start=True, stop=True)
                return mm

            def each_turned(out, a):
                for at in range(0, SEQ, P):
                    mm = nc.tensor.transpose(out[:, at:at + P], a[:, at:at + P], const("ident"))
                return mm

            A, B, C, O = [[bank(4 * d + x) for d in range(2)] for x in range(4)]

            def hidden_out(n, step):
                if step == 0:
                    pe.wait_ge(sem("lora2_landed"), n(16, 16))
                else:
                    pe.wait_ge(sem("z_taken"), n(6, 2 * step))
                for d in range(2):
                    k = 2 * step + d
                    nc.tensor.matmul(O[d], lora2[:, k * P:(k + 1) * P], [lo_w, lo_w, lo_a, lo_a, lo_g[0], lo_g[1]][k],
                                     start=True, stop=True).then_inc(sem("z_ready"), 1)

            def out_means(n, F):
                for d in range(2):
                    pe.wait_ge(sem("o_copied"), n(2, d + 1))
                    nc.tensor.matmul(O[d], const("head_mean"), F[d]["al"], start=True, stop=True
                                     ).then_inc(sem("mean_ready"), 1)

            def out_bonus(n, F):
                for d in range(2):
                    pe.wait_ge(sem("o_centered"), n(2, d + 1))
                    pe.wait_ge(sem("bonus_terms"), n(2, d + 1))
                    nc.tensor.matmul(O[d], const("head_sum"), F[d]["kd"], start=True, stop=True
                                     ).then_inc(sem("bonus_ready"), 1)

            def out_variances(n, F):
                for d in range(2):
                    pe.wait_ge(sem("bonus_done"), n(2, d + 1))
                    pe.wait_ge(sem("o_squared"), n(2, d + 1))
                    nc.tensor.matmul(O[d], const("head_mean"), F[d]["be"], start=True, stop=True
                                     ).then_inc(sem("var_ready"), 1)

            def pair(parity, n, prev, nxt):
                F = feats[parity]
                for d in range(2):
                    pe.wait_ge(sem("features_v"), n(2, d + 1))
                    pe.wait_ge(sem("features_p"), n(2, d + 1))
                    each(A[d], F[d]["be"], F[d]["al"]).then_inc(sem("scores_ready"), 1)
                if prev:
                    out_means(prev, feats[1 - parity])
                for d in range(2):
                    each(C[d], F[d]["ka"], F[d]["al"]).then_inc(sem("scores_ready"), 1)
                if prev:
                    out_bonus(prev, feats[1 - parity])
                for d in range(2):
                    pe.wait_ge(sem("n_copied"), n(2, d + 1))
                    each_turned(B[d], R[d]["X"]).then_inc(sem("scores_ready"), 1)
                if prev:
                    out_variances(prev, feats[1 - parity])
                for d in range(2):
                    each(A[d], F[d]["be"], F[d]["ro"]).then_inc(sem("scores_ready"), 1)
                for d in range(2):
                    pe.wait_ge(sem("l_copied"), n(2, d + 1))
                    each_turned(B[d], F[d]["be"]).then_inc(sem("scores_ready"), 1)
                for d in range(2):
                    if prev:
                        pe.wait_ge(sem("deviation"), prev(2, d + 1))
                    each(O[d], F[d]["ka"], F[d]["ro"]).then_inc(sem("scores_ready"), 1)
                for d in range(2):
                    pe.wait_ge(sem("masked_v"), n(6, 1 + d))
                    each_turned(C[d], F[d]["ka"]).then_inc(sem("scores_ready"), 1)
                pe.wait_ge(sem("masked_v"), n(6, 4))
                pe.wait_ge(sem("v_staged"), n(1, 1))
                each_turned(A[0], v_st).then_inc(sem("scores_ready"), 1)
                pe.wait_ge(sem("turned"), n(5, 5))
                for l in range(1, LEVELS):
                    for d in range(2):
                        k = 2 * (l - 1) + d
                        pe.wait_ge(sem("level_masked"), n(10, k + 1))
                        if l == 1:
                            pe.wait_ge(sem("t_started"), n(2, d + 1))
                        each(A[d], R[d]["LM"], R[d]["T"]).then_inc(sem("x_ready"), 1)
                    for d in range(2):
                        k = 2 * (l - 1) + d
                        pe.wait_ge(sem("x_taken"), n(10, k + 1))
                        if l == 1:
                            pe.wait_ge(sem("tt_started"), n(2, d + 1))
                        else:
                            pe.wait_ge(sem("tt_taken"), n(8, k - 1))
                        each(B[d], R[d]["TT"], R[d]["X"]).then_inc(sem("dt_ready"), 1)
                    for d in range(2):
                        pe.wait_ge(sem("t_updated"), n(10, 2 * (l - 1) + d + 1))
                        if l < LEVELS - 1:
                            each_turned(C[d], R[d]["T"]).then_inc(sem("tt_ready"), 1)
                    if nxt and l <= 3:
                        if l == 1:
                            pe.wait_ge(sem("masked_v"), n(6, 6))
                        hidden_out(nxt, l - 1)
                if nxt:
                    pe.wait_ge(sem("z_taken"), nxt(6, 6))
                for j in range(NCH):
                    for d in range(2):
                        k = 2 * j + d
                        c = j if d == 0 else NCH - 1 - j
                        at = slice(c * CH, (c + 1) * CH)
                        if j:
                            pe.wait_ge(sem("state_ready"), n(14, k - 1))
                        pe.nop(nofuse=True)
                        for e in range(2):
                            rows = slice(e * HEAD, (e + 1) * HEAD)
                            mm = nc.tensor.matmul(A[d][rows, 0:CH], R[d]["Ma"][rows, at], vt[rows, at],
                                                  start=True, stop=j == 0)
                            if j:
                                mm = nc.tensor.matmul(A[d][rows, 0:CH], F[d]["al"][rows, at], st_s[d][j % 2][rows, :],
                                                      start=False, stop=True)
                        mm.then_inc(sem("w_ready"), 1)
                    for d in range(2):
                        k = 2 * j + d
                        c = j if d == 0 else NCH - 1 - j
                        at = slice(c * CH, (c + 1) * CH)
                        pe.wait_ge(sem("w_taken"), n(16, k + 1))
                        pe.nop(nofuse=True)
                        for e in range(2):
                            rows = slice(e * HEAD, (e + 1) * HEAD)
                            mm = nc.tensor.matmul(B[d][rows, 0:CH], R[d]["T"][rows, at], st_w[d][rows, :],
                                                  start=True, stop=True)
                        mm.then_inc(sem("u_ready"), 1)
                    for d in range(2):
                        k = 2 * j + d
                        c = j if d == 0 else NCH - 1 - j
                        at = slice(c * CH, (c + 1) * CH)
                        pe.wait_ge(sem("u_taken"), n(16, k + 1))
                        pe.nop(nofuse=True)
                        if j < NCH - 1:
                            for e in range(2):
                                rows = slice(e * HEAD, (e + 1) * HEAD)
                                nc.tensor.matmul(C[d][rows, 0:CH], F[d]["be"][rows, at], st_u[d][rows, :],
                                                 start=True, stop=False)
                                mm = nc.tensor.matmul(C[d][rows, 0:CH], F[d]["ka"][rows, at], vt[rows, at],
                                                      start=False, stop=True)
                            mm.then_inc(sem("s_ready_rw"), 1)
                        for e in range(2):
                            rows = slice(e * HEAD, (e + 1) * HEAD)
                            nc.tensor.matmul(O[d][rows, at], st_u[d][rows, :], R[d]["Mb"][rows, at],
                                             start=True, stop=False)
                            mm = nc.tensor.matmul(O[d][rows, at], vt[rows, at], R[d]["Mr"][rows, at],
                                                  start=False, stop=j == 0)
                            if j:
                                mm = nc.tensor.matmul(O[d][rows, at], st_s[d][j % 2][rows, :], F[d]["ro"][rows, at],
                                                      start=False, stop=True)
                        mm.then_inc(sem("o_ready_rw"), 1)

            first, last = (lambda per, c=0: c), (lambda per, c=0: (DT - 1) * per + c)
            for step in range(3):
                hidden_out(first, step)
            pe.wait_ge(sem("z_taken"), 6)
            over_pairs(pe, pair)
            out_means(last, feats[(DT - 1) % 2])
            out_bonus(last, feats[(DT - 1) % 2])
            out_variances(last, feats[(DT - 1) % 2])
            pe.wait_ge(sem("pair_done"), DT)
            dense("o", lambda x: tile(rT, x))
            mean_square(5)
            mlp(1, 6)
            mean_square(8)
            dense("w_in", lambda x: (tile(in_u_hi, x), u_lo_tile(x)), steps=5, rhs_ready=split_tile(3))
            dense("w_in_end", lambda x: (tile(in_u_hi, x), u_lo_tile(x)))
            pe.wait_ge(sem("s5b_landed"), 16)
            pe.wait_ge(y_taken, FIRST_TILE["glu"])

            def s5_out(j):
                pe.wait_ge(sem("s5_turned"), 2 * (j + 1))
                m, rows = j // 4, slice(j % 4 * 32, j % 4 * 32 + 32)
                if j % 4 == 0 and m >= 2:
                    pe.wait_ge(sem("s5_skipped"), m - 1)
                nc.tensor.matmul(bank(6 + m % 2)[rows, :], s5c[:, j * 64:j * 64 + 32], V[j % 2]["v1"],
                                 start=True, stop=False)
                nc.tensor.matmul(bank(6 + m % 2)[rows, :], s5c[:, j * 64 + 32:j * 64 + 64], V[j % 2]["v3"],
                                 start=False, stop=True).then_inc(sem("s5_out"), 1)

            for j in range(ST):
                if j >= 2:
                    pe.wait_ge(sem("s5_in_taken"), 4 * (j - 1))
                for x in range(2):
                    nc.tensor.matmul(bank(2 + 2 * (j % 2) + x), s5b[:, (2 * j + x) * P:(2 * j + x + 1) * P],
                                     tile(s5x, j // 4), start=True, stop=True).then_inc(sem("s5_in"), 1)
                if j >= 1:
                    s5_out(j - 1)
            s5_out(ST - 1)
            dense("glu", lambda x: tile(s5x, x),
                  rhs_ready=lambda j, x: pe.wait_ge(sem("gelu_ready"), x + 1) if j == 0 else None)
            dense("w_bs", lambda x: tile(s5g, x),
                  rhs_ready=lambda j, x: pe.wait_ge(sem("s5_gated"), x + 1) if j == 0 else None)
            t0, b0 = FIRST_TILE["lru"], FIRST_BLOCK["lru"]
            for n in range(2 * LT):
                pe.wait_ge(y_taken, t0 + n - 1)
                if n % UPB == 0:
                    b = b0 + n // UPB
                    pe.wait_ge(landed[b % RING], 16 * (b // RING + 1))
                at = ((b0 + n // UPB) % RING) * BLOCK + n % UPB * P
                pe.wait_ge(sem("conv_ready"), n // 2 + 1)
                nc.tensor.matmul(bank((t0 + n) % 2), ring[:, at:at + P], conv[n // 2], start=True, stop=True
                                 ).then_inc(y_ready, 1)
            dense("w_bl", lambda x: tile(lrug, x),
                  rhs_ready=lambda j, x: pe.wait_ge(sem("lru_gated"), x + 1) if j == 0 else None)
            dense("w_out", lambda x: tile(gs, x),
                  rhs_ready=lambda j, x: pe.wait_ge(sem("merged"), x + 1) if j == 0 else None)
            mean_square(9)
            pe.wait_ge(sem("p_loaded"), 16)
            dense("ple", lambda x: pT[:, x * SEQ:(x + 1) * SEQ])
            dense("gate", lambda x: tile(h, x),
                  rhs_ready=lambda j, x: pe.wait_ge(sem("h_ready"), 4 * DT + x + 1) if j == 0 else None)

        @block.scalar
        def _(act):
            def squares(n, x, src):
                if n % 2 == 0 and x >= 2:
                    act.wait_ge(sem("sq_used"), DT * n + x - 1)
                nc.scalar.activation(square_tile(n, x), src, ACT.Square).then_inc(sem("sq_ready"), 1)

            def split_high(b, i=0, step=0):
                slot = slice(b % RING * BLOCK, (b % RING + 1) * BLOCK)
                act.wait_ge(landed[b % RING], i * (16 * step // RING) + 16 * (b // RING + 1))
                nc.scalar.activation(ring_hi[:, slot], ring[:, slot], ACT.Copy).then_inc(sem("weights_high"), 1)

            def split_u_high(n, u_hi):
                for x in range(DT):
                    act.wait_ge(sem("normed"), n * DT + x + 1)
                    nc.scalar.activation(tile(u_hi, x), u_tile(x), ACT.Copy).then_inc(sem("u_high"), 1)

            def root_mean(n):
                act.wait_ge(sem("sq_used"), DT * (n + 1))
                if n:
                    act.wait_ge(sem("normed"), DT * n)
                nc.scalar.activation(rstd[:, :], bank(7), ACT.Sqrt, bias=const("eps", 0, 1)).then_inc(sem("rms_ready"), 1)

            def pre_norm(n):
                for x in range(DT):
                    if n == 0:
                        act.wait_ge(sem("x_loaded"), 16)
                    else:
                        act.wait_ge(sem("h_ready"), (n // 2 - 1) * DT + x + 1)
                    squares(n, x, tile(h, x))
                root_mean(n)

            def take_out(name, n, dst=wbuf, splits=False):
                for x in range(DT):
                    if splits and x + AHEAD < DT:
                        split_high(FIRST_BLOCK[name] + x + AHEAD)
                    act.wait_ge(y_ready, FIRST_TILE[name] + x + 1)
                    squares(n, x, bank((FIRST_TILE[name] + x) % 2))
                    nc.scalar.activation(tile(dst, x), bank((FIRST_TILE[name] + x) % 2), ACT.Copy).then_inc(y_taken, 1)
                root_mean(n)

            def take_tile(name, x, dst, func=ACT.Copy, **kw):
                act.wait_ge(y_ready, FIRST_TILE[name] + x + 1)
                nc.scalar.activation(dst, bank((FIRST_TILE[name] + x) % 2), func, **kw).then_inc(y_taken, 1)

            act.wait_ge(sem("cols_loaded"), 16)
            act.wait_ge(sem("consts_loaded"), 16)
            nc.scalar.activation(derived(DT_, ST), cols[:, COLS["log_dt"]:COLS["log_dt"] + ST], ACT.Exp
                                 ).then_inc(sem("dt_exp"), 1)
            act.wait_ge(sem("s5_angles"), 1)
            nc.scalar.activation(derived(MAG, ST), derived(X_, ST), ACT.Exp).then_inc(sem("s5_exp"), 1)
            nc.scalar.activation(tmp(0), derived(X_, ST), ACT.Tanh, scale=0.5).then_inc(sem("s5_exp"), 1)
            nc.scalar.activation(tmp(1), derived(TH_, ST), ACT.Sin).then_inc(sem("s5_exp"), 1)
            nc.scalar.activation(tmp(2), derived(TH_, ST), ACT.Sin, scale=0.5).then_inc(sem("s5_exp"), 1)
            act.wait_ge(sem("lam_abs"), 1)
            nc.scalar.activation(tmp(10)[:, 0:LT], tmp(9)[:, 0:LT], ACT.Exp, scale=-1.0).then_inc(sem("lam_exp"), 1)
            act.wait_ge(sem("lines_summed"), 2)
            act.dma_start(lines_dram[:, :], line_sb).then_inc(sem("lines_stored"), 16)

            pre_norm(0)
            for b in range(AHEAD):
                split_high(b)
            split_u_high(0, attn_u_hi)
            for x in range(DT):
                split_high(x + AHEAD)
                take_tile("qk", x, tile(qT, x), scale=float(HEAD) ** -0.5)
            for x in range(5):
                split_high(DT + x + AHEAD)
                take_tile("qk", DT + x, tile(kT, x))
            for x in range(5):
                split_high(DT + 5 + x + AHEAD)
                take_tile("v", x, vtok.rearrange("p (t n) -> p t n", t=4)[:, :, x * P:(x + 1) * P])
            with act.Fori(0, 4) as i:
                def exponent(n):
                    head = (2 * i + n % 2) if n < 8 else (i + 8 + 4 * (n % 2))
                    act.wait_ge(sem("max_ready"), i * 16 + (n + 1))
                    if n >= 2:
                        act.wait_ge(sem("pt_ready"), i * 16 + (n - 1))
                    r = n % 4
                    nc.scalar.activation(p_sb[n % 2], s_sb[n % 2], ACT.Exp, bias=small[:, 4 + r:5 + r],
                                         accum_out=small[:, 8 + r:9 + r]).then_inc(sem("p_ready"), 1)
                    nc.scalar.activation(small[:, 12 + r:13 + r], col("sink", head), ACT.Exp,
                                         bias=small[:, 4 + r:5 + r]).then_inc(sem("sink_ready"), 1)

                def output(n):
                    act.wait_ge(sem("o_ready"), i * 16 + (n + 1))
                    act.wait_ge(sem("rden_ready"), i * 16 + (n + 1))
                    m, r = n // 2, n % 4
                    if m >= 2:
                        act.wait_ge(sem("ot_ready"), i * 8 + (m - 1))
                    nc.scalar.activation(o_tok[m % 2][:, n % 2 * HEAD:(n % 2 + 1) * HEAD],
                                         bank(6 + n % 2, HEAD), ACT.Copy,
                                         scale=small[:, 16 + r:17 + r]).then_inc(sem("o_taken"), 1)

                def turned(m):
                    act.wait_ge(sem("ot_ready"), i * 8 + (m + 1))
                    at = m % 4 * P + (4 * SEQ if m >= 4 else 0)
                    nc.scalar.activation(attnT[:, bass.ds(i * SEQ + at, P)], bank(m % 2, P)[:, ::-1],
                                         ACT.Copy).then_inc(sem("ot_taken"), 1)

                for n in range(16):
                    exponent(n)
                    if n >= 2:
                        output(n - 2)
                    if n >= 5 and n % 2:
                        turned((n - 5) // 2)
                output(14)
                turned(6)
                output(15)
                turned(7)
            act.wait_ge(sem("ot_taken"), 33)
            for x in range(DT):
                nc.scalar.activation(tile(attnT_hi, x), tile(attnT, x), ACT.Copy).then_inc(sem("attn_high"), 1)
            take_out("attn_out", 1, splits=True)

            def mlp(n, first_norm):
                for b in range(AHEAD):
                    split_high(FIRST_BLOCK[f"up{n}a"] + b)
                pre_norm(first_norm)
                split_u_high(first_norm, mlp_u_hi)
                for half, part in enumerate("ab"):
                    t0, b0 = FIRST_TILE[f"up{n}{part}"], FIRST_BLOCK[f"up{n}{part}"]
                    with act.Fori(0, 2) as i:
                        for j in range(8):
                            split_high(b0 + j + AHEAD, i, 8)
                            act.wait_ge(y_ready, i * 8 + (t0 + j + 1))
                            nc.scalar.activation(relu[j % 2], bank((t0 + j) % 2), ACT.Relu).then_inc(sem("relu_ready"), 1)
                            act.wait_ge(y_taken, i * 8 + (t0 + j + 1))
                            at = bass.ds(i * (8 * SEQ) + j * SEQ, SEQ)
                            nc.scalar.activation(mid_hi[:, at], mid[:, at], ACT.Copy).then_inc(sem("mid_high"), 1)
                    t0, b0 = FIRST_TILE[f"down{n}{part}"], FIRST_BLOCK[f"down{n}{part}"]
                    for x in range(DT):
                        for b in range(b0 + 2 * x + AHEAD, b0 + 2 * x + 2 + AHEAD):
                            if half == 0 or b < b0 + 2 * DT:
                                split_high(b)
                        if half == 0:
                            act.wait_ge(y_ready, t0 + x + 1)
                            nc.scalar.activation(tile(wbuf, x), bank((t0 + x) % 2), ACT.Copy).then_inc(y_taken, 1)
                        else:
                            act.wait_ge(y_taken, t0 + x + 1)
                            squares(first_norm + 1, x, tile(wbuf, x))
                root_mean(first_norm + 1)

            mlp(0, 2)
            pre_norm(4)
            act.wait_ge(sem("mu_ready"), 1)
            for m, c in enumerate([1, 4, 5, 0, 2, 3]):
                if m >= 2:
                    name = ["lora_w", "lora_a", "lora_g", "r"][m - 2]
                    act.wait_ge(y_ready, FIRST_TILE[name] + SHAPE[name][0])
                for x in range(DT):
                    if m == 0:
                        act.wait_ge(sem("normed"), 4 * DT + x + 1)
                    at = MU0 + c * DT + x
                    nc.scalar.activation(tile(mixb[m % 2], x), u_tile(x), ACT.Copy, scale=der[:, at:at + 1]
                                         ).then_inc(sem("mix_started"), 1)
                if m == 0:
                    continue
                if m == 1:
                    take_tile("lora_w", 0, lo_w, ACT.Tanh)
                elif m == 2:
                    take_tile("lora_a", 0, lo_a)
                elif m == 3:
                    for x in range(2):
                        take_tile("lora_g", x, lo_g[x], ACT.Sigmoid)
                else:
                    for x in range(DT):
                        take_tile("r" if m == 4 else "k", x, tile(rT if m == 4 else kTr, x))
            for x in range(DT):
                take_tile("rv", x, tile(vTr, x))
            for x in range(DT):
                if x >= 2:
                    act.wait_ge(sem("kk_summed"), x - 1)
                nc.scalar.activation(sq[:, x % 2 * SEQ:(x % 2 + 1) * SEQ], tile(kTr, x), ACT.Square,
                                     scale=col("k_k", x)).then_inc(sem("kk_squared"), 1)
                if x >= 1:
                    act.wait_ge(sem("kk_clamped"), x)
                    nc.scalar.activation(tile(kk, x - 1), tile(kk, x - 1), ACT.Sqrt).then_inc(sem("kk_root"), 1)
            act.wait_ge(sem("kk_clamped"), DT)
            nc.scalar.activation(tile(kk, DT - 1), tile(kk, DT - 1), ACT.Sqrt).then_inc(sem("kk_root"), 1)

            def take_turned(dst, src, name):
                for c in range(2):
                    for e in range(2):
                        to = dst.rearrange("p (b c s) -> p b c s", c=2, s=CH)[e * HEAD:(e + 1) * HEAD, :, c, :]
                        of = src.rearrange("p (b e s) -> p b e s", e=2, s=CH)[c * CH:(c + 1) * CH, :, e, :]
                        ins = nc.scalar.activation(to, of, ACT.Copy)
                ins.then_inc(sem(name), 1)

            def features(n, F, step):
                for d in range(2):
                    act.wait_ge(sem("z_ready"), n(6, 2 * step + d + 1))
                    if step == 0:
                        nc.scalar.activation(F[d]["al"], bank(4 * d + 3), ACT.Sigmoid, bias=pair_col("w0", n, d)
                                             ).then_inc(sem("z_taken"), 1)
                    elif step == 1:
                        nc.scalar.activation(F[d]["be"], bank(4 * d + 3), ACT.Sigmoid, bias=pair_col("a0", n, d)
                                             ).then_inc(sem("z_taken"), 1)
                    else:
                        nc.scalar.activation(F[d]["g"], bank(4 * d + 3), ACT.Copy).then_inc(sem("z_taken"), 1)
                if step == 1:
                    for d in range(2):
                        act.wait_ge(sem("decay_summed"), n(2, d + 1))
                        nc.scalar.activation(F[d]["ka"], F[d]["ro"], ACT.Exp, scale=DECAY).then_inc(sem("decays_ready"), 1)
                        nc.scalar.activation(F[d]["al"], F[d]["al"], ACT.Exp, scale=-DECAY).then_inc(sem("decays_ready"), 1)
                        act.wait_ge(sem("decays_ready"), n(6, 3 * d + 1))
                        nc.scalar.activation(F[d]["ro"], F[d]["ro"], ACT.Exp, scale=-DECAY).then_inc(sem("decays_ready"), 1)

            def out_squares(n, F):
                for d in range(2):
                    act.wait_ge(sem("o_centered"), n(2, d + 1))
                    nc.scalar.activation(F[d]["be"], F[d]["al"], ACT.Square).then_inc(sem("o_squared"), 1)

            def out_deviations(n, F):
                for d in range(2):
                    act.wait_ge(sem("var_ready"), n(2, d + 1))
                    nc.scalar.activation(F[d]["ka"], bank(4 * d + 3), ACT.Sqrt, bias=const("eps", 1, 1)
                                         ).then_inc(sem("deviation"), 1)

            def pair(parity, n, prev, nxt):
                F, G = feats[parity], feats[1 - parity]
                for d in range(2):
                    act.wait_ge(sem("scores_ready"), n(15, 1 + d))
                    nc.scalar.activation(R[d]["X"], bank(4 * d), ACT.Copy).then_inc(sem("n_copied"), 1)
                if prev:
                    out_squares(prev, G)
                for d in range(2):
                    act.wait_ge(sem("scores_ready"), n(15, 5 + d))
                    take_turned(R[d]["L"], bank(4 * d + 1), "l_copied")
                if prev:
                    out_deviations(prev, G)
                for ready, name, b in ((9, "be", 1), (13, "ka", 2)):
                    for d in range(2):
                        act.wait_ge(sem("scores_ready"), n(15, ready + d))
                        take_turned(F[d][name], bank(4 * d + b), "turned")
                act.wait_ge(sem("scores_ready"), n(15, 15))
                take_turned(vt, bank(0), "turned")
                for l in range(1, LEVELS):
                    for d in range(2):
                        k = 2 * (l - 1) + d
                        act.wait_ge(sem("x_ready"), n(10, k + 1))
                        nc.scalar.activation(R[d]["X"], bank(4 * d), ACT.Copy).then_inc(sem("x_taken"), 1)
                    if nxt and 2 <= l <= 4:
                        if prev and l == 2:
                            act.wait_ge(sem("pair_done"), n(1))
                        features(nxt, G, l - 2)
                    for d in range(2):
                        if l < LEVELS - 1:
                            act.wait_ge(sem("tt_ready"), n(8, 2 * (l - 1) + d + 1))
                            take_turned(R[d]["TT"], bank(4 * d + 2), "tt_taken")
                for k in range(2 * NCH):
                    act.wait_ge(sem("w_ready"), n(16, k + 1))
                    nc.scalar.activation(st_w[k % 2], bank(4 * (k % 2), CH), ACT.Copy).then_inc(sem("w_taken"), 1)
                for d in range(2):
                    act.wait_ge(sem("o_ready_rw"), n(16, 15 + d))
                    nc.scalar.activation(F[d]["al"], bank(4 * d + 3), ACT.Copy).then_inc(sem("o_copied"), 1)

            first, last = (lambda per, c=0: c), (lambda per, c=0: (DT - 1) * per + c)
            for step in range(3):
                features(first, feats[0], step)
            over_pairs(act, pair)
            out_squares(last, feats[(DT - 1) % 2])
            out_deviations(last, feats[(DT - 1) % 2])
            take_out("o", 5, kTr)
            mlp(1, 6)
            for b in range(AHEAD):
                split_high(FIRST_BLOCK["w_in"] + b)
            pre_norm(8)
            split_u_high(8, in_u_hi)
            tiles = ([("s5x", x) for x in range(XT)] + [("s5g", x) for x in range(XT)]
                     + [("lrux", x) for x in range(LT)] + [("lrug", x) for x in range(LT)]
                     + [("gs", x) for x in range(DT)] + [("gl", x) for x in range(DT)])
            t0 = FIRST_TILE["w_in"]
            gated = []
            for n, (name, x) in enumerate(tiles):
                if n + AHEAD < len(tiles):
                    split_high(FIRST_BLOCK["w_in"] + n + AHEAD)
                act.wait_ge(y_ready, t0 + n + 1)
                src = bank((t0 + n) % 2)
                if name in ("s5g", "lrug"):
                    if len(gated) >= 2:
                        act.wait_ge(y_taken, t0 + gated[-2] + 1)
                    nc.scalar.activation(sgt[len(gated) % 2], src, ACT.Sigmoid).then_inc(sem("silu_sigmoid"), 1)
                    gated.append(n)
                    continue
                if n in (2 * XT, 2 * XT + 2 * LT):
                    act.wait_ge(y_taken, t0 + n)
                if name == "s5x":
                    nc.scalar.activation(tile(s5x, x), src, ACT.Copy).then_inc(y_taken, 1)
                elif name == "lrux":
                    nc.scalar.activation(lrux[:, x * LPAD + CONV - 1:(x + 1) * LPAD], src, ACT.Copy).then_inc(y_taken, 1)
                else:
                    nc.scalar.activation(tile(gs if name == "gs" else gl, x), src, ACT.Sigmoid).then_inc(y_taken, 1)
            act.dma_start(s5b, t["s5_b"]).then_inc(sem("s5b_landed"), 16)
            for j in range(ST):
                v = V[j % 2]
                act.wait_ge(sem("s5_phase"), j + 1)
                nc.scalar.activation(v["S"], v["A"], ACT.Sin, scale=TWO_PI).then_inc(sem("s5_sine"), 1)
                nc.scalar.activation(v["C"], v["A"], ACT.Sin, scale=TWO_PI / 2).then_inc(sem("s5_sine"), 1)
            for x in range(XT):
                act.wait_ge(sem("s5_skipped"), x + 1)
                nc.scalar.activation(tile(s5x, x), tile(s5x, x), ACT.Gelu_apprx_tanh).then_inc(sem("gelu_ready"), 1)
            act.wait_ge(sem("gelu_ready"), XT)
            t0 = FIRST_TILE["glu"]
            for x in range(XT):
                act.wait_ge(y_ready, t0 + 2 * x + 1)
                if x >= 2:
                    act.wait_ge(sem("s5_gated"), x - 1)
                nc.scalar.activation(sgt[x % 2], bank((t0 + 2 * x) % 2), ACT.Sigmoid).then_inc(sem("glu_sigmoid"), 1)
            t0 = FIRST_TILE["lru"]
            act.wait_ge(y_taken, t0)
            for x in range(LT):
                act.wait_ge(y_ready, t0 + 2 * x + 1)
                nc.scalar.activation(rate[x], bank((t0 + 2 * x) % 2), ACT.Sigmoid, bias=col("b_a", x)).then_inc(y_taken, 1)
                act.wait_ge(y_ready, t0 + 2 * x + 2)
                if x >= 2:
                    act.wait_ge(sem("lru_in"), x - 1)
                nc.scalar.activation(i_t[x % 2], bank((t0 + 2 * x + 1) % 2), ACT.Sigmoid, bias=col("b_x", x)).then_inc(y_taken, 1)
                act.wait_ge(y_taken, t0 + 2 * x + 1)
                nc.scalar.activation(rate[x], rate[x], ACT.Tanh, scale=der[:, SP4 + x:SP4 + x + 1]).then_inc(sem("tanh_ready"), 1)
            for x in range(LT):
                act.wait_ge(sem("tanh_ready"), x + 1)
                if x >= 2:
                    act.wait_ge(sem("lru_b"), x - 1)
                nc.scalar.activation(root[x % 2], rate[x], ACT.Sqrt, scale=4.0).then_inc(sem("root_ready"), 1)
            act.wait_ge(y_ready, FIRST_TILE["lru"])
            act.dma_start(pT, t["p"]).then_inc(sem("p_loaded"), 16)
            take_out("w_out", 9)
            for x in range(DT):
                take_tile("ple", x, tile(gl, x))
            for x in range(DT):
                act.wait_ge(y_ready, FIRST_TILE["gate"] + x + 1)
                if x >= 2:
                    act.wait_ge(sem("gated"), x - 1)
                nc.scalar.activation(sgt[x % 2], bank((FIRST_TILE["gate"] + x) % 2), ACT.Sigmoid).then_inc(y_taken, 1)
            for x in range(DT):
                act.wait_ge(sem("final"), x + 1)
                act.dma_start(out[:, x * SEQ:(x + 1) * SEQ], tile(gl, x)).then_inc(sem("out_stored"), 16)
            act.wait_ge(sem("out_stored"), 16 * DT)

        @block.vector
        def _(dve):
            V_ = nc.vector
            steps = [0]

            def link(ins):
                steps[0] += 1
                ins.then_inc(sem("param_step"), 1)
                dve.wait_ge(sem("param_step"), steps[0])

            def normalise(n, g, x_of, out_of):
                dve.wait_ge(sem("rms_ready"), n + 1)
                V_.reciprocal(rstd[:, :], rstd[:, :]).then_inc(sem("rstd_ready"), 1)
                dve.wait_ge(sem("rstd_ready"), n + 1)
                for x in range(DT):
                    V_.scalar_tensor_tensor(out=out_of(x), in0=x_of(x), scalar=col(g[0], g[1] + x), in1=rstd[:, :],
                                            op0=ALU.mult, op1=ALU.mult).then_inc(sem("normed"), 1)

            def pre_norm(n, g):
                normalise(n, g, lambda x: tile(h, x), u_tile)

            def split_u_low(n, u_hi):
                for x in range(DT):
                    dve.wait_ge(sem("u_high"), n * DT + x + 1)
                    TT(u_lo_tile(x), u_tile(x), tile(u_hi, x).bitcast(F32), ALU.subtract).then_inc(sem("u_split"), 1)

            def post_norm(n, g, buf=wbuf):
                normalise(n, g, lambda x: tile(buf, x), lambda x: tile(buf, x))

            dve.wait_ge(sem("line_const_loaded"), 16)
            dve.wait_ge(sem("lines_ready"), 1)
            for half in range(2):
                at = slice(half * SEQ, (half + 1) * SEQ)
                V_.tensor_tensor(line_sb[:, at], bank(5 + half)[0:16, :], line_const[:, at], ALU.add
                                 ).then_inc(sem("lines_summed"), 1)
            dve.wait_ge(sem("cols_loaded"), 16)

            def cs(name, n):
                return cols[:, COLS[name]:COLS[name] + n]

            dve.wait_ge(sem("dt_exp"), 1)
            TT, TS, STT = V_.tensor_tensor, V_.tensor_scalar, V_.scalar_tensor_tensor
            TT(derived(X_, ST), cs("a_re", ST), derived(DT_, ST), ALU.mult).then_inc(sem("param_x"), 1)
            link(TT(derived(TH_, ST), cs("a_im", ST), derived(DT_, ST), ALU.mult))
            th = derived(TH_, ST)
            link(TS(tmp(3), th, 1.0 / TWO_PI, ROUND, ALU.mult, ALU.add))
            link(TS(tmp(3), tmp(3), -ROUND, None, ALU.add))
            for part in TURN_PARTS:
                link(STT(out=th, in0=tmp(3), scalar=-part, in1=th, op0=ALU.mult, op1=ALU.add))
            dve.wait_ge(sem("param_x"), 1)
            TS(th, th, PI_BELOW, -PI_BELOW, ALU.min, ALU.max).then_inc(sem("s5_angles"), 1)
            dve.wait_ge(sem("s5_angles"), 1)
            link(TS(tmp(4), th, 1.0 / TWO_PI, None, ALU.mult))
            link(TS(tmp(5), tmp(4), ROUND12, None, ALU.add))
            link(TS(derived(PHH, ST), tmp(5), -ROUND12, None, ALU.add))
            link(TT(derived(PHL, ST), tmp(4), derived(PHH, ST), ALU.subtract))
            dve.wait_ge(sem("s5_exp"), 4)
            t_, sin_, sh_ = tmp(0), tmp(1), tmp(2)
            link(TS(tmp(3), t_, -1.0, 1.0, ALU.mult, ALU.add))
            link(V_.reciprocal(tmp(3), tmp(3)))
            link(STT(out=t_, in0=t_, scalar=2.0, in1=tmp(3), op0=ALU.mult, op1=ALU.mult))
            link(TT(sh_, sh_, sh_, ALU.mult))
            link(TS(tmp(3), sh_, -2.0, 1.0, ALU.mult, ALU.add))
            link(TT(tmp(3), tmp(3), t_, ALU.mult))
            link(STT(out=tmp(3), in0=sh_, scalar=-2.0, in1=tmp(3), op0=ALU.mult, op1=ALU.add))
            link(TT(tmp(4), derived(MAG, ST), sin_, ALU.mult))
            re, im = cs("a_re", ST), cs("a_im", ST)
            link(TT(tmp(5), re, re, ALU.mult))
            link(TT(tmp(6), im, im, ALU.mult))
            link(TT(tmp(5), tmp(5), tmp(6), ALU.add))
            link(V_.reciprocal(tmp(5), tmp(5)))
            link(TT(tmp(6), tmp(3), re, ALU.mult))
            link(TT(tmp(7), tmp(4), im, ALU.mult))
            link(TT(tmp(6), tmp(6), tmp(7), ALU.add))
            link(TT(derived(ZRE, ST), tmp(6), tmp(5), ALU.mult))
            link(TT(tmp(6), tmp(4), re, ALU.mult))
            link(TT(tmp(7), tmp(3), im, ALU.mult))
            link(TT(tmp(6), tmp(6), tmp(7), ALU.subtract))
            link(TT(derived(ZIM, ST), tmp(6), tmp(5), ALU.mult))
            dve.wait_ge(sem("s5_c_loaded"), 16)
            cin = s5_in.rearrange("p (j r n) -> p j r n", j=ST, r=2)
            cout = s5c[:, :].rearrange("p (j r n) -> p j r n", j=ST, r=2)
            ca, cb = [a.rearrange("p (j n) -> p j n", j=ST) for a in s5_t]
            zre = derived(ZRE, ST).unsqueeze(2).to_broadcast([P, ST, 32])
            zim = derived(ZIM, ST).unsqueeze(2).to_broadcast([P, ST, 32])
            link(TT(ca, cin[:, :, 0, :], zre, ALU.mult))
            link(TT(cb, cin[:, :, 1, :], zim, ALU.mult))
            link(TT(cout[:, :, 0, :], ca, cb, ALU.subtract))
            link(TT(ca, cin[:, :, 0, :], zim, ALU.mult))
            link(TT(cb, cin[:, :, 1, :], zre, ALU.mult))
            link(TT(ca, ca, cb, ALU.add))
            link(TS(cout[:, :, 1, :], ca, -1.0, None, ALU.mult))
            lam, y, z, z2, acc = cs("lam", LT), tmp(10)[:, 0:LT], tmp(11)[:, 0:LT], tmp(12)[:, 0:LT], tmp(13)[:, 0:LT]
            STT(out=tmp(9)[:, 0:LT], in0=lam, scalar=-1.0, in1=lam, op0=ALU.mult, op1=ALU.max).then_inc(sem("lam_abs"), 1)
            dve.wait_ge(sem("lam_exp"), 1)
            link(TS(z, y, 2.0, None, ALU.add))
            link(V_.reciprocal(z, z))
            link(TT(z, z, y, ALU.mult))
            link(TT(z2, z, z, ALU.mult))
            link(TS(acc, z2, 1.0 / 17, 1.0 / 15, ALU.mult, ALU.add))
            for n in (13, 11, 9, 7, 5, 3, 1):
                link(TT(acc, acc, z2, ALU.mult))
                link(TS(acc, acc, 1.0 / n, None, ALU.add))
            link(TT(acc, acc, z, ALU.mult))
            link(TS(z2, lam, -1.0, 0.0, ALU.mult, ALU.max))
            link(STT(out=z2, in0=acc, scalar=2.0, in1=z2, op0=ALU.mult, op1=ALU.add))
            link(TS(der[:, SP4:SP4 + LT], z2, 4.0, None, ALU.mult))
            mu0 = der[:, MU0:MU0 + 6 * DT]
            link(TT(mu0, cs("mu_prev", 6 * DT), cs("mu_next", 6 * DT), ALU.add))
            TS(mu0, mu0, -1.0, 1.0, ALU.mult, ALU.add).then_inc(sem("mu_ready"), 1)
            link(TS(der[:, OMKA:OMKA + DT], cs("k_a", DT), -1.0, 1.0, ALU.mult, ALU.add))
            V_.tensor_copy(small[:, 40:41], der[:, OMKA:OMKA + 1]).then_inc(sem("s5c_ready"), 1)

            pre_norm(0, ("norm_g", 0))
            split_u_low(0, attn_u_hi)
            with dve.Fori(0, 4) as i:
                def biased(n):
                    half, qi, e = n // 8, n % 8 // 2, n % 2
                    head = (2 * i + e) if n < 8 else (i + 8 + 4 * e)
                    r = n % 4
                    dve.wait_ge(sem("s_ready"), i * 16 + (n + 1))
                    if n % 8 < 2:
                        dve.wait_ge(sem(f"bias_landed_{2 * half + e}"), i * 16 + 16)
                    if n >= 2:
                        dve.wait_ge(sem("p_ready"), i * 16 + (n - 1))
                    dve.nop(nofuse=True)
                    V_.tensor_tensor_reduce(s_sb[n % 2], bank(2 + n % 2), bias[2 * half + e][:, (3 - qi) * P:(3 - qi) * P + SEQ],
                                            1.0, -3.0e38, ALU.add, ALU.max, small[:, r:r + 1]).then_inc(sem("s_biased"), 1)
                    dve.wait_ge(sem("s_biased"), i * 16 + (n + 1))
                    TS(small[:, 4 + r:5 + r], small[:, r:r + 1], col("sink", head), -1.0, ALU.max, ALU.mult
                       ).then_inc(sem("max_ready"), 1)

                def denominator(n):
                    r = n % 4
                    dve.wait_ge(sem("sink_ready"), i * 16 + (n + 1))
                    TT(small[:, 20 + r:21 + r], small[:, 8 + r:9 + r], small[:, 12 + r:13 + r], ALU.add
                       ).then_inc(sem("den_ready"), 1)
                    dve.wait_ge(sem("den_ready"), i * 16 + (n + 1))
                    V_.reciprocal(small[:, 16 + r:17 + r], small[:, 20 + r:21 + r]).then_inc(sem("rden_ready"), 1)

                def turned(n):
                    dve.wait_ge(sem("pt_ready"), i * 16 + (n + 1))
                    if n >= 2:
                        dve.wait_ge(sem("o_ready"), i * 16 + (n - 1))
                    V_.tensor_copy(pt_sb[n % 2], bank(4 + n % 2)).then_inc(sem("pt_taken"), 1)

                for n in range(16):
                    biased(n)
                    if n >= 1:
                        denominator(n - 1)
                        turned(n - 1)
                denominator(15)
                turned(15)
            for x in range(DT):
                dve.wait_ge(sem("attn_high"), x + 1)
                TT(tile(attnT_lo, x), tile(attnT, x), tile(attnT_hi, x).bitcast(F32), ALU.subtract).then_inc(sem("attn_split"), 1)
            post_norm(1, ("norm_g", DT))
            def mlp(n, first_norm, g):
                pre_norm(first_norm, ("norm_g", g * DT))
                split_u_low(n + 1, mlp_u_hi)
                for half, part in enumerate("ab"):
                    t0, done = FIRST_TILE[f"up{n}{part}"], n * FT + half * FT // 2
                    with dve.Fori(0, 2) as i:
                        for j in range(8):
                            at = bass.ds(i * (8 * SEQ) + j * SEQ, SEQ)
                            dve.wait_ge(sem("relu_ready"), i * 8 + (done + j + 1))
                            TT(mid[:, at], bank((t0 + j) % 2), relu[j % 2], ALU.mult).then_inc(y_taken, 1)
                            dve.wait_ge(sem("mid_high"), i * 8 + (done + j + 1))
                            TT(mid_lo[:, at], mid[:, at], mid_hi[:, at].bitcast(F32), ALU.subtract).then_inc(sem("mid_split"), 1)
                t0 = FIRST_TILE[f"down{n}b"]
                for x in range(DT):
                    dve.wait_ge(y_ready, t0 + x + 1)
                    TT(tile(wbuf, x), tile(wbuf, x), bank((t0 + x) % 2), ALU.add).then_inc(y_taken, 1)
                post_norm(first_norm + 1, ("norm_g", (g + 1) * DT))

            mlp(0, 2, 2)
            pre_norm(4, ("norm_g", 4 * DT))
            dve.wait_ge(sem("normed"), 5 * DT)
            dve.wait_ge(sem("pads_zeroed"), 2)
            for m, c in enumerate([1, 4, 5, 0, 2, 3]):
                for x in range(DT):
                    dve.wait_ge(sem("mix_started"), m * DT + x + 1)
                    STT(out=tile(mixb[m % 2], x), in0=u_tile(x, -1), scalar=col("mu_prev", c * DT + x),
                        in1=tile(mixb[m % 2], x), op0=ALU.mult, op1=ALU.add).then_inc(sem("mix_half"), 1)
                for x in range(DT):
                    dve.wait_ge(sem("mix_half"), m * DT + x + 1)
                    STT(out=tile(mixb[m % 2], x), in0=u_tile(x, 1), scalar=col("mu_next", c * DT + x),
                        in1=tile(mixb[m % 2], x), op0=ALU.mult, op1=ALU.add).then_inc(sem("mixed"), 1)
            for x in range(DT):
                dve.wait_ge(sem("kk_summed"), x + 1)
                TS(tile(kk, x), bank(6 + x % 2), 1e-24, None, ALU.max).then_inc(sem("kk_clamped"), 1)
            for x in range(DT):
                dve.wait_ge(sem("kk_root"), x + 1)
                V_.reciprocal(tile(kk, x), tile(kk, x)).then_inc(sem("kk_inverse"), 1)
            for x in range(DT):
                dve.wait_ge(sem("kk_inverse"), x + 1)
                STT(out=tile(kk, x), in0=tile(kTr, x), scalar=col("k_k", x), in1=tile(kk, x),
                    op0=ALU.mult, op1=ALU.mult).then_inc(sem("kk_ready"), 1)

            dve.wait_ge(sem("kk_ready"), DT)
            def ends(a, d):
                return chunks(a)[:, :, CH - 1] if d == 0 else chunks(a)[:, :, 0]

            def features(n, F, ends_at, step):
                if step == 0:
                    for d in range(2):
                        r = F[d]
                        dve.wait_ge(sem("z_taken"), n(6, 1 + d))
                        src, dst = (r["al"], r["ro"]) if d == 0 else (r["al"][:, ::-1], r["ro"][:, ::-1])
                        V_.tensor_tensor_scan(dst, const("carry", 0, SEQ), src, 0.0, ALU.mult, ALU.add
                                              ).then_inc(sem("decay_scanned"), 1)
                    for d in range(2):
                        r = F[d]
                        dve.wait_ge(sem("decay_scanned"), n(2, d + 1))
                        TT(r["al"], r["ro"], r["al"], ALU.subtract).then_inc(sem("decay_summed"), 1)
                    return
                for d in range(2):
                    r = F[d]
                    dve.wait_ge(sem("z_taken"), n(6, 3 + d))
                    TS(r["kd"], r["be"], pair_col("k_a", n), der[:, bass.ds(n(1, OMKA), 1)], ALU.mult, ALU.add
                       ).then_inc(sem("kd_factor"), 1)
                for d in range(2):
                    r = F[d]
                    dve.wait_ge(sem("decays_ready"), n(6, 3 * (d + 1)))
                    V_.tensor_copy(ends_at[d], ends(r["ro"], d)).then_inc(sem("p_end_ready"), 1)
                    STT(out=r["al"], in0=r["al"], scalar=-1.0, in1=pair_tile(kk, n), op0=ALU.mult, op1=ALU.mult
                        ).then_inc(sem("al_ready"), 1)
                    dve.wait_ge(sem("p_end_ready"), n(2, d + 1))
                    TT(r["ro"], r["ro"], pair_tile(rT, n), ALU.mult).then_inc(sem("features_v"), 1)

            def out_centered(n, F):
                for d in range(2):
                    dve.wait_ge(sem("mean_ready"), n(2, d + 1))
                    TT(F[d]["al"], F[d]["al"], bank(4 * d + 3), ALU.subtract).then_inc(sem("o_centered"), 1)

            def out_bonus(n, F):
                for d in range(2):
                    dve.wait_ge(sem("bonus_ready"), n(2, d + 1))
                    TT(F[d]["ro"], pair_tile(vTr, n), bank(4 * d + 3), ALU.mult).then_inc(sem("bonus_done"), 1)

            def out_scaled(n, F):
                for d in range(2):
                    dve.wait_ge(sem("deviation"), n(2, d + 1))
                    V_.reciprocal(F[d]["ka"], F[d]["ka"]).then_inc(sem("deviation_inverse"), 1)
                for d in range(2):
                    dve.wait_ge(sem("deviation_inverse"), n(2, d + 1))
                    TT(F[d]["al"], F[d]["al"], F[d]["ka"], ALU.mult).then_inc(sem("o_scaled"), 1)
                for d in range(2):
                    dve.wait_ge(sem("o_scaled"), n(2, d + 1))
                    dve.wait_ge(sem("bonus_done"), n(2, d + 1))
                    STT(out=F[d]["al"], in0=F[d]["al"], scalar=pair_col("gn_w", n), in1=F[d]["ro"], op0=ALU.mult, op1=ALU.add
                        ).then_inc(sem("with_bonus"), 1)
                for d in range(2):
                    dve.wait_ge(sem("with_bonus"), n(2, d + 1))
                    STT(out=F[d]["al"], in0=F[d]["al"], scalar=pair_col("gn_b", n), in1=F[d]["g"], op0=ALU.add, op1=ALU.mult
                        ).then_inc(sem("dir_gated"), 1)
                dve.wait_ge(sem("dir_gated"), n(2, 2))
                TT(pair_tile(rT, n), F[0]["al"], F[1]["al"], ALU.add).then_inc(sem("pair_done"), 1)

            def pair(parity, n, prev, nxt):
                F, G = feats[parity], feats[1 - parity]

                def masked(ready, name, b, kind):
                    for d in range(2):
                        dve.wait_ge(sem("scores_ready"), n(15, ready + d))
                        TT(chunks(R[d][name]), chunks(bank(4 * d + b)), mask(kind, d), ALU.mult).then_inc(sem("masked_v"), 1)

                for d in range(2):
                    r = F[d]
                    dve.wait_ge(sem("features_p"), n(2, d + 1))
                    STT(out=r["kd"], in0=r["kd"], scalar=pair_col("r_k", n), in1=pair_tile(rT, n), op0=ALU.mult, op1=ALU.mult
                        ).then_inc(sem("bonus_terms"), 1)
                for d in range(2):
                    dve.wait_ge(sem("n_copied"), n(2, d + 1))
                    TT(chunks(R[d]["T"]), chunks(R[d]["X"]), mask("level_n", d), ALU.mult).then_inc(sem("n_masked"), 1)
                if prev:
                    out_centered(prev, G)
                masked(3, "Ma", 2, "strict")
                if prev:
                    out_bonus(prev, G)
                masked(7, "Mb", 0, "incl")
                if prev:
                    out_scaled(prev, G)
                masked(11, "Mr", 3, "incl")
                for l in range(1, LEVELS):
                    for d in range(2):
                        k = 2 * (l - 1) + d
                        dve.wait_ge(sem("dt_ready"), n(10, k + 1))
                        TT(R[d]["T"], R[d]["T"], bank(4 * d + 1), ALU.add).then_inc(sem("t_updated"), 1)
                    if nxt and 2 <= l <= 3:
                        features(nxt, G, p_end[1 - parity], l - 2)
                for j in range(NCH):
                    for d in range(2):
                        dve.wait_ge(sem("u_ready"), n(16, 2 * j + d + 1))
                        V_.tensor_copy(st_u[d], bank(4 * d + 1, CH)).then_inc(sem("u_taken"), 1)
                    if j == NCH - 1:
                        break
                    for d in range(2):
                        k = 2 * j + d
                        c = j if d == 0 else NCH - 1 - j
                        decay = p_end[parity][d][:, c:c + 1]
                        new = st_s[d][(j + 1) % 2]
                        dve.wait_ge(sem("s_ready_rw"), n(14, k + 1))
                        if j == 0:
                            TS(new, bank(4 * d + 2, CH), decay, None, ALU.mult).then_inc(sem("state_ready"), 1)
                        else:
                            dve.wait_ge(sem("state_decayed"), n(12, k - 1))
                            STT(out=new, in0=bank(4 * d + 2, CH), scalar=decay, in1=st_p[d],
                                op0=ALU.mult, op1=ALU.add).then_inc(sem("state_ready"), 1)
                    if j < NCH - 2:
                        for d in range(2):
                            k = 2 * j + d
                            c = j if d == 0 else NCH - 1 - j
                            nxt_c = c + 1 if d == 0 else c - 1
                            dve.wait_ge(sem("state_ready"), n(14, k + 1))
                            TS(st_p[d], st_s[d][(j + 1) % 2], p_end[parity][d][:, nxt_c:nxt_c + 1], None, ALU.mult
                               ).then_inc(sem("state_decayed"), 1)

            first, last = (lambda per, c=0: c), (lambda per, c=0: (DT - 1) * per + c)
            for step in range(2):
                features(first, feats[0], p_end[0], step)
            over_pairs(dve, pair)
            out_centered(last, feats[(DT - 1) % 2])
            out_bonus(last, feats[(DT - 1) % 2])
            out_scaled(last, feats[(DT - 1) % 2])
            post_norm(5, ("norm_g", 5 * DT), kTr)
            mlp(1, 6, 6)
            pre_norm(8, ("g_pre", 0))
            split_u_low(3, in_u_hi)
            t0 = FIRST_TILE["w_in"]
            gates = 0
            for n in list(range(XT, 2 * XT)) + list(range(2 * XT + LT, 2 * XT + 2 * LT)):
                dst = tile(s5g, n - XT) if n < 2 * XT else tile(lrug, n - 2 * XT - LT)
                dve.wait_ge(sem("silu_sigmoid"), gates + 1)
                if n in (XT, 2 * XT + LT):
                    dve.wait_ge(y_taken, t0 + n)
                TT(dst, bank((t0 + n) % 2), sgt[gates % 2], ALU.mult).then_inc(y_taken, 1)
                gates += 1

            def phase(j):
                v = V[j % 2]
                a, b = v["A"], v["B"]
                if j >= 2:
                    dve.wait_ge(sem("s5_turned"), 2 * (j - 1))
                else:
                    dve.wait_ge(y_taken, FIRST_TILE["glu"])
                iota = const("iota", 0, SEQ)
                link(TS(a, iota, der[:, PHH + j:PHH + j + 1], None, ALU.mult))
                link(TS(b, a, ROUND, -ROUND, ALU.add, ALU.add))
                link(TT(a, a, b, ALU.subtract))
                link(STT(out=a, in0=iota, scalar=der[:, PHL + j:PHL + j + 1], in1=a, op0=ALU.mult, op1=ALU.add))
                link(TS(b, a, ROUND, -ROUND, ALU.add, ALU.add))
                TT(a, a, b, ALU.subtract).then_inc(sem("s5_phase"), 1)

            phase(0)
            for j in range(ST):
                v = V[j % 2]
                if j + 1 < ST:
                    phase(j + 1) if False else None
                dve.wait_ge(sem("s5_sine"), 2 * (j + 1))
                link(TT(v["C"], v["C"], v["C"], ALU.mult))
                link(TS(v["C"], v["C"], -2.0, 1.0, ALU.mult, ALU.add))
                dve.wait_ge(sem("s5_in"), 2 * (j + 1))
                br, bi = bank(2 + 2 * (j % 2)), bank(3 + 2 * (j % 2))
                TT(v["v1"], br, v["C"], ALU.mult).then_inc(sem("s5_in_taken"), 1)
                TT(v["v2"], bi, v["S"], ALU.mult).then_inc(sem("s5_in_taken"), 1)
                TT(v["v3"], bi, v["C"], ALU.mult).then_inc(sem("s5_in_taken"), 1)
                TT(v["v4"], br, v["S"], ALU.mult).then_inc(sem("s5_in_taken"), 1)
                mag = der[:, MAG + j:MAG + j + 1].to_broadcast([P, SEQ])
                dve.wait_ge(sem("s5_back"), 2 * j + 1)
                V_.tensor_tensor_scan(v["A"], mag, v["v1"], 0.0, ALU.mult, ALU.add).then_inc(sem("s5_scanned"), 1)
                dve.wait_ge(sem("s5_back"), 2 * j + 2)
                V_.tensor_tensor_scan(v["B"], mag, v["v3"], 0.0, ALU.mult, ALU.add).then_inc(sem("s5_scanned"), 1)
                if j + 1 < ST:
                    phase(j + 1)
                if j % 4 == 3:
                    m = j // 4
                    dve.wait_ge(sem("s5_out"), j + 1)
                    STT(out=tile(s5x, m), in0=tile(s5x, m), scalar=col("s5_d", m), in1=bank(6 + m % 2),
                        op0=ALU.mult, op1=ALU.add).then_inc(sem("s5_skipped"), 1)
            t0 = FIRST_TILE["glu"]
            for x in range(XT):
                dve.wait_ge(y_ready, t0 + 2 * x + 2)
                dve.wait_ge(sem("glu_sigmoid"), x + 1)
                TT(sgt[x % 2], bank((t0 + 2 * x + 1) % 2), sgt[x % 2], ALU.mult).then_inc(y_taken, 2)
                dve.wait_ge(y_taken, t0 + 2 * x + 2)
                TT(tile(s5g, x), tile(s5g, x), sgt[x % 2], ALU.mult).then_inc(sem("s5_gated"), 1)
            t0 = FIRST_TILE["w_bs"]
            for x in range(DT):
                dve.wait_ge(y_ready, t0 + x + 1)
                TT(tile(gs, x), tile(gs, x), bank((t0 + x) % 2), ALU.mult).then_inc(y_taken, 1)
            dve.wait_ge(sem("conv_zeroed"), 1)
            dve.wait_ge(y_ready, FIRST_TILE["w_bs"])
            for x in range(LT):
                def tap(n):
                    return lrux[:, x * LPAD + n:x * LPAD + n + SEQ]
                link(TS(conv[x], tap(0), col("conv_w", x), col("conv_b", x), ALU.mult, ALU.add))
                for n in range(1, CONV):
                    ins = STT(out=conv[x], in0=tap(n), scalar=col("conv_w", n * LT + x), in1=conv[x], op0=ALU.mult, op1=ALU.add)
                    if n < CONV - 1:
                        link(ins)
                    else:
                        ins.then_inc(sem("conv_ready"), 1)
            for x in range(LT):
                dve.wait_ge(sem("tanh_ready"), x + 1)
                a, b = fa[x % 2], fb[x % 2]
                link(TS(b, rate[x], 1.0, None, ALU.add))
                link(V_.reciprocal(b, b))
                link(TS(a, rate[x], -1.0, 1.0, ALU.mult, ALU.add))
                link(TT(a, a, b, ALU.mult))
                dve.wait_ge(sem("root_ready"), x + 1)
                link(TT(b, b, root[x % 2], ALU.mult))
                dve.wait_ge(sem("lru_in"), x + 1)
                TT(b, b, conv[x], ALU.mult).then_inc(sem("lru_b"), 1)
                dve.wait_ge(sem("lru_b"), x + 1)
                link(V_.tensor_tensor_scan(rate[x], a, b, 0.0, ALU.mult, ALU.add))
                TT(tile(lrug, x), tile(lrug, x), rate[x], ALU.mult).then_inc(sem("lru_gated"), 1)
            t0 = FIRST_TILE["w_bl"]
            for x in range(DT):
                dve.wait_ge(y_ready, t0 + x + 1)
                TT(tile(gl, x), tile(gl, x), bank((t0 + x) % 2), ALU.mult).then_inc(y_taken, 1)
            post_norm(9, ("g_post", 0))
            t0 = FIRST_TILE["gate"]
            for x in range(DT):
                dve.wait_ge(y_taken, t0 + x + 1)
                TT(tile(gl, x), tile(gl, x), sgt[x % 2], ALU.mult).then_inc(sem("gated"), 1)

        @block.gpsimd
        def _(pool):
            G = nc.gpsimd
            up = u[:, :].rearrange("p (t n) -> p t n", t=DT)
            G.memset(up[:, :, 0:1], 0.0).then_inc(sem("pads_zeroed"), 1)
            G.memset(up[:, :, PAD - 1:PAD], 0.0).then_inc(sem("pads_zeroed"), 1)
            G.memset(small[:, 48:49], 0.0).then_inc(sem("ot_taken"), 1)

            def split_low(b, i=0, step=0):
                slot = slice(b % RING * BLOCK, (b % RING + 1) * BLOCK)
                pool.wait_ge(sem("weights_high"), i * step + SPLIT_COUNT[b])
                G.tensor_tensor(ring_lo[:, slot], ring[:, slot], ring_hi[:, slot].bitcast(F32), ALU.subtract
                                ).then_inc(sem("weights_split"), 1)

            def split_stream(first, end):
                assert (end - first) % RING == 0
                with pool.Fori(0, (end - first) // RING) as i:
                    for j in range(RING):
                        split_low(first + j, i, RING)

            def add_out(n, buf=wbuf):
                for x in range(DT):
                    pool.wait_ge(sem("normed"), n * DT + x + 1)
                    G.tensor_tensor(tile(h, x), tile(h, x), tile(buf, x), ALU.add).then_inc(sem("h_ready"), 1)

            for b in range(FIRST_BLOCK["attn_out"] + AHEAD):
                split_low(b)
            with pool.Fori(0, 4) as i:
                pool.wait_ge(y_taken, FIRST_TILE["attn_out"])
                pool.wait_ge(sem("ot_taken"), i * 8 + 1)
                G.tensor_copy(k_st, kT[:, bass.ts(i, SEQ)]).then_inc(sem("k_staged"), 1)
                for half in range(2):
                    by_block = qT[:, bass.ds(i * SEQ + half * 4 * SEQ, SEQ)].rearrange("p (b s) -> p b s", s=P)
                    G.tensor_copy(q_st[half].rearrange("p (b s) -> p b s", s=P)[:, :, ::-1], by_block).then_inc(sem("q_staged"), 1)
            for b in range(FIRST_BLOCK["attn_out"] + AHEAD, FIRST_BLOCK["up0a"]):
                split_low(b)
            add_out(1)
            split_stream(FIRST_BLOCK["up0a"], FIRST_BLOCK["lora_w"])
            add_out(3)
            pool.wait_ge(y_taken, FIRST_TILE["o"])
            pool.wait_ge(sem("kk_ready"), DT)

            def stage_v(n):
                G.tensor_copy(v_st, pair_tile(vTr, n)).then_inc(sem("v_staged"), 1)

            def features(n, F, step):
                for d in range(2):
                    r = F[d]
                    if step == 0:
                        pool.wait_ge(sem("kd_factor"), n(2, d + 1))
                        pool.nop(nofuse=True)
                        G.tensor_tensor(r["kd"], r["kd"], pair_tile(kTr, n), ALU.mult).then_inc(sem("kd_ready"), 1)
                        G.tensor_tensor(r["be"], r["be"], pair_tile(kk, n), ALU.mult).then_inc(sem("rate_kk"), 1)
                    else:
                        pool.wait_ge(sem("decays_ready"), n(6, 3 * (d + 1)))
                        pool.wait_ge(sem("rate_kk"), n(2, d + 1))
                        G.tensor_tensor(r["be"], r["be"], r["ka"], ALU.mult).then_inc(sem("be_ready"), 1)
                        pool.wait_ge(sem("be_ready"), n(2, d + 1))
                        pool.wait_ge(sem("kd_ready"), n(2, d + 1))
                        G.tensor_tensor(r["ka"], r["ka"], r["kd"], ALU.mult).then_inc(sem("features_p"), 1)

            def pair(parity, n, prev, nxt):
                def level_mask(l, d):
                    G.tensor_tensor(chunks(R[d]["LM"]), chunks(R[d]["L"]), mask("level", d * LEVELS + l), ALU.mult
                                    ).then_inc(sem("level_masked"), 1)

                eye = const("eye", 0, CH).unsqueeze(1).to_broadcast([P, NCH, CH])
                for d in range(2):
                    pool.wait_ge(sem("n_masked"), n(2, d + 1))
                    G.tensor_tensor(chunks(R[d]["T"]), chunks(R[d]["T"]), eye, ALU.add).then_inc(sem("t_started"), 1)
                for d in range(2):
                    pool.wait_ge(sem("l_copied"), n(2, d + 1))
                    level_mask(1, d)
                for d in range(2):
                    G.tensor_tensor(chunks(R[d]["TT"]), chunks(R[d]["L"]), mask("level", d * LEVELS), ALU.mult
                                    ).then_inc(sem("tt_masked"), 1)
                for d in range(2):
                    pool.wait_ge(sem("tt_masked"), n(2, d + 1))
                    G.tensor_tensor(chunks(R[d]["TT"]), chunks(R[d]["TT"]), eye, ALU.add).then_inc(sem("tt_started"), 1)
                if nxt:
                    pool.wait_ge(sem("scores_ready"), n(15, 15))
                    pool.nop(nofuse=True)
                    stage_v(nxt)
                for l in range(2, LEVELS):
                    for d in range(2):
                        pool.wait_ge(sem("x_ready"), n(10, 2 * (l - 2) + d + 1))
                        level_mask(l, d)
                    if nxt and l >= 4:
                        features(nxt, feats[1 - parity], l - 4)

            first = lambda per, c=0: c
            stage_v(first)
            for step in range(2):
                features(first, feats[0], step)
            over_pairs(pool, pair)
            add_out(5, kTr)
            split_stream(FIRST_BLOCK["up1a"], FIRST_BLOCK["w_in"])
            add_out(7)
            split_stream(FIRST_BLOCK["w_in"], FIRST_BLOCK["glu"])

            pool.wait_ge(sem("rms_ready"), 9)
            pool.wait_ge(y_ready, FIRST_TILE["w_in"])
            G.memset(lrux.rearrange("p (t n) -> p t n", t=LT)[:, :, 0:CONV - 1], 0.0).then_inc(sem("conv_zeroed"), 1)
            for j in range(ST):
                v = V[j % 2]
                pool.wait_ge(sem("s5_in_taken"), 4 * j + 2)
                G.tensor_tensor(v["v1"], v["v1"], v["v2"], ALU.add).then_inc(sem("s5_back"), 1)
                pool.wait_ge(sem("s5_in_taken"), 4 * j + 4)
                G.tensor_tensor(v["v3"], v["v3"], v["v4"], ALU.subtract).then_inc(sem("s5_back"), 1)
                pool.wait_ge(sem("s5_scanned"), 2 * (j + 1))
                G.tensor_tensor(v["v1"], v["A"], v["C"], ALU.mult).then_inc(sem("s5_part"), 1)
                G.tensor_tensor(v["v2"], v["B"], v["S"], ALU.mult).then_inc(sem("s5_part"), 1)
                G.tensor_tensor(v["v3"], v["B"], v["C"], ALU.mult).then_inc(sem("s5_part"), 1)
                G.tensor_tensor(v["v4"], v["A"], v["S"], ALU.mult).then_inc(sem("s5_part"), 1)
                pool.wait_ge(sem("s5_part"), 4 * j + 2)
                G.tensor_tensor(v["v1"], v["v1"], v["v2"], ALU.subtract).then_inc(sem("s5_turned"), 1)
                pool.wait_ge(sem("s5_part"), 4 * j + 4)
                G.tensor_tensor(v["v3"], v["v3"], v["v4"], ALU.add).then_inc(sem("s5_turned"), 1)
            for x in range(LT):
                pool.wait_ge(y_taken, FIRST_TILE["lru"] + 2 * x + 2)
                G.tensor_tensor(conv[x], conv[x], i_t[x % 2], ALU.mult).then_inc(sem("lru_in"), 1)
            for x in range(DT):
                pool.wait_ge(y_taken, FIRST_TILE["w_bl"] + x + 1)
                G.tensor_tensor(tile(gs, x), tile(gs, x), tile(gl, x), ALU.add).then_inc(sem("merged"), 1)
            add_out(9)
            for x in range(DT):
                pool.wait_ge(sem("gated"), x + 1)
                G.tensor_tensor(tile(gl, x), tile(gl, x), tile(h, x), ALU.add).then_inc(sem("final"), 1)


def units(w):
    k, n = w.shape
    return w.reshape(k // P, P, n // P, P).transpose(2, 0, 1, 3)


def columns(a):
    return np.ascontiguousarray(a.reshape(-1, P).T)


def tiles(a):
    return np.ascontiguousarray(a.reshape(-1, P, a.shape[1]).transpose(1, 0, 2).reshape(P, -1))


def lay_out(**inputs):
    a = {n: np.asarray(v) for n, v in inputs.items()}
    zeros = np.zeros
    wi, wo = a["attn_w_in"][0], a["attn_w_out"][0]
    na = 8 * HEAD
    order = np.concatenate([np.arange(HEAD) + HEAD * hd for pair in range(4) for hd in (pair, pair + 4)])
    qk = np.concatenate([wi[:, 0:na], wi[:, 3 * na:4 * na][:, order], wi[:, na:2 * na], wi[:, 4 * na:4 * na + P]], axis=1)
    v = np.concatenate([wi[:, 2 * na:3 * na], wi[:, 4 * na + P:]], axis=1)
    wo = np.concatenate([wo[0:na], wo[na:][order]])
    both = lambda w: np.concatenate([w[0, 0], w[0, 1]], axis=1)
    glu = a["w_glu_2"][0]
    glu = np.concatenate([glu[:, o + x * P:o + (x + 1) * P] for x in range(XT) for o in (S5W, 0)], axis=1)
    lru = np.stack([w[0, n] for n in range(LT) for w in (a["lru_w_a_2"], a["lru_w_x_2"])])[:, None]
    w_in = units(a["w_in_2"][0])
    parts = {"qk": units(qk), "v": units(v), "attn_out": units(wo),
             "lora_w": units(both(a["rk_w1"])), "lora_a": units(both(a["rk_a1"])), "lora_g": units(both(a["rk_g1"])),
             "r": units(a["rk_w_r"][0]), "k": units(a["rk_w_k"][0]), "rv": units(a["rk_w_v"][0]), "o": units(a["rk_w_o"][0]),
             "w_in": w_in[0:40], "w_in_end": w_in[40:], "glu": units(glu), "w_bs": units(a["w_bs_2"][0]), "lru": lru,
             "w_bl": units(a["w_bl_2"][0]), "w_out": units(a["w_out_2"][0]), "ple": units(a["w_ple_2"][0]),
             "gate": units(a["w_ple_gate_2"][0])}
    half = FF // 2
    for n in range(2):
        for part, at in (("a", slice(0, half)), ("b", slice(half, FF))):
            parts[f"up{n}{part}"], parts[f"down{n}{part}"] = units(a["mlp_w1"][n][:, at]), units(a["mlp_w2"][n][at])
    wall = zeros((NBLOCKS, P, UPB, P), np.float32)
    for name, n, k in DENSE:
        w = parts[name].reshape(n * k, P, P)
        for x in range(0, n * k, UPB):
            some = w[x:x + UPB]
            wall[FIRST_BLOCK[name] + x // UPB][:, 0:len(some)] = some.transpose(1, 0, 2)
    lora2 = zeros((DT, P, 6, P), np.float32)
    for d in range(2):
        half = slice(64 * d, 64 * d + 64)
        lora2[:, half, d] = a["rk_w2"][0, d].reshape(64, DT, P).transpose(1, 0, 2)
        lora2[:, half, 2 + d] = a["rk_a2"][0, d].reshape(64, DT, P).transpose(1, 0, 2)
        lora2[:, :, 4 + d] = a["rk_g2"][0, d].reshape(P, DT, P).transpose(1, 0, 2)
    sink = np.full(16, NEG, np.float32)
    sink[8:] = a["attn_sink"][0]
    fields = {"norm_g": a["norm_g"], "mu_prev": a["rk_mu_prev"], "mu_next": a["rk_mu_next"], "k_k": a["rk_k_k"],
              "k_a": a["rk_k_a"], "r_k": a["rk_r_k"], "gn_w": a["rk_gn_w"], "gn_b": a["rk_gn_b"], "w0": a["rk_w0"],
              "a0": a["rk_a0"], "g_pre": a["g_pre_2"], "g_post": a["g_post_2"], "a_re": a["s5_a_re_2"],
              "a_im": a["s5_a_im_2"], "log_dt": np.repeat(a["s5_log_dt_2"][0], S5N), "s5_d": a["s5_d_2"],
              "conv_w": a["conv_w_2"], "conv_b": a["conv_b_2"], "b_a": a["lru_b_a_2"], "b_x": a["lru_b_x_2"],
              "lam": a["lru_lambda_2"]}
    cols = np.zeros((P, NCOLS), np.float32)
    for name, value in fields.items():
        c = columns(value)
        cols[:, COLS[name]:COLS[name] + c.shape[1]] = c
    cols[:, COLS["sink"]:COLS["sink"] + 16] = sink
    s5_b = zeros((P, ST, 2, P), np.float32)
    s5_c = zeros((P, ST, 2, 32), np.float32)
    for g in range(S5G):
        j, n, rows = g // 2, S5N * (g % 2), g * 16 % P
        for x, (b, c) in enumerate([("s5_b_re_2", "s5_c_re_2"), ("s5_b_im_2", "s5_c_im_2")]):
            s5_b[rows:rows + 16, j, x, n:n + S5N] = a[b][0, g].T
            s5_c[n:n + S5N, j, x, 16 * (g % 2):16 * (g % 2) + 16] = a[c][0, g].T
    onehot, lines = bias_constants()
    return {"x": tiles(a["x"][0].T), "wall": wall.reshape(NBLOCKS, P, BLOCK), "lora2": lora2.reshape(DT, P, 6 * P),
            "cols": cols, "consts": constants(), "rel_table": a["rel_table"], "onehot": onehot, "lines": lines,
            "s5_b": s5_b.reshape(P, -1), "s5_c": s5_c.reshape(P, -1), "p": tiles(a["p_2"][0, 0].T)}


def kernel(**inputs):
    import concourse.bacc as bacc
    from concourse.bass_utils import run_bass_kernel_spmd

    nc = bacc.Bacc("TRN2", target_bir_lowering=False, num_devices=1)
    arrays = {f"in_{n}": v for n, v in lay_out(**inputs).items()}
    t = {n[3:]: nc.dram_tensor(n, v.shape, F32, kind="ExternalInput").ap() for n, v in arrays.items()}
    out = nc.dram_tensor("out", (P, DT * SEQ), F32, kind="ExternalOutput").ap()
    program(nc, t, out)
    got = run_bass_kernel_spmd(nc, [arrays], core_ids=[0]).results[0]["out"]
    return np.ascontiguousarray(got.reshape(P, DT, SEQ).transpose(2, 1, 0)).reshape(1, SEQ, D)
```

```python
from contextlib import ExitStack

import numpy as np

import concourse.bass as bass
from concourse import mybir

P = 128
SEQ = 512
D = 1024
DT = D // P
FF = 4 * D
FT = FF // P
HEAD = 64
NORM_EPS = 1e-6
GN_EPS = 64e-5
NEG = -1e30
ARENA = 30800
UPB = 8
RING = 4
AHEAD = 2
BLOCK = UPB * P
CH = 64
NCH = SEQ // CH
LEVELS = 6
S5W, S5G, S5N = 512, 32, 64
ST = S5G * S5N // P
XT = S5W // P
LRUW = 1280
LT = LRUW // P
CONV = 4
PLE = 256
TWO_PI = 6.283185
PI_BELOW = 3.1415925
ROUND = 1.5 * 2.0 ** 23
ROUND12 = 1.5 * 2.0 ** 11
TURN_PARTS = [6.28125, 0.0019350051879882812, 3.01991598196e-07]
DECAY = float(np.exp(-0.5))
SINK_W = 3 * P + SEQ
PAD = SEQ + 2
LPAD = SEQ + CONV - 1

F32 = mybir.dt.float32
F32R = mybir.dt.float32r
ALU = mybir.AluOpType
ACT = mybir.ActivationFunctionType
AX = mybir.AxisListType

DENSE = [
    ("qk", 13, DT), ("v", 5, DT), ("attn_out", DT, DT),
    ("up0a", FT // 2, DT), ("down0a", DT, FT // 2), ("up0b", FT // 2, DT), ("down0b", DT, FT // 2),
    ("lora_w", 1, DT), ("lora_a", 1, DT), ("lora_g", 2, DT),
    ("r", DT, DT), ("k", DT, DT), ("rv", DT, DT), ("o", DT, DT),
    ("up1a", FT // 2, DT), ("down1a", DT, FT // 2), ("up1b", FT // 2, DT), ("down1b", DT, FT // 2),
    ("w_in", 40, DT), ("w_in_end", 2 * XT + 2 * LT + 2 * DT - 40, DT), ("glu", 2 * XT, XT), ("w_bs", DT, XT),
    ("lru", 2 * LT, 1), ("w_bl", DT, LT), ("w_out", DT, DT), ("ple", DT, PLE // P), ("gate", DT, DT),
]


SPLIT = {"qk", "v", "attn_out", "w_in", "w_in_end", "up0a", "down0a", "up0b", "down0b", "up1a", "down1a", "up1b", "down1b"}


def plan():
    first_block, first_tile, last_tile, split_count = {}, {}, [], []
    tile = split = 0
    for name, n, k in DENSE:
        first_block[name], first_tile[name] = len(last_tile), tile
        units = n * k
        for b in range(-(-units // UPB)):
            last = min(units, (b + 1) * UPB) - 1
            last_tile.append(tile + last // k + 1)
            split += name in SPLIT
            split_count.append(split)
        tile += n
    return first_block, first_tile, last_tile, split_count


FIRST_BLOCK, FIRST_TILE, LAST_TILE, SPLIT_COUNT = plan()
SHAPE = {name: (n, k) for name, n, k in DENSE}
NBLOCKS = len(LAST_TILE)

COLS = {}
_at = 0
for _name, _n in [("norm_g", 8 * DT), ("mu_prev", 6 * DT), ("mu_next", 6 * DT), ("k_k", DT), ("k_a", DT),
                  ("r_k", DT), ("gn_w", DT), ("gn_b", DT), ("w0", 2 * DT), ("a0", 2 * DT), ("g_pre", DT),
                  ("g_post", DT), ("a_re", ST), ("a_im", ST), ("log_dt", ST), ("s5_d", XT),
                  ("conv_w", CONV * LT), ("conv_b", LT), ("b_a", LT), ("b_x", LT), ("lam", LT),
                  ("sink", 16)]:
    COLS[_name] = _at
    _at += _n
NCOLS = _at

CONSTS = {}
_at = 0
for _name, _n in [("mean", P), ("head_sum", P), ("head_mean", P), ("ident", P), ("iota", SEQ), ("carry", SEQ),
                  ("eye", CH), ("incl", 2 * CH), ("strict", 2 * CH), ("level_n", 2 * CH),
                  ("level", 2 * LEVELS * CH), ("eps", 4)]:
    CONSTS[_name] = _at
    _at += _n
NCONST = _at


def constants():
    c = np.zeros((P, NCONST), np.float32)

    def put(name, a):
        c[:, CONSTS[name]:CONSTS[name] + a.shape[1]] = a

    heads = np.kron(np.eye(P // HEAD), np.ones((HEAD, HEAD)))
    put("mean", np.full((P, P), 1.0 / D))
    put("head_sum", heads)
    put("head_mean", heads / HEAD)
    put("ident", np.eye(P))
    put("iota", np.broadcast_to(np.arange(SEQ, dtype=np.float32), (P, SEQ)))
    put("carry", np.broadcast_to(np.arange(SEQ) % CH != 0, (P, SEQ)))
    row, col = np.arange(CH)[:, None], np.arange(CH)[None, :]

    def both(m):
        return np.concatenate([m, m], axis=0)

    def level(rows_first, l):
        w = 1 << l
        same = (row // (2 * w)) == (col // (2 * w))
        low, high = (row, col) if rows_first else (col, row)
        return same & (low // w % 2 == 0) & (high // w % 2 == 1)

    put("eye", both(np.eye(CH)))
    put("incl", np.concatenate([both(row <= col), both(row >= col)], axis=1))
    put("strict", np.concatenate([both(row < col), both(row > col)], axis=1))
    put("level_n", np.concatenate([both(level(True, 0)), both(level(False, 0))], axis=1))
    put("level", np.concatenate([both(level(d == 1, l)) for d in range(2) for l in range(LEVELS)], axis=1))
    put("eps", np.broadcast_to(np.array([NORM_EPS, GN_EPS, 0.0, 1.0], np.float32), (P, 4)))
    return c


def bias_constants():
    d = np.arange(2 * SEQ) - (SEQ - 1)
    n = np.abs(d)
    nf = np.maximum(n, 1).astype(np.float32)
    large = 8 + (np.log(nf / np.float32(8)) / np.float32(np.log(1024 / 8)) * np.float32(8)).astype(np.int32)
    bucket = np.where(d > 0, 16, 0) + np.where(n < 8, n, np.minimum(large, 15))
    onehot = np.zeros((32, 2 * SEQ), np.float32)
    onehot[bucket, np.arange(2 * SEQ)] = 1.0
    count = sum(((n % dil == 0) & (n // dil <= window // 2 // dil)).astype(np.int64)
                for window, dil in ((128, 1), (512, 4), (2048, 16)))
    line_a = np.where(count > 0, np.log(np.maximum(count, 1)), NEG)
    line_b = np.where(n <= 128, 0.0, NEG)
    lines = np.concatenate([np.broadcast_to(line_a, (8, 2 * SEQ)), np.broadcast_to(line_b, (8, 2 * SEQ))])
    return onehot, lines.astype(np.float32)




def program(nc, t, out):
    ctx = ExitStack()
    with ctx:
        def sb(name, width):
            return ctx.enter_context(nc.sbuf_tensor(name, [P, width], F32))

        sems = {}

        def sem(name):
            if name not in sems:
                sems[name] = ctx.enter_context(nc.semaphore(name))
            return sems[name]

        def rounded(name, buf, width, first=0, dtype=F32R):
            return nc.alloc_sbuf_tensor_at(name, [P, width], dtype, offset=nc.lookup_mloc(buf).addr + 4 * first)

        ring = sb("ring", RING * BLOCK)
        ring_lo = rounded("ring_lo", ring, RING * BLOCK)
        ring_hi = ctx.enter_context(nc.sbuf_tensor("ring_hi", [P, RING * BLOCK], F32R))
        h = sb("h", DT * SEQ)
        u = sb("u", DT * PAD)
        u_lo = rounded("u_lo", u, DT * PAD)
        cols = sb("cols", NCOLS)
        consts = sb("consts", NCONST)
        sq = sb("sq", 2 * SEQ)
        rstd = sb("rstd", SEQ)
        small = sb("small", 64)
        der = sb("der", 6 * DT + DT + 8 * ST + 2 * LT)
        s5c = sb("s5c", ST * 2 * 32)
        arena = sb("arena", ARENA)

        ps = ctx.enter_context(nc.psum_tensor("ps", [P, 8 * SEQ], F32))
        lines_dram = nc.dram_tensor("bias_lines", [16, 2 * SEQ], F32)

        top = [0]

        def take(width):
            a = arena[:, top[0]:top[0] + width]
            top[0] += width
            assert top[0] <= ARENA, top[0]
            return a

        def take_rounded(name, width):
            take(width)
            return rounded(name, arena, width, top[0] - width)

        def take_parts(name, width):
            value, low = take(width), rounded(name + "_lo", arena, width, top[0] - width)
            return value, low, take_rounded(name + "_hi", width)

        def bank(b, width=SEQ):
            return ps[:, b * SEQ:b * SEQ + width]

        def tile(buf, i):
            return buf[:, bass.ts(i, SEQ)]

        def u_tile(i, shift=0):
            return u[:, bass.ds(i * PAD + 1 + shift, SEQ)]

        def u_lo_tile(i):
            return u_lo[:, bass.ds(i * PAD + 1, SEQ)]

        def col(name, i=0):
            return cols[:, bass.ds(COLS[name] + i, 1)]

        def const(name, i=0, width=P):
            return consts[:, CONSTS[name] + i * width:CONSTS[name] + (i + 1) * width]

        def square_tile(n, x):
            return u_tile(x) if n % 2 else sq[:, x % 2 * SEQ:(x % 2 + 1) * SEQ]

        def of_head(a, e):
            return a[e * HEAD:(e + 1) * HEAD, :]

        def chunks(a):
            return a.rearrange("p (c s) -> p c s", c=NCH)

        def mask(name, i):
            return const(name, i, CH).unsqueeze(1).to_broadcast([P, NCH, CH])

        MU0, OMKA, DT_, X_, TH_, MAG, PHH, PHL, ZRE, ZIM = [
            0, 48, 56, 56 + ST, 56 + 2 * ST, 56 + 3 * ST, 56 + 4 * ST, 56 + 5 * ST, 56 + 6 * ST, 56 + 7 * ST]
        SP4, SP8 = 56 + 8 * ST, 56 + 8 * ST + LT

        def derived(at, n=1):
            return der[:, at:at + n]

        wbuf = take(DT * SEQ)
        stage0 = top[0]
        qT = take(DT * SEQ)
        kT = take(5 * SEQ)
        qkT = arena[:, stage0:top[0]]
        vtok = take(4 * 640)
        attnT = take(DT * SEQ)
        bias = [take(SINK_W) for _ in range(4)]
        q_st = [take(SEQ) for _ in range(2)]
        k_st = [take(SEQ) for _ in range(2)]
        v_pair = take(SEQ)
        s_sb = [take(SEQ) for _ in range(2)]
        p_sb = [take(SEQ) for _ in range(2)]
        pt_sb = [take(SEQ) for _ in range(2)]
        line_sb, line_const = attnT[0:16, 0:2 * SEQ], attnT[0:16, 2 * SEQ:4 * SEQ]
        rel_sb, onehot = attnT[0:32, 4 * SEQ:4 * SEQ + 16], attnT[0:32, 5 * SEQ:7 * SEQ]
        bias0 = stage0 + (DT + 5 + DT) * SEQ + 4 * 640
        attn_u_hi = take_rounded("attn_u_hi", DT * SEQ)
        k_win = [arena[:, top[0] - (n + 1) * SEQ:top[0] - n * SEQ] for n in range(2)]
        attnT_lo = rounded("attnT_lo", arena, DT * SEQ, bias0 - DT * SEQ)
        attnT_hi = rounded("attnT_hi", arena, DT * SEQ, top[0] - DT * SEQ)
        s5_in = arena[:, bias0:bias0 + ST * 64]
        s5_t = [arena[:, bias0 + ST * (64 + 32 * n):bias0 + ST * (96 + 32 * n)] for n in range(2)]
        tmp0 = bias0 + ST * 128
        top[0] = stage0
        mid, mid_lo, mid_hi = take_parts("mid", FT // 2 * SEQ)
        mlp_u_hi = take_rounded("mlp_u_hi", DT * SEQ)
        relu = [take(SEQ) for _ in range(2)]
        top[0] = stage0
        rT = wbuf
        kk = take(DT * SEQ)
        kTr = take(DT * SEQ)
        vTr = take(DT * SEQ)
        lo_w, lo_a = take(SEQ), take(SEQ)
        lo_g = [take(SEQ) for _ in range(2)]
        lora2 = take(6 * P)
        pair0 = top[0]
        mixb = [take(DT * SEQ) for _ in range(2)]
        top[0] = pair0
        spare = [u[:, n * SEQ:(n + 1) * SEQ] for n in range(DT)]
        ring_hi_values = rounded("ring_hi_values", ring_hi, RING * BLOCK, dtype=F32)
        spare += [b[:, n * SEQ:(n + 1) * SEQ] for b in (ring, ring_hi_values) for n in range(RING * BLOCK // SEQ)]
        spare += [take(SEQ) for _ in range((ARENA - top[0]) // SEQ - 1)] + [rstd[:, :]]
        FEATURES, SCORES = ["al", "ro", "ka", "be", "kd", "g"], ["L", "Ma", "Mb", "Mr", "T", "TT", "LM"]
        feats = [[{name: spare.pop(0) for name in FEATURES} for _ in range(2)] for _ in range(2)]
        R = [{name: spare.pop(0) for name in SCORES} for _ in range(2)]
        alone_a, alone_b = [[[spare.pop(0) for _ in range(2)] for _ in range(2)] for _ in range(2)]
        for d in range(2):
            R[d]["al_alone"] = R[d]["X_alone"] = alone_a[d]
            R[d]["ro_alone"] = R[d]["T_alone"] = alone_b[d]
            R[d]["N"] = R[d]["LM"]
        v_alone = [sq[:, e * SEQ:(e + 1) * SEQ] for e in range(2)]
        v_st = R[0]["TT"]
        w_alone, u_alone, *s_alone = [[[alone_b[d][e][:, k * CH:(k + 1) * CH] for e in range(2)] for d in range(2)]
                                      for k in range(4)]
        st_p = [take(CH) for _ in range(2)]
        p_end = [[take(NCH) for _ in range(2)] for _ in range(2)]

        def over_pairs(engine, body):
            def fixed(i):
                return lambda per, c=0: i * per + c

            body(0, fixed(0), None, fixed(1))
            with engine.Fori(0, (DT - 2) // 2) as r:
                for q in range(2):
                    prev, n, nxt = [lambda per, c=0, k=k: r * (2 * per) + (k * per + c) for k in (q, q + 1, q + 2)]
                    body(1 - q, n, prev, nxt)
            body((DT - 1) % 2, fixed(DT - 1), fixed(DT - 2), None)

        def pair_tile(buf, n):
            return buf[:, bass.ds(n(SEQ), SEQ)]

        def pair_col(name, n, d=0):
            return cols[:, bass.ds(n(1, COLS[name] + d * DT), 1)]
        top[0] = stage0
        in_u_hi = rounded("in_u_hi", arena, DT * SEQ)
        s5x = take(XT * SEQ)
        s5g = take(XT * SEQ)
        lrug = take(LT * SEQ)
        gs = take(DT * SEQ)
        gl = take(DT * SEQ)
        lrux = take(LT * LPAD)
        free0 = [take(SEQ) for _ in range((ARENA - top[0]) // SEQ)]
        sgt = free0[0:2]
        s5b = u[:, 0:2 * ST * P]
        free1 = [tile(wbuf, n) for n in range(DT)] + free0
        free1 += [ring_hi_values[:, n * SEQ:(n + 1) * SEQ] for n in range(RING * BLOCK // SEQ)]
        TURNS = [dict(zip(["A", "B", "S", "C"], free1[4 * n:])) for n in range(3)]
        PARTS = [dict(zip(["v1", "v2", "v3", "v4"], free1[12 + 4 * n:])) for n in range(2)]
        s5c_negated = free1[20][:, 0:ST * 32]
        conv = [lrux[:, x * LPAD + CONV - 1:(x + 1) * LPAD] for x in range(LT)]
        conv_sum = free0[2:4]
        lru_a = [u[:, n * SEQ:(n + 1) * SEQ] for n in range(DT)] + [tile(s5x, n) for n in range(2)]
        rate = [tile(wbuf, n) for n in range(DT)] + [tile(s5x, n) for n in range(2, 4)]
        i_t, root, fa, fb = free0[0:2], free0[2:4], free0[4:6], free0[6:8]
        pT = s5g[:, 0:2 * SEQ]

        def tmp(n):
            return arena[:, tmp0 + n * ST:tmp0 + (n + 1) * ST]

        y_ready, y_taken = sem("y_ready"), sem("y_taken")
        landed = [sem(f"weights_landed_{s}") for s in range(RING)]
        block = ctx.enter_context(nc.Block())

        @block.sync
        def _(sp):
            def stream(first, end):
                b = first
                while b < end:
                    step, m = None, 1
                    while b >= RING and b + RING * (m + 1) <= end:
                        now = [LAST_TILE[b + RING * m + j - RING] for j in range(RING)]
                        was = [LAST_TILE[b + RING * (m - 1) + j - RING] for j in range(RING)]
                        gaps = {x - y for x, y in zip(now, was)}
                        if len(gaps) != 1 or step not in (None, min(gaps)):
                            break
                        step, m = min(gaps), m + 1
                    if m >= 2:
                        with sp.Fori(0, m) as i:
                            for j in range(RING):
                                sp.wait_ge(y_ready, i * step + LAST_TILE[b + j - RING])
                                slot = (b + j) % RING
                                sp.dma_start(ring[:, slot * BLOCK:(slot + 1) * BLOCK],
                                             t["wall"][bass.ds(i * RING + b + j, 1)].rearrange("a p n -> (a p) n")
                                             ).then_inc(landed[slot], 16)
                        b += RING * m
                    else:
                        if b >= RING:
                            sp.wait_ge(y_ready, LAST_TILE[b - RING])
                        slot = b % RING
                        sp.dma_start(ring[:, slot * BLOCK:(slot + 1) * BLOCK], t["wall"][b]).then_inc(landed[slot], 16)
                        b += 1

            sp.dma_start(h[:, :], t["x"]).then_inc(sem("x_loaded"), 16)
            sp.dma_start(consts[:, :], t["consts"]).then_inc(sem("consts_loaded"), 16)
            sp.dma_start(cols[:, :], t["cols"]).then_inc(sem("cols_loaded"), 16)
            sp.dma_start(rel_sb, t["rel_table"]).then_inc(sem("rel_loaded"), 16)
            sp.dma_start(onehot, t["onehot"]).then_inc(sem("onehot_loaded"), 16)
            sp.dma_start(line_const, t["lines"]).then_inc(sem("line_const_loaded"), 16)
            sp.dma_start(s5_in, t["s5_c"]).then_inc(sem("s5_c_loaded"), 16)
            stream(0, FIRST_BLOCK["attn_out"] + RING)

            def load_bias(i, half):
                for e in range(2):
                    head = i * 2 + e if half == 0 else i + 8 + 4 * e
                    src = bass.AP(lines_dram, head * (2 * SEQ), [[1, P], [1, SINK_W]])
                    sp.dma_start(bias[2 * half + e], src).then_inc(sem(f"bias_landed_{2 * half + e}"), 16)

            sp.wait_ge(sem("lines_stored"), 16)
            sp.wait_ge(sem("s5c_ready"), 1)
            load_bias(0, 0)
            load_bias(0, 1)
            with sp.Fori(1, 4) as i:
                for half in range(2):
                    sp.wait_ge(sem("s_biased"), i * 16 + (8 * half - 8))
                    load_bias(i, half)
            stream(FIRST_BLOCK["attn_out"] + RING, FIRST_BLOCK["o"])

            def load_lora2(i):
                sp.dma_start(lora2, t["lora2"][bass.ds(i, 1)].rearrange("a p n -> (a p) n")
                             ).then_inc(sem("lora2_landed"), 16)

            sp.wait_ge(y_ready, FIRST_TILE["r"])
            load_lora2(0)
            with sp.Fori(1, DT) as i:
                sp.wait_ge(sem("z_ready"), i * 6)
                load_lora2(i)
            sp.wait_ge(sem("pair_done"), DT)
            stream(FIRST_BLOCK["o"], NBLOCKS)

        @block.tensor
        def _(pe):
            def dense(name, rhs, steps=1, rhs_ready=None, first=0, count=None):
                n, k = SHAPE[name]
                per = n // steps
                b0, t0 = FIRST_BLOCK[name], FIRST_TILE[name]

                def step(i):
                    for j in range(per):
                        if t0 + j >= 2:
                            pe.wait_ge(y_taken, i * per + (t0 + j - 1))
                        for x in range(k):
                            unit = j * k + x
                            b = b0 + unit // UPB
                            if unit % UPB == 0 or x == 0:
                                if name in SPLIT:
                                    pe.wait_ge(sem("weights_split"), i * (per * k // UPB) + SPLIT_COUNT[b])
                                else:
                                    rounds = per * k // UPB // RING if steps > 1 else 0
                                    pe.wait_ge(landed[b % RING], i * (16 * rounds) + 16 * (b // RING + 1))
                            if rhs_ready is not None:
                                rhs_ready(j, x)
                            at = (b % RING) * BLOCK + unit % UPB * P
                            if name in SPLIT:
                                high, low = rhs(x)
                                y, w_hi, w_lo = bank((t0 + j) % 2), ring_hi[:, at:at + P], ring_lo[:, at:at + P]
                                nc.tensor.matmul(y, w_hi, high, start=x == 0, stop=False)
                                nc.tensor.matmul(y, w_hi, low, start=False, stop=False)
                                mm = nc.tensor.matmul(y, w_lo, high, start=False, stop=x == k - 1)
                                continue
                            mm = nc.tensor.matmul(bank((t0 + j) % 2), ring[:, at:at + P], rhs(x),
                                                  start=x == 0, stop=x == k - 1)
                        mm.then_inc(y_ready, 1)

                if steps == 1:
                    step(0)
                else:
                    assert per % 2 == 0 and per * k % (UPB * RING) == 0
                    with pe.Fori(0, steps) as i:
                        step(i)

            def mean_square(n):
                for x in range(DT):
                    pe.wait_ge(sem("sq_ready"), DT * n + x + 1)
                    if x == 0 and n:
                        pe.wait_ge(sem("rms_ready"), n)
                    nc.tensor.matmul(bank(7), const("mean"), square_tile(n, x),
                                     start=x == 0, stop=x == DT - 1).then_inc(sem("sq_used"), 1)

            def split_tile(n):
                return lambda j, x: pe.wait_ge(sem("u_split"), DT * n + x + 1) if j == 0 else None

            pe.wait_ge(sem("rel_loaded"), 16)
            pe.wait_ge(sem("onehot_loaded"), 16)
            for half in range(2):
                mm = nc.tensor.matmul(bank(5 + half)[0:16, :], rel_sb, onehot[:, half * SEQ:(half + 1) * SEQ],
                                      start=True, stop=True)
            mm.then_inc(sem("lines_ready"), 1)

            pe.wait_ge(sem("consts_loaded"), 16)
            mean_square(0)
            dense("qk", lambda x: (tile(attn_u_hi, x), u_lo_tile(x)), rhs_ready=split_tile(0))
            t0, b0 = FIRST_TILE["v"], FIRST_BLOCK["qk"]
            for j in range(5):
                pe.wait_ge(y_taken, t0 + j - 1)
                first = SHAPE["qk"][0] * DT + j * DT
                b = b0 + first // UPB
                pe.wait_ge(sem("weights_split"), SPLIT_COUNT[b])
                for tok in range(4):
                    for x in range(DT):
                        at = (b % RING) * BLOCK + x * P
                        y = bank((t0 + j) % 2)[:, tok * P:(tok + 1) * P]
                        high = attn_u_hi[:, x * SEQ + tok * P:x * SEQ + (tok + 1) * P]
                        low = u_lo[:, x * PAD + 1 + tok * P:x * PAD + 1 + (tok + 1) * P]
                        w_hi, w_lo = ring_hi[:, at:at + P], ring_lo[:, at:at + P]
                        nc.tensor.matmul(y, high, w_hi, start=x == 0, stop=False)
                        nc.tensor.matmul(y, high, w_lo, start=False, stop=False)
                        mm = nc.tensor.matmul(y, low, w_hi, start=False, stop=x == DT - 1)
                mm.then_inc(y_ready, 1)
            pe.wait_ge(y_taken, FIRST_TILE["attn_out"])

            with pe.Fori(0, 4) as i:
                def place(n):
                    return n // 8, n % 8 // 2, n % 2

                def scores(n):
                    half, qi, e = place(n)
                    if n % 8 == 0:
                        pe.wait_ge(sem("q_staged"), i * 2 + (half + 1))
                        pe.wait_ge(sem("k_staged"), i + 1)
                    if n >= 4:
                        pe.wait_ge(sem("s_biased"), i * 16 + (n - 3))
                    keys = k_st[e] if half == 0 else k_win[e]
                    nc.tensor.matmul(bank(n % 4), q_st[half][:, qi * P:(qi + 1) * P], keys,
                                     start=True, stop=True).then_inc(sem("s_ready"), 1)

                def turn(n):
                    pe.wait_ge(sem("p_scaled"), i * 16 + (n + 1))
                    if n >= 2:
                        pe.wait_ge(sem("pt_taken"), i * 16 + (n - 1))
                    for x in range(4):
                        tr = nc.tensor.transpose(bank(4 + n % 2)[:, x * P:(x + 1) * P],
                                                 p_sb[n % 2][:, x * P:(x + 1) * P], const("ident"))
                    tr.then_inc(sem("pt_ready"), 1)

                def values(n):
                    half, qi, e = place(n)
                    pe.wait_ge(sem("pt_taken"), i * 16 + (n + 1))
                    if n == 0:
                        pe.wait_ge(sem("v_pair_staged"), i + 1)
                    for x in range(4):
                        at = x * 640 + 512 + e * HEAD
                        v = v_pair[:, x * P + e * HEAD:x * P + (e + 1) * HEAD] if half == 0 else vtok[:, at:at + HEAD]
                        mm = nc.tensor.matmul(bank(6 + half)[e * HEAD:(e + 1) * HEAD, qi * P:(qi + 1) * P], v,
                                              pt_sb[n % 2][:, x * P:(x + 1) * P], start=x == 0, stop=x == 3)
                    mm.then_inc(sem("o_ready"), 1)

                pe.wait_ge(sem("ot_taken"), i * 2 + 1)
                for n in range(3):
                    scores(n)
                for n in range(16):
                    if n + 3 < 16:
                        scores(n + 3)
                    turn(n)
                    if n >= 1:
                        values(n - 1)
                values(15)

            pe.wait_ge(sem("ot_taken"), 9)
            dense("attn_out", lambda x: (tile(attnT_hi, x), tile(attnT_lo, x)),
                  rhs_ready=lambda j, x: pe.wait_ge(sem("attn_split"), x + 1) if j == 0 else None)
            mean_square(1)
            def mlp(n, first_norm):
                mean_square(first_norm)
                for half, part in enumerate("ab"):
                    dense(f"up{n}{part}", lambda x: (tile(mlp_u_hi, x), u_lo_tile(x)), steps=2,
                          rhs_ready=split_tile(n + 1))
                    dense(f"down{n}{part}", lambda x: (tile(mid_hi, x), tile(mid_lo, x)), steps=4, rhs_ready=lambda j, x: (
                        pe.wait_ge(sem("mid_split"), FT * n + FT // 2 * half + x + 1) if j == 0 else None))
                mean_square(first_norm + 1)

            mlp(0, 2)
            mean_square(4)
            def head_norm(x):
                pe.wait_ge(sem("kk_squared"), x + 1)
                if x >= 2:
                    pe.wait_ge(sem("kk_clamped"), x - 1)
                nc.tensor.matmul(bank(6 + x % 2), const("head_sum"), sq[:, x % 2 * SEQ:(x % 2 + 1) * SEQ],
                                 start=True, stop=True).then_inc(sem("kk_summed"), 1)

            for m, name in enumerate(["lora_w", "lora_a", "lora_g", "r", "k", "rv"]):
                def mix_ready(j, x):
                    if j == 0:
                        pe.wait_ge(sem("mixed"), DT * m + x + 1)
                    elif name == "rv" and x == DT // 2:
                        head_norm(j - 1)

                dense(name, lambda x: tile(mixb[m % 2], x), rhs_ready=mix_ready)
            head_norm(DT - 1)
            pe.wait_ge(sem("kk_ready"), DT)
            pe.wait_ge(sem("alone_zeroed"), 10)

            def each(out, a, alone):
                pe.nop(nofuse=True)
                for c in range(NCH):
                    for e in range(2):
                        rows, at = slice(e * HEAD, (e + 1) * HEAD), slice(c * CH, (c + 1) * CH)
                        mm = nc.tensor.matmul(out[rows, at], a[:, at], alone[e][:, at], start=True, stop=True)
                return mm

            def each_turned(out, a):
                for at in range(0, SEQ, P):
                    mm = nc.tensor.transpose(out[:, at:at + P], a[:, at:at + P], const("ident"))
                return mm

            A, B, C, O = [[bank(4 * d + x) for d in range(2)] for x in range(4)]

            def hidden_out(n, step):
                if step == 0:
                    pe.wait_ge(sem("lora2_landed"), n(16, 16))
                else:
                    pe.wait_ge(sem("z_taken"), n(6, 2 * step))
                for d in range(2):
                    k = 2 * step + d
                    nc.tensor.matmul(O[d], lora2[:, k * P:(k + 1) * P], [lo_w, lo_w, lo_a, lo_a, lo_g[0], lo_g[1]][k],
                                     start=True, stop=True).then_inc(sem("z_ready"), 1)

            def out_means(n, F):
                for d in range(2):
                    pe.wait_ge(sem("o_copied"), n(2, d + 1))
                    nc.tensor.matmul(O[d], const("head_mean"), F[d]["al"], start=True, stop=True
                                     ).then_inc(sem("mean_ready"), 1)

            def out_bonus(n, F):
                for d in range(2):
                    pe.wait_ge(sem("o_centered"), n(2, d + 1))
                    pe.wait_ge(sem("bonus_terms"), n(2, d + 1))
                    nc.tensor.matmul(O[d], const("head_sum"), F[d]["kd"], start=True, stop=True
                                     ).then_inc(sem("bonus_ready"), 1)

            def out_variances(n, F):
                for d in range(2):
                    pe.wait_ge(sem("bonus_done"), n(2, d + 1))
                    pe.wait_ge(sem("o_squared"), n(2, d + 1))
                    nc.tensor.matmul(O[d], const("head_mean"), F[d]["be"], start=True, stop=True
                                     ).then_inc(sem("var_ready"), 1)

            def pair(parity, n, prev, nxt):
                F = feats[parity]
                for d in range(2):
                    pe.wait_ge(sem("spread"), n(4, d + 1))
                    pe.wait_ge(sem("features_p"), n(2, d + 1))
                    each(A[d], F[d]["be"], R[d]["al_alone"]).then_inc(sem("scores_ready"), 1)
                pe.wait_ge(sem("v_staged"), n(1, 1))
                each_turned(B[0], v_st).then_inc(sem("scores_ready"), 1)
                if prev:
                    out_means(prev, feats[1 - parity])
                for d in range(2):
                    each(C[d], F[d]["ka"], R[d]["al_alone"]).then_inc(sem("scores_ready"), 1)
                if prev:
                    out_bonus(prev, feats[1 - parity])
                for d in range(2):
                    pe.wait_ge(sem("n_copied"), n(2, d + 1))
                    if d == 0:
                        pe.wait_ge(sem("v_turned"), n(1, 1))
                    each_turned(B[d], R[d]["N"]).then_inc(sem("scores_ready"), 1)
                if prev:
                    out_variances(prev, feats[1 - parity])
                for d in range(2):
                    pe.wait_ge(sem("spread"), n(4, d + 3))
                    each(A[d], F[d]["be"], R[d]["ro_alone"]).then_inc(sem("scores_ready"), 1)
                for d in range(2):
                    if prev:
                        pe.wait_ge(sem("deviation"), prev(2, d + 1))
                    each(O[d], F[d]["ka"], R[d]["ro_alone"]).then_inc(sem("scores_ready"), 1)
                for d in range(2):
                    pe.wait_ge(sem("l_copied"), n(2, d + 1))
                    each_turned(B[d], F[d]["be"]).then_inc(sem("scores_ready"), 1)
                for d in range(2):
                    pe.wait_ge(sem("masked_v"), n(6, 1 + d))
                    each_turned(C[d], F[d]["ka"]).then_inc(sem("scores_ready"), 1)
                pe.wait_ge(sem("masked_v"), n(6, 4))
                for l in range(1, LEVELS):
                    for d in range(2):
                        k = 2 * (l - 1) + d
                        pe.wait_ge(sem("level_masked"), n(10, k + 1))
                        if l == 1:
                            pe.wait_ge(sem("t_alone"), n(2, d + 1))
                        else:
                            pe.wait_ge(sem("t_alone_updated"), n(8, k - 1))
                        each(A[d], R[d]["LM"], R[d]["T_alone"]).then_inc(sem("x_ready"), 1)
                    for d in range(2):
                        k = 2 * (l - 1) + d
                        pe.wait_ge(sem("x_taken"), n(10, k + 1))
                        if l == 1:
                            pe.wait_ge(sem("tt_started"), n(2, d + 1))
                            pe.wait_ge(sem("turned"), n(4, d + 1))
                        else:
                            pe.wait_ge(sem("tt_taken"), n(8, k - 1))
                        each(B[d], R[d]["TT"], R[d]["X_alone"]).then_inc(sem("dt_ready"), 1)
                    if l == LEVELS - 1:
                        break
                    for d in range(2):
                        pe.wait_ge(sem("t_updated"), n(10, 2 * (l - 1) + d + 1))
                        if l == 1:
                            pe.wait_ge(sem("turned"), n(4, d + 3))
                        each_turned(C[d], R[d]["T"]).then_inc(sem("tt_ready"), 1)
                        if d == (l == 2) and nxt and l <= 3:
                            if l == 1:
                                pe.wait_ge(sem("masked_v"), n(6, 6))
                            hidden_out(nxt, l - 1)
                if nxt:
                    pe.wait_ge(sem("z_taken"), nxt(6, 6))
                pe.wait_ge(sem("masked_v"), n(6, 6))
                for j in range(NCH):
                    for d in range(2):
                        k = 2 * j + d
                        c = j if d == 0 else NCH - 1 - j
                        at = slice(c * CH, (c + 1) * CH)
                        if j:
                            pe.wait_ge(sem("state_ready"), n(14, k - 1))
                        pe.nop(nofuse=True)
                        for e in range(2):
                            rows = slice(e * HEAD, (e + 1) * HEAD)
                            if j == 0:
                                mm = nc.tensor.matmul(A[d][rows, 0:CH], R[d]["Ma"][:, at], v_alone[e][:, at],
                                                      start=True, stop=True)
                            else:
                                mm = nc.tensor.matmul(A[d][rows, 0:CH], F[d]["al"][:, at], s_alone[j % 2][d][e],
                                                      start=False, stop=True)
                        mm.then_inc(sem("w_ready"), 1)
                    for d in range(2):
                        c = j if d == 0 else NCH - 1 - j
                        at = slice(c * CH, (c + 1) * CH)
                        for e in range(2):
                            rows = slice(e * HEAD, (e + 1) * HEAD)
                            if j < NCH - 1:
                                nc.tensor.matmul(C[d][rows, 0:CH], F[d]["ka"][:, at], v_alone[e][:, at],
                                                 start=True, stop=False)
                    for d in range(2):
                        k = 2 * j + d
                        c = j if d == 0 else NCH - 1 - j
                        at = slice(c * CH, (c + 1) * CH)
                        if j == 0:
                            pe.wait_ge(sem("t_updated"), n(10, 2 * (LEVELS - 2) + d + 1))
                        pe.wait_ge(sem("w_taken"), n(16, k + 1))
                        pe.nop(nofuse=True)
                        for e in range(2):
                            rows = slice(e * HEAD, (e + 1) * HEAD)
                            mm = nc.tensor.matmul(B[d][rows, 0:CH], R[d]["T"][:, at], w_alone[d][e], start=True, stop=True)
                        mm.then_inc(sem("u_ready"), 1)
                    for d in range(2):
                        c = j if d == 0 else NCH - 1 - j
                        at = slice(c * CH, (c + 1) * CH)
                        for e in range(2):
                            nc.tensor.matmul(O[d][e * HEAD:(e + 1) * HEAD, at], v_alone[e][:, at], R[d]["Mr"][:, at],
                                             start=True, stop=False)
                            if j:
                                nc.tensor.matmul(O[d][e * HEAD:(e + 1) * HEAD, at], s_alone[j % 2][d][e], F[d]["ro"][:, at],
                                                 start=False, stop=False)
                    for d in range(2):
                        k = 2 * j + d
                        c = j if d == 0 else NCH - 1 - j
                        at = slice(c * CH, (c + 1) * CH)
                        pe.wait_ge(sem("u_taken"), n(16, k + 1))
                        pe.nop(nofuse=True)
                        if j < NCH - 1:
                            for e in range(2):
                                rows = slice(e * HEAD, (e + 1) * HEAD)
                                mm = nc.tensor.matmul(C[d][rows, 0:CH], F[d]["be"][:, at], u_alone[d][e],
                                                      start=False, stop=True)
                            mm.then_inc(sem("s_ready_rw"), 1)
                        for e in range(2):
                            rows = slice(e * HEAD, (e + 1) * HEAD)
                            mm = nc.tensor.matmul(O[d][rows, at], u_alone[d][e], R[d]["Mb"][:, at],
                                                  start=False, stop=True)
                        mm.then_inc(sem("o_ready_rw"), 1)
                    if j < NCH - 1:
                        for d in range(2):
                            c = j + 1 if d == 0 else NCH - 2 - j
                            at = slice(c * CH, (c + 1) * CH)
                            for e in range(2):
                                nc.tensor.matmul(A[d][e * HEAD:(e + 1) * HEAD, 0:CH], R[d]["Ma"][:, at], v_alone[e][:, at],
                                                 start=True, stop=False)

            first, last = (lambda per, c=0: c), (lambda per, c=0: (DT - 1) * per + c)
            for step in range(3):
                hidden_out(first, step)
            pe.wait_ge(sem("z_taken"), 6)
            over_pairs(pe, pair)
            out_means(last, feats[(DT - 1) % 2])
            out_bonus(last, feats[(DT - 1) % 2])
            out_variances(last, feats[(DT - 1) % 2])
            pe.wait_ge(sem("pair_done"), DT)
            dense("o", lambda x: tile(rT, x))
            mean_square(5)
            mlp(1, 6)
            mean_square(8)
            dense("w_in", lambda x: (tile(in_u_hi, x), u_lo_tile(x)), steps=5, rhs_ready=split_tile(3))
            dense("w_in_end", lambda x: (tile(in_u_hi, x), u_lo_tile(x)))
            pe.wait_ge(sem("s5b_landed"), 16)
            pe.wait_ge(y_taken, FIRST_TILE["glu"])

            def s5_out(j):
                pe.wait_ge(sem("s5_part"), 4 * (j + 1))
                m, rows = j // 4, slice(j % 4 * 32, j % 4 * 32 + 32)
                if j % 4 == 0 and m >= 2:
                    pe.wait_ge(sem("s5_skipped"), m - 1)
                w_re, w_im = [s5c[:, j * 64 + x * 32:j * 64 + (x + 1) * 32] for x in range(2)]
                w_neg = s5c_negated[:, j * 32:(j + 1) * 32]
                for name, w in [("v1", w_re), ("v2", w_neg), ("v3", w_im), ("v4", w_im)]:
                    mm = nc.tensor.matmul(bank(6 + m % 2)[rows, :], w, PARTS[j % 2][name],
                                          start=name == "v1", stop=name == "v4")
                mm.then_inc(sem("s5_out"), 1)

            for j in range(ST):
                if j >= 2:
                    pe.wait_ge(sem("s5_in_taken"), 4 * (j - 1))
                for x in range(2):
                    nc.tensor.matmul(bank(2 + 2 * (j % 2) + x), s5b[:, (2 * j + x) * P:(2 * j + x + 1) * P],
                                     tile(s5x, j // 4), start=True, stop=True).then_inc(sem("s5_in"), 1)
                if j >= 2:
                    s5_out(j - 2)
            for j in range(ST - 2, ST):
                s5_out(j)
            dense("glu", lambda x: tile(s5x, x),
                  rhs_ready=lambda j, x: pe.wait_ge(sem("gelu_ready"), x + 1) if j == 0 else None)
            dense("w_bs", lambda x: tile(s5g, x),
                  rhs_ready=lambda j, x: pe.wait_ge(sem("s5_gated"), x + 1) if j == 0 else None)
            t0, b0 = FIRST_TILE["lru"], FIRST_BLOCK["lru"]
            for n in range(2 * LT):
                pe.wait_ge(y_taken, t0 + n - 1)
                if n % UPB == 0:
                    b = b0 + n // UPB
                    pe.wait_ge(landed[b % RING], 16 * (b // RING + 1))
                at = ((b0 + n // UPB) % RING) * BLOCK + n % UPB * P
                pe.wait_ge(sem("conv_ready"), n // 2 + 1)
                nc.tensor.matmul(bank((t0 + n) % 2), ring[:, at:at + P], conv[n // 2], start=True, stop=True
                                 ).then_inc(y_ready, 1)
            dense("w_bl", lambda x: tile(lrug, x),
                  rhs_ready=lambda j, x: pe.wait_ge(sem("lru_gated"), x + 1) if j == 0 else None)
            dense("w_out", lambda x: tile(gs, x),
                  rhs_ready=lambda j, x: pe.wait_ge(sem("merged"), x + 1) if j == 0 else None)
            mean_square(9)
            pe.wait_ge(sem("p_loaded"), 16)
            dense("ple", lambda x: pT[:, x * SEQ:(x + 1) * SEQ])
            dense("gate", lambda x: tile(h, x),
                  rhs_ready=lambda j, x: pe.wait_ge(sem("h_ready"), 4 * DT + x + 1) if j == 0 else None)

        @block.scalar
        def _(act):
            def squares(n, x, src):
                if n % 2 == 0 and x >= 2:
                    act.wait_ge(sem("sq_used"), DT * n + x - 1)
                nc.scalar.activation(square_tile(n, x), src, ACT.Square).then_inc(sem("sq_ready"), 1)

            def split_high(b, i=0, step=0):
                slot = slice(b % RING * BLOCK, (b % RING + 1) * BLOCK)
                act.wait_ge(landed[b % RING], i * (16 * step // RING) + 16 * (b // RING + 1))
                nc.scalar.activation(ring_hi[:, slot], ring[:, slot], ACT.Copy).then_inc(sem("weights_high"), 1)

            def split_u_high(n, u_hi):
                for x in range(DT):
                    act.wait_ge(sem("normed"), n * DT + x + 1)
                    nc.scalar.activation(tile(u_hi, x), u_tile(x), ACT.Copy).then_inc(sem("u_high"), 1)

            def root_mean(n):
                act.wait_ge(sem("sq_used"), DT * (n + 1))
                if n:
                    act.wait_ge(sem("normed"), DT * n)
                nc.scalar.activation(rstd[:, :], bank(7), ACT.Sqrt, bias=const("eps", 0, 1)).then_inc(sem("rms_ready"), 1)

            def pre_norm(n):
                for x in range(DT):
                    if n == 0:
                        act.wait_ge(sem("x_loaded"), 16)
                    else:
                        act.wait_ge(sem("h_ready"), (n // 2 - 1) * DT + x + 1)
                    squares(n, x, tile(h, x))
                root_mean(n)

            def take_out(name, n, dst=wbuf, splits=False):
                for x in range(DT):
                    if splits and x + AHEAD < DT:
                        split_high(FIRST_BLOCK[name] + x + AHEAD)
                    act.wait_ge(y_ready, FIRST_TILE[name] + x + 1)
                    squares(n, x, bank((FIRST_TILE[name] + x) % 2))
                    nc.scalar.activation(tile(dst, x), bank((FIRST_TILE[name] + x) % 2), ACT.Copy).then_inc(y_taken, 1)
                root_mean(n)

            def take_tile(name, x, dst, func=ACT.Copy, **kw):
                act.wait_ge(y_ready, FIRST_TILE[name] + x + 1)
                nc.scalar.activation(dst, bank((FIRST_TILE[name] + x) % 2), func, **kw).then_inc(y_taken, 1)

            act.wait_ge(sem("cols_loaded"), 16)
            act.wait_ge(sem("consts_loaded"), 16)
            nc.scalar.activation(derived(DT_, ST), cols[:, COLS["log_dt"]:COLS["log_dt"] + ST], ACT.Exp
                                 ).then_inc(sem("dt_exp"), 1)
            act.wait_ge(sem("s5_angles"), 1)
            nc.scalar.activation(derived(MAG, ST), derived(X_, ST), ACT.Exp).then_inc(sem("s5_exp"), 1)
            nc.scalar.activation(tmp(0), derived(X_, ST), ACT.Tanh, scale=0.5).then_inc(sem("s5_exp"), 1)
            nc.scalar.activation(tmp(1), derived(TH_, ST), ACT.Sin).then_inc(sem("s5_exp"), 1)
            nc.scalar.activation(tmp(2), derived(TH_, ST), ACT.Sin, scale=0.5).then_inc(sem("s5_exp"), 1)
            act.wait_ge(sem("lam_abs"), 1)
            nc.scalar.activation(tmp(10)[:, 0:LT], tmp(9)[:, 0:LT], ACT.Exp, scale=-1.0).then_inc(sem("lam_exp"), 1)
            act.wait_ge(sem("lines_summed"), 2)
            act.dma_start(lines_dram[:, :], line_sb).then_inc(sem("lines_stored"), 16)

            pre_norm(0)
            for b in range(AHEAD):
                split_high(b)
            split_u_high(0, attn_u_hi)
            for x in range(DT):
                split_high(x + AHEAD)
                take_tile("qk", x, tile(qT, x), scale=float(HEAD) ** -0.5)
            for x in range(5):
                split_high(DT + x + AHEAD)
                take_tile("qk", DT + x, tile(kT, x))
            for x in range(5):
                split_high(DT + 5 + x + AHEAD)
                take_tile("v", x, vtok.rearrange("p (t n) -> p t n", t=4)[:, :, x * P:(x + 1) * P])
            def head_rows_of(e):
                return slice(e * HEAD, (e + 1) * HEAD)

            def stage_keys(i):
                for e in range(2):
                    ins = nc.scalar.activation(k_st[e][head_rows_of(e), :], kT[head_rows_of(e), bass.ts(i, SEQ)], ACT.Copy)
                ins.then_inc(sem("k_staged"), 1)

            act.wait_ge(sem("keys_zeroed"), 4)
            act.wait_ge(y_taken, FIRST_TILE["attn_out"])
            for e in range(2):
                nc.scalar.activation(k_win[e][head_rows_of(e), :], kT[head_rows_of(e), 4 * SEQ:5 * SEQ], ACT.Copy)
            stage_keys(0)
            with act.Fori(0, 4) as i:
                def exponent(n):
                    head = (2 * i + n % 2) if n < 8 else (i + 8 + 4 * (n % 2))
                    act.wait_ge(sem("max_ready"), i * 16 + (n + 1))
                    if n >= 2:
                        act.wait_ge(sem("pt_ready"), i * 16 + (n - 1))
                    r = n % 4
                    nc.scalar.activation(p_sb[n % 2], s_sb[n % 2], ACT.Exp, bias=small[:, 4 + r:5 + r],
                                         accum_out=small[:, 8 + r:9 + r]).then_inc(sem("p_ready"), 1)
                    nc.scalar.activation(small[:, 12 + r:13 + r], col("sink", head), ACT.Exp,
                                         bias=small[:, 4 + r:5 + r]).then_inc(sem("sink_ready"), 1)

                def turned(n):
                    act.wait_ge(sem("pt_ready"), i * 16 + (n + 1))
                    if n >= 2:
                        act.wait_ge(sem("o_ready"), i * 16 + (n - 1))
                    nc.scalar.activation(pt_sb[n % 2], bank(4 + n % 2), ACT.Copy).then_inc(sem("pt_taken"), 1)

                def output(half):
                    act.wait_ge(sem("o_ready"), i * 16 + (8 * half + 8))
                    by_block = bank(6 + half).rearrange("p (b s) -> p b s", s=P)[:, :, ::-1]
                    to = attnT[:, bass.ds(i * SEQ + half * 4 * SEQ, SEQ)].rearrange("p (b s) -> p b s", s=P)
                    nc.scalar.activation(to, by_block, ACT.Copy).then_inc(sem("ot_taken"), 1)

                for n in range(16):
                    exponent(n)
                    if n >= 1:
                        turned(n - 1)
                    if n == 10:
                        output(0)
                        stage_keys(i + 1)
                turned(15)
                output(1)
            act.wait_ge(sem("ot_taken"), 9)
            for x in range(DT):
                nc.scalar.activation(tile(attnT_hi, x), tile(attnT, x), ACT.Copy).then_inc(sem("attn_high"), 1)
            take_out("attn_out", 1, splits=True)

            def mlp(n, first_norm):
                for b in range(AHEAD):
                    split_high(FIRST_BLOCK[f"up{n}a"] + b)
                pre_norm(first_norm)
                split_u_high(first_norm, mlp_u_hi)
                for half, part in enumerate("ab"):
                    t0, b0 = FIRST_TILE[f"up{n}{part}"], FIRST_BLOCK[f"up{n}{part}"]
                    with act.Fori(0, 2) as i:
                        for j in range(8):
                            split_high(b0 + j + AHEAD, i, 8)
                            act.wait_ge(y_ready, i * 8 + (t0 + j + 1))
                            nc.scalar.activation(relu[j % 2], bank((t0 + j) % 2), ACT.Relu).then_inc(sem("relu_ready"), 1)
                            act.wait_ge(y_taken, i * 8 + (t0 + j + 1))
                            at = bass.ds(i * (8 * SEQ) + j * SEQ, SEQ)
                            nc.scalar.activation(mid_hi[:, at], mid[:, at], ACT.Copy).then_inc(sem("mid_high"), 1)
                    t0, b0 = FIRST_TILE[f"down{n}{part}"], FIRST_BLOCK[f"down{n}{part}"]
                    for x in range(DT):
                        for b in range(b0 + 2 * x + AHEAD, b0 + 2 * x + 2 + AHEAD):
                            if half == 0 or b < b0 + 2 * DT:
                                split_high(b)
                        if half == 0:
                            act.wait_ge(y_ready, t0 + x + 1)
                            nc.scalar.activation(tile(wbuf, x), bank((t0 + x) % 2), ACT.Copy).then_inc(y_taken, 1)
                        else:
                            act.wait_ge(y_taken, t0 + x + 1)
                            squares(first_norm + 1, x, tile(wbuf, x))
                root_mean(first_norm + 1)

            mlp(0, 2)
            pre_norm(4)
            act.wait_ge(sem("mu_ready"), 1)
            for m, c in enumerate([1, 4, 5, 0, 2, 3]):
                if m >= 2:
                    name = ["lora_w", "lora_a", "lora_g", "r"][m - 2]
                    act.wait_ge(y_ready, FIRST_TILE[name] + SHAPE[name][0])
                for x in range(DT):
                    if m == 0:
                        act.wait_ge(sem("normed"), 4 * DT + x + 1)
                    at = MU0 + c * DT + x
                    nc.scalar.activation(tile(mixb[m % 2], x), u_tile(x), ACT.Copy, scale=der[:, at:at + 1]
                                         ).then_inc(sem("mix_started"), 1)
                if m == 0:
                    continue
                if m == 1:
                    take_tile("lora_w", 0, lo_w, ACT.Tanh)
                elif m == 2:
                    take_tile("lora_a", 0, lo_a)
                elif m == 3:
                    for x in range(2):
                        take_tile("lora_g", x, lo_g[x], ACT.Sigmoid)
                else:
                    for x in range(DT):
                        take_tile("r" if m == 4 else "k", x, tile(rT if m == 4 else kTr, x))
            for x in range(DT):
                take_tile("rv", x, tile(vTr, x))
                if x >= 2:
                    act.wait_ge(sem("kk_summed"), x - 1)
                nc.scalar.activation(sq[:, x % 2 * SEQ:(x % 2 + 1) * SEQ], tile(kTr, x), ACT.Square,
                                     scale=col("k_k", x)).then_inc(sem("kk_squared"), 1)
                if x >= 1:
                    act.wait_ge(sem("kk_clamped"), x)
                    nc.scalar.activation(tile(kk, x - 1), tile(kk, x - 1), ACT.Sqrt).then_inc(sem("kk_root"), 1)
            act.wait_ge(sem("kk_clamped"), DT)
            nc.scalar.activation(tile(kk, DT - 1), tile(kk, DT - 1), ACT.Sqrt).then_inc(sem("kk_root"), 1)

            def take_turned(dst, src, name):
                for c in range(2):
                    for e in range(2):
                        to = (dst[e] if isinstance(dst, list) else dst).rearrange("p (b c s) -> p b c s", c=2, s=CH)[e * HEAD:(e + 1) * HEAD, :, c, :]
                        of = src.rearrange("p (b e s) -> p b e s", e=2, s=CH)[c * CH:(c + 1) * CH, :, e, :]
                        ins = nc.scalar.activation(to, of, ACT.Copy)
                ins.then_inc(sem(name), 1)

            def alone(dst, src, name):
                for e in range(2):
                    ins = nc.scalar.activation(of_head(dst[e], e), of_head(src, e), ACT.Copy)
                ins.then_inc(sem(name), 1)

            def spread(n, F, k):
                name, d = ("al", "ro")[k // 2], k % 2
                act.wait_ge(sem("features_v"), n(2, d + 1))
                alone(R[d][name + "_alone"], F[d][name], "spread")

            act.wait_ge(sem("alone_zeroed"), 10)

            def features(n, F, step):
                for d in range(2):
                    act.wait_ge(sem("z_ready"), n(6, 2 * step + d + 1))
                    if step == 0:
                        nc.scalar.activation(F[d]["al"], bank(4 * d + 3), ACT.Sigmoid, bias=pair_col("w0", n, d)
                                             ).then_inc(sem("z_taken"), 1)
                    elif step == 1:
                        nc.scalar.activation(F[d]["be"], bank(4 * d + 3), ACT.Sigmoid, bias=pair_col("a0", n, d)
                                             ).then_inc(sem("z_taken"), 1)
                    else:
                        nc.scalar.activation(F[d]["g"], bank(4 * d + 3), ACT.Copy).then_inc(sem("z_taken"), 1)

            def decays(n, F, d):
                act.wait_ge(sem("decay_summed"), n(2, d + 1))
                nc.scalar.activation(F[d]["ka"], F[d]["ro"], ACT.Exp, scale=DECAY).then_inc(sem("decays_ready"), 1)
                nc.scalar.activation(F[d]["al"], F[d]["al"], ACT.Exp, scale=-DECAY).then_inc(sem("decays_ready"), 1)
                act.wait_ge(sem("decays_ready"), n(6, 3 * d + 1))
                nc.scalar.activation(F[d]["ro"], F[d]["ro"], ACT.Exp, scale=-DECAY).then_inc(sem("decays_ready"), 1)

            def out_squares(n, F):
                for d in range(2):
                    act.wait_ge(sem("o_centered"), n(2, d + 1))
                    nc.scalar.activation(F[d]["be"], F[d]["al"], ACT.Square).then_inc(sem("o_squared"), 1)

            def out_deviations(n, F):
                for d in range(2):
                    act.wait_ge(sem("var_ready"), n(2, d + 1))
                    nc.scalar.activation(F[d]["ka"], bank(4 * d + 3), ACT.Sqrt, bias=const("eps", 1, 1)
                                         ).then_inc(sem("deviation"), 1)

            def pair(parity, n, prev, nxt):
                F, G = feats[parity], feats[1 - parity]
                for d in range(2):
                    act.wait_ge(sem("scores_ready"), n(15, 1 + d))
                    nc.scalar.activation(R[d]["N"], bank(4 * d), ACT.Copy).then_inc(sem("n_copied"), 1)
                act.wait_ge(sem("scores_ready"), n(15, 3))
                take_turned(v_alone, bank(1), "v_turned")
                if prev:
                    for k in range(2, 4):
                        spread(n, F, k)
                if prev:
                    out_squares(prev, G)
                for d in range(2):
                    act.wait_ge(sem("scores_ready"), n(15, 6 + d))
                    take_turned(R[d]["L"], bank(4 * d + 1), "l_copied")
                if prev:
                    out_deviations(prev, G)
                act.wait_ge(sem("scores_ready"), n(15, 11))
                for d in range(2):
                    act.wait_ge(sem("t_started"), n(2, d + 1))
                    alone(R[d]["T_alone"], R[d]["T"], "t_alone")
                def features_turned(ready, name, b):
                    for d in range(2):
                        act.wait_ge(sem("scores_ready"), n(15, ready + d))
                        take_turned(F[d][name], bank(4 * d + b), "turned")

                features_turned(12, "be", 1)
                for l in range(1, LEVELS):
                    for d in range(2):
                        k = 2 * (l - 1) + d
                        act.wait_ge(sem("x_ready"), n(10, k + 1))
                        alone(R[d]["X_alone"], bank(4 * d), "x_taken")
                    if l == 1:
                        features_turned(14, "ka", 2)
                    if nxt and 2 <= l <= 4:
                        if prev and l == 2:
                            act.wait_ge(sem("pair_done"), n(1))
                        features(nxt, G, l - 2)
                    if nxt and l >= 4:
                        decays(nxt, G, l - 4)
                    for d in range(2):
                        if l < LEVELS - 1:
                            act.wait_ge(sem("tt_ready"), n(8, 2 * (l - 1) + d + 1))
                            take_turned(R[d]["TT"], bank(4 * d + 2), "tt_taken")
                for k in range(2 * NCH):
                    act.wait_ge(sem("w_ready"), n(16, k + 1))
                    alone(w_alone[k % 2], bank(4 * (k % 2), CH), "w_taken")
                    if nxt and k % 2 and 2 <= k // 2 < 4:
                        spread(nxt, G, k // 2 - 2)
                for d in range(2):
                    act.wait_ge(sem("o_ready_rw"), n(16, 15 + d))
                    nc.scalar.activation(F[d]["al"], bank(4 * d + 3), ACT.Copy).then_inc(sem("o_copied"), 1)

            first, last = (lambda per, c=0: c), (lambda per, c=0: (DT - 1) * per + c)
            for step in range(3):
                features(first, feats[0], step)
            for d in range(2):
                decays(first, feats[0], d)
            for k in range(4):
                spread(first, feats[0], k)
            over_pairs(act, pair)
            out_squares(last, feats[(DT - 1) % 2])
            out_deviations(last, feats[(DT - 1) % 2])
            take_out("o", 5, kTr)
            mlp(1, 6)
            for b in range(AHEAD):
                split_high(FIRST_BLOCK["w_in"] + b)
            pre_norm(8)
            split_u_high(8, in_u_hi)
            tiles = ([("s5x", x) for x in range(XT)] + [("s5g", x) for x in range(XT)]
                     + [("lrux", x) for x in range(LT)] + [("lrug", x) for x in range(LT)]
                     + [("gs", x) for x in range(DT)] + [("gl", x) for x in range(DT)])
            t0 = FIRST_TILE["w_in"]
            gated = []
            for n, (name, x) in enumerate(tiles):
                if n + AHEAD < len(tiles):
                    split_high(FIRST_BLOCK["w_in"] + n + AHEAD)
                act.wait_ge(y_ready, t0 + n + 1)
                src = bank((t0 + n) % 2)
                if name in ("s5g", "lrug"):
                    if len(gated) >= 2:
                        act.wait_ge(y_taken, t0 + gated[-2] + 1)
                    nc.scalar.activation(sgt[len(gated) % 2], src, ACT.Sigmoid).then_inc(sem("silu_sigmoid"), 1)
                    gated.append(n)
                    continue
                if n in (2 * XT, 2 * XT + 2 * LT):
                    act.wait_ge(y_taken, t0 + n)
                if name == "s5x":
                    nc.scalar.activation(tile(s5x, x), src, ACT.Copy).then_inc(y_taken, 1)
                elif name == "lrux":
                    nc.scalar.activation(lrux[:, x * LPAD + CONV - 1:(x + 1) * LPAD], src, ACT.Copy).then_inc(y_taken, 1)
                else:
                    nc.scalar.activation(tile(gs if name == "gs" else gl, x), src, ACT.Sigmoid).then_inc(y_taken, 1)
            act.dma_start(s5b, t["s5_b"]).then_inc(sem("s5b_landed"), 16)
            act.wait_ge(y_taken, FIRST_TILE["glu"])
            nc.scalar.activation(s5c_negated.rearrange("p (j n) -> p j n", j=ST),
                                 s5c[:, :].rearrange("p (j r n) -> p j r n", j=ST, r=2)[:, :, 0, :], ACT.Copy, scale=-1.0)
            for j in range(ST):
                v = TURNS[j % 3]
                act.wait_ge(sem("s5_phase"), j + 1)
                nc.scalar.activation(v["C"], v["A"], ACT.Sin, scale=TWO_PI / 2).then_inc(sem("s5_half"), 1)
                nc.scalar.activation(v["S"], v["A"], ACT.Sin, scale=TWO_PI)
                act.wait_ge(sem("s5_half"), 2 * j + 1)
                nc.scalar.activation(v["C"], v["C"], ACT.Square).then_inc(sem("s5_half"), 1)
                act.wait_ge(sem("s5_half"), 2 * j + 2)
                nc.scalar.activation(v["C"], v["C"], ACT.Copy, scale=-2.0, bias=1.0).then_inc(sem("s5_cosine"), 1)
            for x in range(XT):
                act.wait_ge(sem("s5_skipped"), x + 1)
                nc.scalar.activation(tile(s5x, x), tile(s5x, x), ACT.Gelu_apprx_tanh).then_inc(sem("gelu_ready"), 1)
            act.wait_ge(sem("gelu_ready"), XT)
            t0 = FIRST_TILE["glu"]
            for x in range(XT):
                act.wait_ge(y_ready, t0 + 2 * x + 1)
                if x >= 2:
                    act.wait_ge(sem("s5_gated"), x - 1)
                nc.scalar.activation(sgt[x % 2], bank((t0 + 2 * x) % 2), ACT.Sigmoid).then_inc(sem("glu_sigmoid"), 1)
            t0 = FIRST_TILE["lru"]
            act.wait_ge(y_taken, t0)
            for x in range(LT):
                act.wait_ge(y_ready, t0 + 2 * x + 1)
                nc.scalar.activation(rate[x], bank((t0 + 2 * x) % 2), ACT.Sigmoid, bias=col("b_a", x)).then_inc(y_taken, 1)
                act.wait_ge(y_ready, t0 + 2 * x + 2)
                if x >= 2:
                    act.wait_ge(sem("lru_in"), x - 1)
                nc.scalar.activation(i_t[x % 2], bank((t0 + 2 * x + 1) % 2), ACT.Sigmoid, bias=col("b_x", x)).then_inc(y_taken, 1)
            for x in range(LT):
                act.wait_ge(y_taken, t0 + 2 * x + 1)
                nc.scalar.activation(lru_a[x], rate[x], ACT.Exp, scale=der[:, SP8 + x:SP8 + x + 1]).then_inc(sem("a_ready"), 1)
                act.wait_ge(sem("a_ready"), x + 1)
                nc.scalar.activation(rate[x], rate[x], ACT.Tanh, scale=der[:, SP4 + x:SP4 + x + 1]).then_inc(sem("tanh_ready"), 1)
            for x in range(LT):
                act.wait_ge(sem("tanh_ready"), x + 1)
                if x >= 2:
                    act.wait_ge(sem("lru_b"), x - 1)
                nc.scalar.activation(root[x % 2], rate[x], ACT.Sqrt).then_inc(sem("root_ready"), 1)
            act.wait_ge(y_ready, FIRST_TILE["lru"])
            act.dma_start(pT, t["p"]).then_inc(sem("p_loaded"), 16)
            take_out("w_out", 9)
            for x in range(DT):
                take_tile("ple", x, tile(gl, x))
            for x in range(DT):
                act.wait_ge(y_ready, FIRST_TILE["gate"] + x + 1)
                if x >= 2:
                    act.wait_ge(sem("gated"), x - 1)
                nc.scalar.activation(sgt[x % 2], bank((FIRST_TILE["gate"] + x) % 2), ACT.Sigmoid).then_inc(y_taken, 1)
            for x in range(DT):
                act.wait_ge(sem("final"), x + 1)
                act.dma_start(out[:, x * SEQ:(x + 1) * SEQ], tile(gl, x)).then_inc(sem("out_stored"), 16)
            act.wait_ge(sem("out_stored"), 16 * DT)

        @block.vector
        def _(dve):
            V_ = nc.vector
            steps = [0]

            def link(ins):
                steps[0] += 1
                ins.then_inc(sem("param_step"), 1)
                dve.wait_ge(sem("param_step"), steps[0])

            def normalise(n, g, x_of, out_of):
                dve.wait_ge(sem("rms_ready"), n + 1)
                V_.reciprocal(rstd[:, :], rstd[:, :]).then_inc(sem("rstd_ready"), 1)
                dve.wait_ge(sem("rstd_ready"), n + 1)
                for x in range(DT):
                    V_.scalar_tensor_tensor(out=out_of(x), in0=x_of(x), scalar=col(g[0], g[1] + x), in1=rstd[:, :],
                                            op0=ALU.mult, op1=ALU.mult).then_inc(sem("normed"), 1)

            def pre_norm(n, g):
                normalise(n, g, lambda x: tile(h, x), u_tile)

            def split_u_low(n, u_hi):
                for x in range(DT):
                    dve.wait_ge(sem("u_high"), n * DT + x + 1)
                    TT(u_lo_tile(x), u_tile(x), tile(u_hi, x).bitcast(F32), ALU.subtract).then_inc(sem("u_split"), 1)

            def post_norm(n, g, buf=wbuf):
                normalise(n, g, lambda x: tile(buf, x), lambda x: tile(buf, x))

            dve.wait_ge(sem("line_const_loaded"), 16)
            dve.wait_ge(sem("lines_ready"), 1)
            for half in range(2):
                at = slice(half * SEQ, (half + 1) * SEQ)
                V_.tensor_tensor(line_sb[:, at], bank(5 + half)[0:16, :], line_const[:, at], ALU.add
                                 ).then_inc(sem("lines_summed"), 1)
            dve.wait_ge(sem("cols_loaded"), 16)

            def cs(name, n):
                return cols[:, COLS[name]:COLS[name] + n]

            dve.wait_ge(sem("dt_exp"), 1)
            TT, TS, STT = V_.tensor_tensor, V_.tensor_scalar, V_.scalar_tensor_tensor
            TT(derived(X_, ST), cs("a_re", ST), derived(DT_, ST), ALU.mult).then_inc(sem("param_x"), 1)
            link(TT(derived(TH_, ST), cs("a_im", ST), derived(DT_, ST), ALU.mult))
            th = derived(TH_, ST)
            link(TS(tmp(3), th, 1.0 / TWO_PI, ROUND, ALU.mult, ALU.add))
            link(TS(tmp(3), tmp(3), -ROUND, None, ALU.add))
            for part in TURN_PARTS:
                link(STT(out=th, in0=tmp(3), scalar=-part, in1=th, op0=ALU.mult, op1=ALU.add))
            dve.wait_ge(sem("param_x"), 1)
            TS(th, th, PI_BELOW, -PI_BELOW, ALU.min, ALU.max).then_inc(sem("s5_angles"), 1)
            dve.wait_ge(sem("s5_angles"), 1)
            link(TS(tmp(4), th, 1.0 / TWO_PI, None, ALU.mult))
            link(TS(tmp(5), tmp(4), ROUND12, None, ALU.add))
            link(TS(derived(PHH, ST), tmp(5), -ROUND12, None, ALU.add))
            link(TT(derived(PHL, ST), tmp(4), derived(PHH, ST), ALU.subtract))
            dve.wait_ge(sem("s5_exp"), 4)
            t_, sin_, sh_ = tmp(0), tmp(1), tmp(2)
            link(TS(tmp(3), t_, -1.0, 1.0, ALU.mult, ALU.add))
            link(V_.reciprocal(tmp(3), tmp(3)))
            link(STT(out=t_, in0=t_, scalar=2.0, in1=tmp(3), op0=ALU.mult, op1=ALU.mult))
            link(TT(sh_, sh_, sh_, ALU.mult))
            link(TS(tmp(3), sh_, -2.0, 1.0, ALU.mult, ALU.add))
            link(TT(tmp(3), tmp(3), t_, ALU.mult))
            link(STT(out=tmp(3), in0=sh_, scalar=-2.0, in1=tmp(3), op0=ALU.mult, op1=ALU.add))
            link(TT(tmp(4), derived(MAG, ST), sin_, ALU.mult))
            re, im = cs("a_re", ST), cs("a_im", ST)
            link(TT(tmp(5), re, re, ALU.mult))
            link(TT(tmp(6), im, im, ALU.mult))
            link(TT(tmp(5), tmp(5), tmp(6), ALU.add))
            link(V_.reciprocal(tmp(5), tmp(5)))
            link(TT(tmp(6), tmp(3), re, ALU.mult))
            link(TT(tmp(7), tmp(4), im, ALU.mult))
            link(TT(tmp(6), tmp(6), tmp(7), ALU.add))
            link(TT(derived(ZRE, ST), tmp(6), tmp(5), ALU.mult))
            link(TT(tmp(6), tmp(4), re, ALU.mult))
            link(TT(tmp(7), tmp(3), im, ALU.mult))
            link(TT(tmp(6), tmp(6), tmp(7), ALU.subtract))
            link(TT(derived(ZIM, ST), tmp(6), tmp(5), ALU.mult))
            dve.wait_ge(sem("s5_c_loaded"), 16)
            cin = s5_in.rearrange("p (j r n) -> p j r n", j=ST, r=2)
            cout = s5c[:, :].rearrange("p (j r n) -> p j r n", j=ST, r=2)
            ca, cb = [a.rearrange("p (j n) -> p j n", j=ST) for a in s5_t]
            zre = derived(ZRE, ST).unsqueeze(2).to_broadcast([P, ST, 32])
            zim = derived(ZIM, ST).unsqueeze(2).to_broadcast([P, ST, 32])
            link(TT(ca, cin[:, :, 0, :], zre, ALU.mult))
            link(TT(cb, cin[:, :, 1, :], zim, ALU.mult))
            link(TT(cout[:, :, 0, :], ca, cb, ALU.subtract))
            link(TT(ca, cin[:, :, 0, :], zim, ALU.mult))
            link(TT(cb, cin[:, :, 1, :], zre, ALU.mult))
            link(TT(ca, ca, cb, ALU.add))
            link(TS(cout[:, :, 1, :], ca, -1.0, None, ALU.mult))
            lam, y, z, z2, acc = cs("lam", LT), tmp(10)[:, 0:LT], tmp(11)[:, 0:LT], tmp(12)[:, 0:LT], tmp(13)[:, 0:LT]
            STT(out=tmp(9)[:, 0:LT], in0=lam, scalar=-1.0, in1=lam, op0=ALU.mult, op1=ALU.max).then_inc(sem("lam_abs"), 1)
            dve.wait_ge(sem("lam_exp"), 1)
            link(TS(z, y, 2.0, None, ALU.add))
            link(V_.reciprocal(z, z))
            link(TT(z, z, y, ALU.mult))
            link(TT(z2, z, z, ALU.mult))
            link(TS(acc, z2, 1.0 / 17, 1.0 / 15, ALU.mult, ALU.add))
            for n in (13, 11, 9, 7, 5, 3, 1):
                link(TT(acc, acc, z2, ALU.mult))
                link(TS(acc, acc, 1.0 / n, None, ALU.add))
            link(TT(acc, acc, z, ALU.mult))
            link(TS(z2, lam, -1.0, 0.0, ALU.mult, ALU.max))
            link(STT(out=z2, in0=acc, scalar=2.0, in1=z2, op0=ALU.mult, op1=ALU.add))
            link(TS(der[:, SP4:SP4 + LT], z2, 4.0, None, ALU.mult))
            link(TS(der[:, SP8:SP8 + LT], z2, -8.0, None, ALU.mult))
            mu0 = der[:, MU0:MU0 + 6 * DT]
            link(TT(mu0, cs("mu_prev", 6 * DT), cs("mu_next", 6 * DT), ALU.add))
            TS(mu0, mu0, -1.0, 1.0, ALU.mult, ALU.add).then_inc(sem("mu_ready"), 1)
            link(TS(der[:, OMKA:OMKA + DT], cs("k_a", DT), -1.0, 1.0, ALU.mult, ALU.add))
            V_.tensor_copy(small[:, 40:41], der[:, OMKA:OMKA + 1]).then_inc(sem("s5c_ready"), 1)

            pre_norm(0, ("norm_g", 0))
            split_u_low(0, attn_u_hi)
            with dve.Fori(0, 4) as i:
                def biased(n):
                    half, qi, e = n // 8, n % 8 // 2, n % 2
                    head = (2 * i + e) if n < 8 else (i + 8 + 4 * e)
                    r = n % 4
                    dve.wait_ge(sem("s_ready"), i * 16 + (n + 1))
                    if n % 8 < 2:
                        dve.wait_ge(sem(f"bias_landed_{2 * half + e}"), i * 16 + 16)
                    if n >= 2:
                        dve.wait_ge(sem("p_ready"), i * 16 + (n - 1))
                    dve.nop(nofuse=True)
                    V_.tensor_tensor_reduce(s_sb[n % 2], bank(n % 4), bias[2 * half + e][:, (3 - qi) * P:(3 - qi) * P + SEQ],
                                            1.0, -3.0e38, ALU.add, ALU.max, small[:, r:r + 1]).then_inc(sem("s_biased"), 1)
                    dve.wait_ge(sem("s_biased"), i * 16 + (n + 1))
                    TS(small[:, 4 + r:5 + r], small[:, r:r + 1], col("sink", head), -1.0, ALU.max, ALU.mult
                       ).then_inc(sem("max_ready"), 1)

                def weights(n):
                    r = n % 4
                    dve.wait_ge(sem("sink_ready"), i * 16 + (n + 1))
                    TT(small[:, 20 + r:21 + r], small[:, 8 + r:9 + r], small[:, 12 + r:13 + r], ALU.add
                       ).then_inc(sem("den_ready"), 1)
                    dve.wait_ge(sem("den_ready"), i * 16 + (n + 1))
                    V_.reciprocal(small[:, 16 + r:17 + r], small[:, 20 + r:21 + r]).then_inc(sem("rden_ready"), 1)
                    dve.wait_ge(sem("rden_ready"), i * 16 + (n + 1))
                    TS(p_sb[n % 2], p_sb[n % 2], small[:, 16 + r:17 + r], None, ALU.mult).then_inc(sem("p_scaled"), 1)

                for n in range(16):
                    biased(n)
                    if n >= 1:
                        weights(n - 1)
                weights(15)
            for x in range(DT):
                dve.wait_ge(sem("attn_high"), x + 1)
                TT(tile(attnT_lo, x), tile(attnT, x), tile(attnT_hi, x).bitcast(F32), ALU.subtract).then_inc(sem("attn_split"), 1)
            post_norm(1, ("norm_g", DT))
            def mlp(n, first_norm, g):
                pre_norm(first_norm, ("norm_g", g * DT))
                split_u_low(n + 1, mlp_u_hi)
                for half, part in enumerate("ab"):
                    t0, done = FIRST_TILE[f"up{n}{part}"], n * FT + half * FT // 2
                    with dve.Fori(0, 2) as i:
                        for j in range(8):
                            at = bass.ds(i * (8 * SEQ) + j * SEQ, SEQ)
                            dve.wait_ge(sem("relu_ready"), i * 8 + (done + j + 1))
                            TT(mid[:, at], bank((t0 + j) % 2), relu[j % 2], ALU.mult).then_inc(y_taken, 1)
                            dve.wait_ge(sem("mid_high"), i * 8 + (done + j + 1))
                            TT(mid_lo[:, at], mid[:, at], mid_hi[:, at].bitcast(F32), ALU.subtract).then_inc(sem("mid_split"), 1)
                t0 = FIRST_TILE[f"down{n}b"]
                for x in range(DT):
                    dve.wait_ge(y_ready, t0 + x + 1)
                    TT(tile(wbuf, x), tile(wbuf, x), bank((t0 + x) % 2), ALU.add).then_inc(y_taken, 1)
                post_norm(first_norm + 1, ("norm_g", (g + 1) * DT))

            mlp(0, 2, 2)
            pre_norm(4, ("norm_g", 4 * DT))
            dve.wait_ge(sem("normed"), 5 * DT)
            dve.wait_ge(sem("pads_zeroed"), 2)
            for m, c in enumerate([1, 4, 5, 0, 2, 3]):
                for x in range(DT):
                    dve.wait_ge(sem("mix_started"), m * DT + x + 1)
                    STT(out=tile(mixb[m % 2], x), in0=u_tile(x, -1), scalar=col("mu_prev", c * DT + x),
                        in1=tile(mixb[m % 2], x), op0=ALU.mult, op1=ALU.add).then_inc(sem("mix_half"), 1)
                for x in range(DT):
                    dve.wait_ge(sem("mix_half"), m * DT + x + 1)
                    STT(out=tile(mixb[m % 2], x), in0=u_tile(x, 1), scalar=col("mu_next", c * DT + x),
                        in1=tile(mixb[m % 2], x), op0=ALU.mult, op1=ALU.add).then_inc(sem("mixed"), 1)
            for n in range(DT + 2):
                if n < DT:
                    dve.wait_ge(sem("kk_summed"), n + 1)
                    TS(tile(kk, n), bank(6 + n % 2), 1e-24, None, ALU.max).then_inc(sem("kk_clamped"), 1)
                if 1 <= n <= DT:
                    dve.wait_ge(sem("kk_root"), n)
                    V_.reciprocal(tile(kk, n - 1), tile(kk, n - 1)).then_inc(sem("kk_inverse"), 1)
                if n >= 2:
                    x = n - 2
                    dve.wait_ge(sem("kk_inverse"), x + 1)
                    STT(out=tile(kk, x), in0=tile(kTr, x), scalar=col("k_k", x), in1=tile(kk, x),
                        op0=ALU.mult, op1=ALU.mult).then_inc(sem("kk_ready"), 1)
            dve.wait_ge(sem("kk_ready"), DT)
            def ends(a, d):
                return chunks(a)[:, :, CH - 1] if d == 0 else chunks(a)[:, :, 0]

            def features(n, F, ends_at, step):
                if step == 0:
                    for d in range(2):
                        r = F[d]
                        dve.wait_ge(sem("z_taken"), n(6, 1 + d))
                        src, dst = (r["al"], r["ro"]) if d == 0 else (r["al"][:, ::-1], r["ro"][:, ::-1])
                        V_.tensor_tensor_scan(dst, const("carry", 0, SEQ), src, 0.0, ALU.mult, ALU.add
                                              ).then_inc(sem("decay_scanned"), 1)
                    for d in range(2):
                        r = F[d]
                        dve.wait_ge(sem("decay_scanned"), n(2, d + 1))
                        TT(r["al"], r["ro"], r["al"], ALU.subtract).then_inc(sem("decay_summed"), 1)
                    return
                if step == 1:
                    for d in range(2):
                        r = F[d]
                        dve.wait_ge(sem("z_taken"), n(6, 3 + d))
                        TS(r["kd"], r["be"], pair_col("k_a", n), der[:, bass.ds(n(1, OMKA), 1)], ALU.mult, ALU.add
                           ).then_inc(sem("kd_factor"), 1)
                    return
                d = step - 2
                r = F[d]
                dve.wait_ge(sem("decays_ready"), n(6, 3 * (d + 1)))
                V_.tensor_copy(ends_at[d], ends(r["ro"], d)).then_inc(sem("p_end_ready"), 1)
                STT(out=r["al"], in0=r["al"], scalar=-1.0, in1=pair_tile(kk, n), op0=ALU.mult, op1=ALU.mult
                    ).then_inc(sem("al_ready"), 1)
                dve.wait_ge(sem("p_end_ready"), n(2, d + 1))
                TT(r["ro"], r["ro"], pair_tile(rT, n), ALU.mult).then_inc(sem("features_v"), 1)

            def out_centered(n, F):
                for d in range(2):
                    dve.wait_ge(sem("mean_ready"), n(2, d + 1))
                    TT(F[d]["al"], F[d]["al"], bank(4 * d + 3), ALU.subtract).then_inc(sem("o_centered"), 1)

            def out_bonus(n, F):
                for d in range(2):
                    dve.wait_ge(sem("bonus_ready"), n(2, d + 1))
                    TT(F[d]["ro"], pair_tile(vTr, n), bank(4 * d + 3), ALU.mult).then_inc(sem("bonus_done"), 1)

            def out_inverses(n, F):
                for d in range(2):
                    dve.wait_ge(sem("deviation"), n(2, d + 1))
                    V_.reciprocal(F[d]["ka"], F[d]["ka"]).then_inc(sem("deviation_inverse"), 1)

            def out_scaled(n, F):
                for d in range(2):
                    dve.wait_ge(sem("deviation_inverse"), n(2, d + 1))
                    TT(F[d]["al"], F[d]["al"], F[d]["ka"], ALU.mult).then_inc(sem("o_scaled"), 1)
                for d in range(2):
                    dve.wait_ge(sem("o_scaled"), n(2, d + 1))
                    dve.wait_ge(sem("bonus_done"), n(2, d + 1))
                    STT(out=F[d]["al"], in0=F[d]["al"], scalar=pair_col("gn_w", n), in1=F[d]["ro"], op0=ALU.mult, op1=ALU.add
                        ).then_inc(sem("with_bonus"), 1)
                for d in range(2):
                    dve.wait_ge(sem("with_bonus"), n(2, d + 1))
                    STT(out=F[d]["al"], in0=F[d]["al"], scalar=pair_col("gn_b", n), in1=F[d]["g"], op0=ALU.add, op1=ALU.mult
                        ).then_inc(sem("dir_gated"), 1)
                dve.wait_ge(sem("dir_gated"), n(2, 2))
                TT(pair_tile(rT, n), F[0]["al"], F[1]["al"], ALU.add).then_inc(sem("pair_done"), 1)

            def pair(parity, n, prev, nxt):
                F, G = feats[parity], feats[1 - parity]

                def masked(ready, name, b, kind):
                    for d in range(2):
                        dve.wait_ge(sem("scores_ready"), n(15, ready + d))
                        TT(chunks(R[d][name]), chunks(bank(4 * d + b)), mask(kind, d), ALU.mult).then_inc(sem("masked_v"), 1)

                for d in range(2):
                    r = F[d]
                    dve.wait_ge(sem("features_p"), n(2, d + 1))
                    STT(out=r["kd"], in0=r["kd"], scalar=pair_col("r_k", n), in1=pair_tile(rT, n), op0=ALU.mult, op1=ALU.mult
                        ).then_inc(sem("bonus_terms"), 1)
                for d in range(2):
                    dve.wait_ge(sem("n_copied"), n(2, d + 1))
                    TT(chunks(R[d]["T"]), chunks(R[d]["N"]), mask("level_n", d), ALU.mult).then_inc(sem("n_masked"), 1)
                if prev:
                    out_centered(prev, G)
                masked(4, "Ma", 2, "strict")
                if prev:
                    out_bonus(prev, G)
                masked(8, "Mb", 0, "incl")
                if prev:
                    out_inverses(prev, G)
                masked(10, "Mr", 3, "incl")
                for l in range(1, LEVELS):
                    for d in range(2):
                        k = 2 * (l - 1) + d
                        dve.wait_ge(sem("dt_ready"), n(10, k + 1))
                        TT(R[d]["T"], R[d]["T"], bank(4 * d + 1), ALU.add).then_inc(sem("t_updated"), 1)
                        if l < LEVELS - 1:
                            for e in range(2):
                                to = of_head(R[d]["T_alone"][e], e)
                                ins = TT(to, to, of_head(bank(4 * d + 1), e), ALU.add)
                            ins.then_inc(sem("t_alone_updated"), 1)
                    if prev and l == 1:
                        out_scaled(prev, G)
                    if nxt and l >= 2:
                        features(nxt, G, p_end[1 - parity], l - 2)
                for j in range(NCH):
                    for d in range(2):
                        dve.wait_ge(sem("u_ready"), n(16, 2 * j + d + 1))
                        for e in range(2):
                            ins = V_.tensor_copy(of_head(u_alone[d][e], e), of_head(bank(4 * d + 1, CH), e))
                        ins.then_inc(sem("u_taken"), 1)
                    if j == NCH - 1:
                        break
                    for d in range(2):
                        k = 2 * j + d
                        c = j if d == 0 else NCH - 1 - j
                        decay = p_end[parity][d][:, c:c + 1]
                        dve.wait_ge(sem("s_ready_rw"), n(14, k + 1))
                        if j:
                            dve.wait_ge(sem("state_decayed"), n(12, k - 1))
                        for e in range(2):
                            new, added = of_head(s_alone[(j + 1) % 2][d][e], e), of_head(bank(4 * d + 2, CH), e)
                            if j == 0:
                                ins = TS(new, added, of_head(decay, e), None, ALU.mult)
                            else:
                                ins = STT(out=new, in0=added, scalar=of_head(decay, e), in1=of_head(st_p[d], e),
                                          op0=ALU.mult, op1=ALU.add)
                        ins.then_inc(sem("state_ready"), 1)
                    if j < NCH - 2:
                        for d in range(2):
                            k = 2 * j + d
                            c = j if d == 0 else NCH - 1 - j
                            nxt_c = c + 1 if d == 0 else c - 1
                            dve.wait_ge(sem("state_ready"), n(14, k + 1))
                            for e in range(2):
                                ins = TS(of_head(st_p[d], e), of_head(s_alone[(j + 1) % 2][d][e], e),
                                         p_end[parity][d][e * HEAD:(e + 1) * HEAD, nxt_c:nxt_c + 1], None, ALU.mult)
                            ins.then_inc(sem("state_decayed"), 1)

            first, last = (lambda per, c=0: c), (lambda per, c=0: (DT - 1) * per + c)
            for step in range(4):
                features(first, feats[0], p_end[0], step)
            over_pairs(dve, pair)
            out_centered(last, feats[(DT - 1) % 2])
            out_bonus(last, feats[(DT - 1) % 2])
            out_inverses(last, feats[(DT - 1) % 2])
            out_scaled(last, feats[(DT - 1) % 2])
            post_norm(5, ("norm_g", 5 * DT), kTr)
            mlp(1, 6, 6)
            pre_norm(8, ("g_pre", 0))
            split_u_low(3, in_u_hi)
            t0 = FIRST_TILE["w_in"]
            gates = 0

            def convolve(x):
                def tap(n):
                    return lrux[:, x * LPAD + n:x * LPAD + n + SEQ]
                part = conv_sum[x % 2]
                dve.wait_ge(y_taken, t0 + 2 * XT + x + 1)
                link(TS(part, tap(0), col("conv_w", x), col("conv_b", x), ALU.mult, ALU.add))
                for n in range(1, CONV):
                    ins = STT(out=part if n < CONV - 1 else conv[x], in0=tap(n), scalar=col("conv_w", n * LT + x),
                              in1=part, op0=ALU.mult, op1=ALU.add)
                    if n < CONV - 1:
                        link(ins)
                    else:
                        ins.then_inc(sem("conv_ready"), 1)

            dve.wait_ge(sem("conv_zeroed"), 1)
            for n in list(range(XT, 2 * XT)) + list(range(2 * XT + LT, 2 * XT + 2 * LT)):
                if n == 2 * XT + LT:
                    for x in range(LT):
                        convolve(x)
                dst = tile(s5g, n - XT) if n < 2 * XT else tile(lrug, n - 2 * XT - LT)
                dve.wait_ge(sem("silu_sigmoid"), gates + 1)
                if n in (XT, 2 * XT + LT):
                    dve.wait_ge(y_taken, t0 + n)
                TT(dst, bank((t0 + n) % 2), sgt[gates % 2], ALU.mult).then_inc(y_taken, 1)
                gates += 1

            def phase(j):
                v = TURNS[j % 3]
                a, b = v["A"], v["B"]
                if j >= 3:
                    dve.wait_ge(sem("s5_part"), 4 * (j - 2))
                else:
                    dve.wait_ge(y_taken, FIRST_TILE["glu"])
                iota = const("iota", 0, SEQ)
                link(TS(a, iota, der[:, PHH + j:PHH + j + 1], None, ALU.mult))
                link(TS(b, a, ROUND, -ROUND, ALU.add, ALU.add))
                link(TT(a, a, b, ALU.subtract))
                link(STT(out=a, in0=iota, scalar=der[:, PHL + j:PHL + j + 1], in1=a, op0=ALU.mult, op1=ALU.add))
                link(TS(b, a, ROUND, -ROUND, ALU.add, ALU.add))
                TT(a, a, b, ALU.subtract).then_inc(sem("s5_phase"), 1)

            def skip(m):
                dve.wait_ge(sem("s5_out"), 4 * (m + 1))
                STT(out=tile(s5x, m), in0=tile(s5x, m), scalar=col("s5_d", m), in1=bank(6 + m % 2),
                    op0=ALU.mult, op1=ALU.add).then_inc(sem("s5_skipped"), 1)

            phase(0)
            for j in range(ST):
                v, w = TURNS[j % 3], PARTS[j % 2]
                dve.wait_ge(sem("s5_cosine"), j + 1)
                dve.wait_ge(sem("s5_in"), 2 * (j + 1))
                if j >= 2:
                    dve.wait_ge(sem("s5_out"), j - 1)
                br, bi = bank(2 + 2 * (j % 2)), bank(3 + 2 * (j % 2))
                TT(w["v1"], br, v["C"], ALU.mult).then_inc(sem("s5_in_taken"), 1)
                TT(w["v2"], bi, v["S"], ALU.mult).then_inc(sem("s5_in_taken"), 1)
                TT(w["v3"], bi, v["C"], ALU.mult).then_inc(sem("s5_in_taken"), 1)
                TT(w["v4"], br, v["S"], ALU.mult).then_inc(sem("s5_in_taken"), 1)
                if j + 1 < ST:
                    phase(j + 1)
                mag = der[:, MAG + j:MAG + j + 1].to_broadcast([P, SEQ])
                dve.wait_ge(sem("s5_back"), 2 * j + 1)
                V_.tensor_tensor_scan(v["A"], mag, w["v1"], 0.0, ALU.mult, ALU.add).then_inc(sem("s5_scanned"), 1)
                dve.wait_ge(sem("s5_back"), 2 * j + 2)
                V_.tensor_tensor_scan(v["B"], mag, w["v3"], 0.0, ALU.mult, ALU.add).then_inc(sem("s5_scanned"), 1)
                if j % 4 == 0 and j:
                    skip(j // 4 - 1)
            skip(XT - 1)
            t0 = FIRST_TILE["glu"]
            for x in range(XT):
                dve.wait_ge(y_ready, t0 + 2 * x + 2)
                dve.wait_ge(sem("glu_sigmoid"), x + 1)
                TT(sgt[x % 2], bank((t0 + 2 * x + 1) % 2), sgt[x % 2], ALU.mult).then_inc(y_taken, 2)
                dve.wait_ge(y_taken, t0 + 2 * x + 2)
                TT(tile(s5g, x), tile(s5g, x), sgt[x % 2], ALU.mult).then_inc(sem("s5_gated"), 1)
            t0 = FIRST_TILE["w_bs"]
            for x in range(DT):
                dve.wait_ge(y_ready, t0 + x + 1)
                TT(tile(gs, x), tile(gs, x), bank((t0 + x) % 2), ALU.mult).then_inc(y_taken, 1)
            for x in range(LT):
                a, b = lru_a[x], fb[x % 2]
                dve.wait_ge(sem("root_ready"), x + 1)
                link(STT(out=b, in0=a, scalar=1.0, in1=root[x % 2], op0=ALU.add, op1=ALU.mult))
                dve.wait_ge(sem("lru_in"), x + 1)
                TT(b, b, conv[x], ALU.mult).then_inc(sem("lru_b"), 1)
                dve.wait_ge(sem("lru_b"), x + 1)
                link(V_.tensor_tensor_scan(rate[x], a, b, 0.0, ALU.mult, ALU.add))
                TT(tile(lrug, x), tile(lrug, x), rate[x], ALU.mult).then_inc(sem("lru_gated"), 1)
            t0 = FIRST_TILE["w_bl"]
            for x in range(DT):
                dve.wait_ge(y_ready, t0 + x + 1)
                TT(tile(gl, x), tile(gl, x), bank((t0 + x) % 2), ALU.mult).then_inc(y_taken, 1)
            post_norm(9, ("g_post", 0))
            t0 = FIRST_TILE["gate"]
            for x in range(DT):
                dve.wait_ge(y_taken, t0 + x + 1)
                TT(tile(gl, x), tile(gl, x), sgt[x % 2], ALU.mult).then_inc(sem("gated"), 1)

        @block.gpsimd
        def _(pool):
            G = nc.gpsimd
            up = u[:, :].rearrange("p (t n) -> p t n", t=DT)
            G.memset(up[:, :, 0:1], 0.0).then_inc(sem("pads_zeroed"), 1)
            G.memset(up[:, :, PAD - 1:PAD], 0.0).then_inc(sem("pads_zeroed"), 1)
            G.memset(small[:, 48:49], 0.0).then_inc(sem("ot_taken"), 1)

            def split_low(b, i=0, step=0):
                slot = slice(b % RING * BLOCK, (b % RING + 1) * BLOCK)
                pool.wait_ge(sem("weights_high"), i * step + SPLIT_COUNT[b])
                G.tensor_tensor(ring_lo[:, slot], ring[:, slot], ring_hi[:, slot].bitcast(F32), ALU.subtract
                                ).then_inc(sem("weights_split"), 1)

            def split_stream(first, end):
                assert (end - first) % RING == 0
                with pool.Fori(0, (end - first) // RING) as i:
                    for j in range(RING):
                        split_low(first + j, i, RING)

            def add_out(n, buf=wbuf):
                for x in range(DT):
                    pool.wait_ge(sem("normed"), n * DT + x + 1)
                    G.tensor_tensor(tile(h, x), tile(h, x), tile(buf, x), ALU.add).then_inc(sem("h_ready"), 1)

            for b in range(FIRST_BLOCK["attn_out"] + AHEAD):
                split_low(b)
            def stage_queries(i, half):
                by_block = qkT[:, bass.ds(i * SEQ + half * 4 * SEQ, SEQ)].rearrange("p (b s) -> p b s", s=P)
                G.tensor_copy(q_st[half].rearrange("p (b s) -> p b s", s=P)[:, :, ::-1], by_block).then_inc(sem("q_staged"), 1)

            def stage_values(i):
                v = vtok.rearrange("p (t n) -> p t n", t=4)[:, :, bass.ds(i * P, P)]
                G.tensor_copy(v_pair.rearrange("p (t n) -> p t n", t=4), v).then_inc(sem("v_pair_staged"), 1)

            pool.wait_ge(y_ready, FIRST_TILE["attn_out"])
            for a in k_win + k_st:
                G.memset(a, 0.0).then_inc(sem("keys_zeroed"), 1)
            pool.wait_ge(y_taken, FIRST_TILE["attn_out"])
            stage_queries(0, 0)
            stage_values(0)
            stage_queries(0, 1)
            with pool.Fori(0, 4) as i:
                pool.wait_ge(sem("s_ready"), i * 16 + 8)
                pool.nop(nofuse=True)
                stage_queries(i + 1, 0)
                pool.wait_ge(sem("o_ready"), i * 16 + 8)
                pool.nop(nofuse=True)
                stage_values(i + 1)
                pool.wait_ge(sem("s_ready"), i * 16 + 16)
                pool.nop(nofuse=True)
                stage_queries(i + 1, 1)
            for b in range(FIRST_BLOCK["attn_out"] + AHEAD, FIRST_BLOCK["up0a"]):
                split_low(b)
            add_out(1)
            split_stream(FIRST_BLOCK["up0a"], FIRST_BLOCK["lora_w"])
            add_out(3)
            pool.wait_ge(y_taken, FIRST_TILE["o"])
            pool.wait_ge(sem("kk_ready"), DT)

            def stage_v(n):
                G.tensor_copy(v_st, pair_tile(vTr, n)).then_inc(sem("v_staged"), 1)

            for a in alone_a + alone_b + [v_alone]:
                for e in range(2):
                    G.memset(a[e], 0.0).then_inc(sem("alone_zeroed"), 1)

            def features(n, F, step):
                for d in range(2):
                    r = F[d]
                    if step == 0:
                        pool.wait_ge(sem("kd_factor"), n(2, d + 1))
                        pool.nop(nofuse=True)
                        G.tensor_tensor(r["kd"], r["kd"], pair_tile(kTr, n), ALU.mult).then_inc(sem("kd_ready"), 1)
                        G.tensor_tensor(r["be"], r["be"], pair_tile(kk, n), ALU.mult).then_inc(sem("rate_kk"), 1)
                    else:
                        pool.wait_ge(sem("decays_ready"), n(6, 3 * (d + 1)))
                        pool.wait_ge(sem("rate_kk"), n(2, d + 1))
                        G.tensor_tensor(r["be"], r["be"], r["ka"], ALU.mult).then_inc(sem("be_ready"), 1)
                        pool.wait_ge(sem("be_ready"), n(2, d + 1))
                        pool.wait_ge(sem("kd_ready"), n(2, d + 1))
                        G.tensor_tensor(r["ka"], r["ka"], r["kd"], ALU.mult).then_inc(sem("features_p"), 1)

            def pair(parity, n, prev, nxt):
                def level_mask(l, d):
                    G.tensor_tensor(chunks(R[d]["LM"]), chunks(R[d]["L"]), mask("level", d * LEVELS + l), ALU.mult
                                    ).then_inc(sem("level_masked"), 1)

                eye = const("eye", 0, CH).unsqueeze(1).to_broadcast([P, NCH, CH])
                for d in range(2):
                    pool.wait_ge(sem("n_masked"), n(2, d + 1))
                    G.tensor_tensor(chunks(R[d]["T"]), chunks(R[d]["T"]), eye, ALU.add).then_inc(sem("t_started"), 1)
                for d in range(2):
                    pool.wait_ge(sem("l_copied"), n(2, d + 1))
                    level_mask(1, d)
                for d in range(2):
                    G.tensor_tensor(chunks(R[d]["TT"]), chunks(R[d]["L"]), mask("level", d * LEVELS), ALU.mult
                                    ).then_inc(sem("tt_masked"), 1)
                for d in range(2):
                    pool.wait_ge(sem("tt_masked"), n(2, d + 1))
                    G.tensor_tensor(chunks(R[d]["TT"]), chunks(R[d]["TT"]), eye, ALU.add).then_inc(sem("tt_started"), 1)
                for l in range(2, LEVELS):
                    for d in range(2):
                        pool.wait_ge(sem("x_ready"), n(10, 2 * (l - 2) + d + 1))
                        level_mask(l, d)
                    if nxt and l >= 4:
                        features(nxt, feats[1 - parity], l - 4)
                if nxt:
                    pool.wait_ge(sem("dt_ready"), n(10, 9))
                    pool.nop(nofuse=True)
                    stage_v(nxt)

            first = lambda per, c=0: c
            stage_v(first)
            for step in range(2):
                features(first, feats[0], step)
            over_pairs(pool, pair)
            add_out(5, kTr)
            split_stream(FIRST_BLOCK["up1a"], FIRST_BLOCK["w_in"])
            add_out(7)
            pool.wait_ge(y_ready, FIRST_TILE["w_in"])
            G.memset(lrux.rearrange("p (t n) -> p t n", t=LT)[:, :, 0:CONV - 1], 0.0).then_inc(sem("conv_zeroed"), 1)
            split_stream(FIRST_BLOCK["w_in"], FIRST_BLOCK["glu"])

            for j in range(ST):
                v, w = TURNS[j % 3], PARTS[j % 2]
                pool.wait_ge(sem("s5_in_taken"), 4 * j + 2)
                G.tensor_tensor(w["v1"], w["v1"], w["v2"], ALU.add).then_inc(sem("s5_back"), 1)
                pool.wait_ge(sem("s5_in_taken"), 4 * j + 4)
                G.tensor_tensor(w["v3"], w["v3"], w["v4"], ALU.subtract).then_inc(sem("s5_back"), 1)
                pool.wait_ge(sem("s5_scanned"), 2 * (j + 1))
                G.tensor_tensor(w["v1"], v["A"], v["C"], ALU.mult).then_inc(sem("s5_part"), 1)
                G.tensor_tensor(w["v2"], v["B"], v["S"], ALU.mult).then_inc(sem("s5_part"), 1)
                G.tensor_tensor(w["v3"], v["B"], v["C"], ALU.mult).then_inc(sem("s5_part"), 1)
                G.tensor_tensor(w["v4"], v["A"], v["S"], ALU.mult).then_inc(sem("s5_part"), 1)
            for x in range(LT):
                pool.wait_ge(y_taken, FIRST_TILE["lru"] + 2 * x + 2)
                G.tensor_tensor(conv[x], conv[x], i_t[x % 2], ALU.mult).then_inc(sem("lru_in"), 1)
            for x in range(DT):
                pool.wait_ge(y_taken, FIRST_TILE["w_bl"] + x + 1)
                G.tensor_tensor(tile(gs, x), tile(gs, x), tile(gl, x), ALU.add).then_inc(sem("merged"), 1)
            add_out(9)
            for x in range(DT):
                pool.wait_ge(sem("gated"), x + 1)
                G.tensor_tensor(tile(gl, x), tile(gl, x), tile(h, x), ALU.add).then_inc(sem("final"), 1)


def units(w):
    k, n = w.shape
    return w.reshape(k // P, P, n // P, P).transpose(2, 0, 1, 3)


def columns(a):
    return np.ascontiguousarray(a.reshape(-1, P).T)


def tiles(a):
    return np.ascontiguousarray(a.reshape(-1, P, a.shape[1]).transpose(1, 0, 2).reshape(P, -1))


def lay_out(**inputs):
    a = {n: np.asarray(v) for n, v in inputs.items()}
    zeros = np.zeros
    wi, wo = a["attn_w_in"][0], a["attn_w_out"][0]
    na = 8 * HEAD
    order = np.concatenate([np.arange(HEAD) + HEAD * hd for pair in range(4) for hd in (pair, pair + 4)])
    qk = np.concatenate([wi[:, 0:na], wi[:, 3 * na:4 * na][:, order], wi[:, na:2 * na], wi[:, 4 * na:4 * na + P]], axis=1)
    v = np.concatenate([wi[:, 2 * na:3 * na], wi[:, 4 * na + P:]], axis=1)
    wo = np.concatenate([wo[0:na], wo[na:][order]])
    both = lambda w: np.concatenate([w[0, 0], w[0, 1]], axis=1)
    glu = a["w_glu_2"][0]
    glu = np.concatenate([glu[:, o + x * P:o + (x + 1) * P] for x in range(XT) for o in (S5W, 0)], axis=1)
    lru = np.stack([w[0, n] for n in range(LT) for w in (a["lru_w_a_2"], a["lru_w_x_2"])])[:, None]
    w_in = units(a["w_in_2"][0])
    parts = {"qk": units(qk), "v": units(v), "attn_out": units(wo),
             "lora_w": units(both(a["rk_w1"])), "lora_a": units(both(a["rk_a1"])), "lora_g": units(both(a["rk_g1"])),
             "r": units(a["rk_w_r"][0]), "k": units(a["rk_w_k"][0]), "rv": units(a["rk_w_v"][0]), "o": units(a["rk_w_o"][0]),
             "w_in": w_in[0:40], "w_in_end": w_in[40:], "glu": units(glu), "w_bs": units(a["w_bs_2"][0]), "lru": lru,
             "w_bl": units(a["w_bl_2"][0]), "w_out": units(a["w_out_2"][0]), "ple": units(a["w_ple_2"][0]),
             "gate": units(a["w_ple_gate_2"][0])}
    half = FF // 2
    for n in range(2):
        for part, at in (("a", slice(0, half)), ("b", slice(half, FF))):
            parts[f"up{n}{part}"], parts[f"down{n}{part}"] = units(a["mlp_w1"][n][:, at]), units(a["mlp_w2"][n][at])
    wall = zeros((NBLOCKS, P, UPB, P), np.float32)
    for name, n, k in DENSE:
        w = parts[name].reshape(n * k, P, P)
        for x in range(0, n * k, UPB):
            some = w[x:x + UPB]
            wall[FIRST_BLOCK[name] + x // UPB][:, 0:len(some)] = some.transpose(1, 0, 2)
    lora2 = zeros((DT, P, 6, P), np.float32)
    for d in range(2):
        half = slice(64 * d, 64 * d + 64)
        lora2[:, half, d] = a["rk_w2"][0, d].reshape(64, DT, P).transpose(1, 0, 2)
        lora2[:, half, 2 + d] = a["rk_a2"][0, d].reshape(64, DT, P).transpose(1, 0, 2)
        lora2[:, :, 4 + d] = a["rk_g2"][0, d].reshape(P, DT, P).transpose(1, 0, 2)
    sink = np.full(16, NEG, np.float32)
    sink[8:] = a["attn_sink"][0]
    fields = {"norm_g": a["norm_g"], "mu_prev": a["rk_mu_prev"], "mu_next": a["rk_mu_next"], "k_k": a["rk_k_k"],
              "k_a": a["rk_k_a"], "r_k": a["rk_r_k"], "gn_w": a["rk_gn_w"], "gn_b": a["rk_gn_b"], "w0": a["rk_w0"],
              "a0": a["rk_a0"], "g_pre": a["g_pre_2"], "g_post": a["g_post_2"], "a_re": a["s5_a_re_2"],
              "a_im": a["s5_a_im_2"], "log_dt": np.repeat(a["s5_log_dt_2"][0], S5N), "s5_d": a["s5_d_2"],
              "conv_w": a["conv_w_2"], "conv_b": a["conv_b_2"], "b_a": a["lru_b_a_2"], "b_x": a["lru_b_x_2"],
              "lam": a["lru_lambda_2"]}
    cols = np.zeros((P, NCOLS), np.float32)
    for name, value in fields.items():
        c = columns(value)
        cols[:, COLS[name]:COLS[name] + c.shape[1]] = c
    cols[:, COLS["sink"]:COLS["sink"] + 16] = sink
    s5_b = zeros((P, ST, 2, P), np.float32)
    s5_c = zeros((P, ST, 2, 32), np.float32)
    for g in range(S5G):
        j, n, rows = g // 2, S5N * (g % 2), g * 16 % P
        for x, (b, c) in enumerate([("s5_b_re_2", "s5_c_re_2"), ("s5_b_im_2", "s5_c_im_2")]):
            s5_b[rows:rows + 16, j, x, n:n + S5N] = a[b][0, g].T
            s5_c[n:n + S5N, j, x, 16 * (g % 2):16 * (g % 2) + 16] = a[c][0, g].T
    onehot, lines = bias_constants()
    return {"x": tiles(a["x"][0].T), "wall": wall.reshape(NBLOCKS, P, BLOCK), "lora2": lora2.reshape(DT, P, 6 * P),
            "cols": cols, "consts": constants(), "rel_table": a["rel_table"], "onehot": onehot, "lines": lines,
            "s5_b": s5_b.reshape(P, -1), "s5_c": s5_c.reshape(P, -1), "p": tiles(a["p_2"][0, 0].T)}


def kernel(**inputs):
    import concourse.bacc as bacc
    from concourse.bass_utils import run_bass_kernel_spmd

    nc = bacc.Bacc("TRN2", target_bir_lowering=False, num_devices=1)
    arrays = {f"in_{n}": v for n, v in lay_out(**inputs).items()}
    t = {n[3:]: nc.dram_tensor(n, v.shape, F32, kind="ExternalInput").ap() for n, v in arrays.items()}
    out = nc.dram_tensor("out", (P, DT * SEQ), F32, kind="ExternalOutput").ap()
    program(nc, t, out)
    got = run_bass_kernel_spmd(nc, [arrays], core_ids=[0]).results[0]["out"]
    return np.ascontiguousarray(got.reshape(P, DT, SEQ).transpose(2, 1, 0)).reshape(1, SEQ, D)
```
